# Optimizing a Trainium2 kernel written in Bass

```python
import jax, jax.numpy as jnp
from jax import lax
import numpy as np

D_MODEL = 2048
BATCH = 1
SEQ = 1024
DEPTH = 1

D_MIX = D_MODEL
HEAD_DIM = 64
RWKV_WIDTH = D_MIX // 2
RWKV_HEADS = RWKV_WIDTH // HEAD_DIM
DECAY_LORA = 64
ICLR_LORA = 64
ATTN_WIDTH = D_MIX - RWKV_WIDTH
ATTN_Q_HEADS = ATTN_WIDTH // HEAD_DIM
GQA_GROUP = 8
ATTN_KV_HEADS = ATTN_Q_HEADS // GQA_GROUP
KV_WIDTH = ATTN_KV_HEADS * HEAD_DIM
WINDOW = 128
BLOCK = 128
RMS_EPS = 1e-5
LNX_EPS = 64e-5
NEG_INF = -1e30

RWKV_COLS = 4 * RWKV_WIDTH + DECAY_LORA + ICLR_LORA
ATTN_COLS = 2 * ATTN_WIDTH + 2 * KV_WIDTH
IN_COLS = RWKV_COLS + ATTN_COLS

kernel_name = "hymba_rwkv7_swa_sink_alibi_block"

def rmsnorm(x, gain):
    xf = x.astype(jnp.float32)
    y = xf * lax.rsqrt(jnp.mean(xf * xf, axis=-1, keepdims=True) + RMS_EPS)
    return (y * gain.astype(jnp.float32)).astype(x.dtype)

def token_shift_lerp(p, mu):
    prev = jnp.pad(p[:, :-1], ((0, 0), (1, 0), (0, 0)))
    return p + (prev - p) * mu

def rwkv7_scan(r, decay, k, v, kk, a):
    B, T, H, N = r.shape
    b = kk * a
    xs = tuple(jnp.swapaxes(t, 0, 1) for t in (r, decay, k, v, kk, b))

    def step(S, inp):
        r_t, w_t, k_t, v_t, kk_t, b_t = inp
        sa = -jnp.einsum('bhvk,bhk->bhv', S, kk_t)
        S = S * w_t[:, :, None, :] + sa[..., None] * b_t[:, :, None, :] + v_t[..., None] * k_t[:, :, None, :]
        y = jnp.einsum('bhvk,bhk->bhv', S, r_t)
        return S, y

    S0 = jnp.zeros((B, H, N, N), jnp.float32)
    _, ys = lax.scan(step, S0, xs)
    return jnp.swapaxes(ys, 0, 1)

def rwkv7_group(p, mu, w0, w_up, a0, a_up, k_k, k_a, r_k, lnx_gain, lnx_bias):
    B, T, _ = p.shape
    H, N = RWKV_HEADS, HEAD_DIM
    p = token_shift_lerp(p, mu)
    cuts = [RWKV_WIDTH, 2 * RWKV_WIDTH, 3 * RWKV_WIDTH, 3 * RWKV_WIDTH + DECAY_LORA,
            3 * RWKV_WIDTH + DECAY_LORA + ICLR_LORA]
    r, k, v, wd, ad, g = jnp.split(p, cuts, axis=-1)
    w_log = -jax.nn.softplus(-(w0 + jnp.tanh(wd) @ w_up)) - 0.5
    decay = jnp.exp(-jnp.exp(w_log))
    a = jax.nn.sigmoid(a0 + ad @ a_up)
    kk = (k * k_k).reshape(B, T, H, N)
    kk = kk / jnp.maximum(jnp.linalg.norm(kk, axis=-1, keepdims=True), 1e-12)
    k = k * (1.0 + (a - 1.0) * k_a)
    rh, kh, vh = (t.reshape(B, T, H, N) for t in (r, k, v))
    y = rwkv7_scan(rh, decay.reshape(B, T, H, N), kh, vh, kk, a.reshape(B, T, H, N))
    mean = jnp.mean(y, axis=-1, keepdims=True)
    var = jnp.mean(jnp.square(y - mean), axis=-1, keepdims=True)
    y = ((y - mean) * lax.rsqrt(var + LNX_EPS)).reshape(B, T, RWKV_WIDTH) * lnx_gain + lnx_bias
    bonus = jnp.sum(rh * kh * r_k, axis=-1, keepdims=True) * vh
    y = y + bonus.reshape(B, T, RWKV_WIDTH)
    return y * jax.nn.silu(g)

def alibi_slopes(n_heads):
    h = jnp.arange(1, n_heads + 1, dtype=jnp.float32)
    return jnp.exp2(-8.0 * h / n_heads)

def swa_sink_alibi_group(p, sinks):
    B, T, _ = p.shape
    nb = T // BLOCK
    cuts = [ATTN_WIDTH, ATTN_WIDTH + KV_WIDTH, ATTN_WIDTH + 2 * KV_WIDTH]
    q, k, v, g = jnp.split(p, cuts, axis=-1)
    qb = q.reshape(B, nb, BLOCK, ATTN_KV_HEADS, GQA_GROUP, HEAD_DIM)

    def band(t):
        tb = t.reshape(B, nb, BLOCK, ATTN_KV_HEADS, HEAD_DIM)
        prev = jnp.concatenate([jnp.zeros_like(tb[:, :1]), tb[:, :-1]], axis=1)
        return jnp.concatenate([prev, tb], axis=2)

    kw, vw = band(k), band(v)
    s = jnp.einsum('bnqhgd,bnkhd->bnhgqk', qb, kw) * (HEAD_DIM ** -0.5)
    qi = jnp.arange(BLOCK)[:, None]
    kj = jnp.arange(2 * BLOCK)[None, :]
    dist = BLOCK + qi - kj
    blk = jnp.arange(nb)[:, None, None]
    valid = (dist >= 0) & (dist < WINDOW) & ((blk - 1) * BLOCK + kj[None] >= 0)
    slopes = alibi_slopes(ATTN_Q_HEADS).reshape(ATTN_KV_HEADS, GQA_GROUP)
    s = s - slopes[:, :, None, None] * dist.astype(jnp.float32)
    s = jnp.where(valid[None, :, None, None], s, NEG_INF)
    sink = jnp.broadcast_to(sinks.reshape(ATTN_KV_HEADS, GQA_GROUP)[None, None, :, :, None, None],
                            s.shape[:-1] + (1,))
    prob = jax.nn.softmax(jnp.concatenate([s, sink], axis=-1), axis=-1)[..., :-1]
    o = jnp.einsum('bnhgqk,bnkhd->bnqhgd', prob, vw).reshape(B, T, ATTN_WIDTH)
    return o * jax.nn.silu(g)

def setup_inputs(seed: int = 0) -> dict:
    key = jax.random.key(seed)
    ks = jax.random.split(key, 20)
    f32 = jnp.float32
    L = DEPTH
    x = jax.random.normal(ks[0], (BATCH, SEQ, D_MODEL), f32)
    norm_gain = 1.0 + 0.05 * jax.random.normal(ks[1], (L, D_MODEL), f32)
    w_in = jax.random.normal(ks[2], (L, D_MODEL, IN_COLS), f32) * D_MODEL ** -0.5
    mu_rwkv = jax.random.uniform(ks[3], (L, RWKV_COLS), f32)
    w0 = jax.random.uniform(ks[4], (L, RWKV_WIDTH), f32, minval=-4.0, maxval=1.0)
    w_up = jax.random.normal(ks[5], (L, DECAY_LORA, RWKV_WIDTH), f32) * 0.5 * DECAY_LORA ** -0.5
    a0 = 0.5 * jax.random.normal(ks[6], (L, RWKV_WIDTH), f32)
    a_up = jax.random.normal(ks[7], (L, ICLR_LORA, RWKV_WIDTH), f32) * 0.5 * ICLR_LORA ** -0.5
    k_k = 0.85 + 0.05 * jax.random.normal(ks[8], (L, RWKV_WIDTH), f32)
    k_a = 1.0 + 0.05 * jax.random.normal(ks[9], (L, RWKV_WIDTH), f32)
    r_k = -0.04 + 0.02 * jax.random.normal(ks[10], (L, RWKV_HEADS, HEAD_DIM), f32)
    lnx_gain = 1.0 + 0.05 * jax.random.normal(ks[11], (L, RWKV_WIDTH), f32)
    lnx_bias = 0.01 * jax.random.normal(ks[12], (L, RWKV_WIDTH), f32)
    attn_sinks = 0.5 * jax.random.normal(ks[13], (L, ATTN_Q_HEADS), f32)
    w_out = jax.random.normal(ks[14], (L, D_MIX, D_MODEL), f32) * D_MIX ** -0.5
    final_gain = 1.0 + 0.05 * jax.random.normal(ks[15], (D_MODEL,), f32)
    return {"x": x, "norm_gain": norm_gain, "w_in": w_in, "mu_rwkv": mu_rwkv, "w0": w0,
            "w_up": w_up, "a0": a0, "a_up": a_up, "k_k": k_k, "k_a": k_a, "r_k": r_k,
            "lnx_gain": lnx_gain, "lnx_bias": lnx_bias, "attn_sinks": attn_sinks,
            "w_out": w_out, "final_gain": final_gain}

def reference(x, norm_gain, w_in, mu_rwkv, w0, w_up, a0, a_up, k_k, k_a, r_k,
              lnx_gain, lnx_bias, attn_sinks, w_out, final_gain):
    f32 = jnp.float32
    for l in range(DEPTH):
        h = rmsnorm(x, norm_gain[l])
        proj = (h @ w_in[l]).astype(f32)
        p_rwkv, p_attn = proj[..., :RWKV_COLS], proj[..., RWKV_COLS:]
        y_rwkv = rwkv7_group(p_rwkv, mu_rwkv[l].astype(f32), w0[l].astype(f32),
                             w_up[l].astype(f32), a0[l].astype(f32), a_up[l].astype(f32),
                             k_k[l].astype(f32), k_a[l].astype(f32), r_k[l].astype(f32),
                             lnx_gain[l].astype(f32), lnx_bias[l].astype(f32))
        y_attn = swa_sink_alibi_group(p_attn, attn_sinks[l].astype(f32))
        mix = jnp.concatenate([y_rwkv, y_attn], axis=-1).astype(x.dtype)
        x = x + mix @ w_out[l]
    return rmsnorm(x, final_gain)


_drawn_inputs = setup_inputs


def setup_inputs(seed=0):
    import zlib

    import numpy as np

    out = dict(_drawn_inputs(seed))
    spreads = {}
    factors = {'w_up': 4.345,
     'k_k': 32.098,
     'k_a': 3.496,
     'r_k': 4.218,
     'lnx_gain': 3.563,
     'lnx_bias': 26.272,
     'attn_sinks': 6.888}
    for name, (base, spread) in spreads.items():
        noise = np.random.default_rng([zlib.crc32(name.encode()), seed]).standard_normal(out[name].shape)
        drawn = base * np.exp(spread * noise) if base else spread * noise
        out[name] = __import__('jax').numpy.asarray(drawn.astype(out[name].dtype))
    for name, factor in factors.items():
        out[name] = (out[name] * factor).astype(out[name].dtype)
    return out
```

```python
import math
from contextlib import ExitStack

import concourse.bass as bass
import numpy as np
from concourse import mybir
from concourse.bass import ds

F32 = mybir.dt.float32
F32R = mybir.dt.float32r
U8 = mybir.dt.uint8
ALU = mybir.AluOpType
ACT = mybir.ActivationFunctionType
AX = mybir.AxisListType.X

P = 128
T = 1024
D = 2048
KC = D // P
HD = 64
PAIRS = 8
HEADS = 2 * PAIRS
LORA = 64
RW = PAIRS * P
AW = PAIRS * P
KVW = 2 * HD
RWKV_COLS = 4 * RW + 2 * LORA
TILES = (RWKV_COLS + 2 * AW + 2 * KVW) // P
C = 64
BT = 128
NB = T // BT
NC_ = T // C
SUB = 16
HALF = T // 2
KH = KC // 2
DECAY = math.exp(-0.5)
RMS_EPS = 1e-5
LNX_EPS = 64e-5

PAR = ["mu_r", "mu_k", "mu_v", "mu_g", "w0", "a0", "k_k", "k_a", "r_k", "gain", "bias"]
NPAR = len(PAR)
CONSTS = {}
_at = 0
for _name, _w in (("ident", 128), ("same_head", 128), ("mean", 128), ("amask", 256), ("m16", 128),
                  ("m32", 128), ("dist", 256), ("head_of", 2)):
    CONSTS[_name] = (_at, _at + _w)
    _at += _w
CONST_COLS = _at


def constants():
    r = np.arange(128)[:, None]
    c = np.arange(128)[None, :]
    t = {}
    t["ident"] = (r == c)
    t["same_head"] = (r // HD == c // HD)
    t["mean"] = np.full((128, 128), 1.0 / D)
    s, u = r % C, np.arange(C)[None, :]
    t["amask"] = np.concatenate([s <= u, s < u, s < u, s <= u], axis=1)
    for m in (16, 32):
        t[f"m{m}"] = (r // (2 * m) == c // (2 * m)) & (r % (2 * m) >= m) & (c % (2 * m) < m)
    key = np.arange(2 * BT)[None, :]
    d = BT + r - key
    t["dist"] = np.where((d >= 0) & (d < BT), d, 1e33)
    t["head_of"] = (r // HD == np.arange(2)[None, :])
    return np.concatenate([t[n].astype(np.float32) for n in CONSTS], axis=1)


def after(n, per, k):
    return n * per + k


def stage_a(nc, io, scr, pc_all, consts):
    with ExitStack() as ctx:
        def sb(name, shape, dt=F32):
            return ctx.enter_context(nc.sbuf_tensor("a_" + name, shape, dt))

        def sem(name):
            return ctx.enter_context(nc.semaphore(name))

        x_hi = sb("x_hi", [P, KC, T], F32R)
        x_lo = sb("x_lo", [P, KC, T], F32R)
        w_raw = sb("w_raw", [P, KH * P])
        w_hi = [sb(f"w_hi{i}", [P, KH * P], F32R) for i in range(2)]
        w_lo = [sb(f"w_lo{i}", [P, KH * P], F32R) for i in range(2)]
        rms = sb("rms", [P, T])
        keep = sb("keep", [P, T], U8)
        lora = sb("lora", [P, T])
        raw = sb("raw", [P, T + 1])
        r = sb("r", [P, T])
        k = sb("k", [P, T])
        v = sb("v", [P, T])
        g = sb("g", [P, T])
        s1 = sb("s1", [P, T])
        s2 = sb("s2", [P, T])
        a = sb("a", [P, T])
        b = sb("b", [P, T])
        decay = sb("decay", [P, NC_, C + 1])
        grow = sb("grow", [P, T])
        par = sb("par", [P, PAIRS, NPAR])
        par1 = sb("par1", [P, KC + 1])
        lora_up = sb("lora_up", [P, P])
        inv2 = sb("inv2", [P, 2 * NB])
        eps = sb("eps", [P, 1])
        cst = consts
        x_in = [r, k, v, g]
        sq = [s1, s2]
        acc = a
        psum = ctx.enter_context(nc.psum_tensor("psum_a", [P, 8, HALF], F32))

        def banks(i):
            return psum[:, i:i + 2, :].rearrange("p b t -> p (b t)")

        par_landed = sem("a_par_landed")
        x_landed = [sem(f"a_x_landed{i}") for i in range(4)]
        x_squared = sem("a_x_squared")
        x_high = sem("a_x_high")
        x_ready = sem("a_x_ready")
        x_summed = sem("a_x_summed")
        ms_done = sem("a_ms_done")
        rms_root = sem("a_rms_root")
        w_landed = sem("a_w_landed")
        w_high = [sem(f"a_w_high{i}") for i in range(2)]
        w_ready = [sem(f"a_w_ready{i}") for i in range(2)]
        w_used = [sem(f"a_w_used{i}") for i in range(2)]
        tile_done = sem("a_tile_done")
        tile_read = sem("a_tile_read")
        up_landed = sem("a_up_landed")
        lora_ready = sem("a_lora_ready")
        lora_done = sem("a_lora_done")
        norm_done = sem("a_norm_done")
        sigma_w = sem("a_sigma_w")
        sigma_a = sem("a_sigma_a")
        summed = sem("a_summed")
        exps = sem("a_exps")
        squares = sem("a_squares")
        k_ready = sem("a_k_ready")
        inv_ready = sem("a_inv_ready")
        inv_spread = sem("a_inv_spread")
        rkr_ready = sem("a_rkr_ready")
        bonus_done = sem("a_bonus_done")
        g_ready = sem("a_g_ready")
        gate_sig = sem("a_gate_sig")
        ga_ready = sem("a_ga_ready")
        ga_sig = sem("a_ga_sig")
        kk_read = sem("a_kk_read")
        bonus_read = sem("a_bonus_read")
        names = ["R", "KK", "K", "B", "V", "GS", "BS", "Q", "SA"]
        made = {x: sem(f"a_made_{x}") for x in names}
        stored = {x: sem(f"a_stored_{x}") for x in names}
        stores_begun = sem("a_stores_begun")
        kv_made = sem("a_kv_made")
        kv_stored = sem("a_kv_stored")
        steps = sem("a_dve_steps")

        PRO = 3
        TP = 6

        with nc.Block() as block:
            @block.sync
            def _(sp):
                def load_half(t, half, first):
                    if not first:
                        if half == 0:
                            sp.wait_ge(w_ready[1], t)
                        else:
                            sp.wait_ge(w_ready[0], t + 1)
                    elif half == 1:
                        sp.wait_ge(w_ready[0], 1)
                    sp.dma_start(w_raw[:], io["w_in"][ds(t, 1), half].rearrange("a p n -> (a p) n")
                                 ).then_inc(w_landed, 16)

                sp.dma_start(par1[:], io["par1"]).then_inc(par_landed, 16)
                sp.dma_start(cst[:], io["consts"]).then_inc(par_landed, 16)
                sp.dma_start(par[:], io["par"]).then_inc(par_landed, 16)
                load_half(0, 0, True)
                for c in range(KC):
                    if c == 2:
                        load_half(0, 1, True)
                    if c >= 4:
                        sp.wait_ge(x_ready, c - 3)
                        sp.wait_ge(x_squared, c - 3)
                    sp.dma_start(x_in[c % 4][:], io["x_t"][c]).then_inc(x_landed[c % 4], 16)
                with sp.Fori(1, TILES) as t:
                    load_half(t, 0, False)
                    load_half(t, 1, False)

            @block.gpsimd
            def _(pool):
                def store(n, name, src):
                    pool.wait_ge(made[name], after(n, 1, 1))
                    pool.sem_inc(stores_begun, 1)
                    if name in ("K", "B", "R", "KK"):
                        dst = scr["KB" if name in ("K", "B") else "QR"]
                        dst = dst[:, :, ds(n, 1)].rearrange("b p j s t -> p (b j) s t")
                        src = src[:].rearrange("p (b s t) -> p b s t", b=NB, s=2)
                        dst = dst[:, :, 0:4:3, :] if name in ("K", "R") else dst[:, :, 1:3, :]
                    else:
                        dst = scr[name][:, :, ds(n, 1)].rearrange("b p j t -> p (b j) t")
                        src = src.rearrange("p (b t) -> p b t", b=NB)
                    if name in ("K", "R"):
                        for c in range(2):
                            pool.dma_start(dst[:, :, c], src[:, :, c]).then_inc(stored[name], 16)
                    else:
                        if name in ("KK", "B"):
                            dst = dst.rearrange("p b s t -> p b (s t)")
                            src = src.rearrange("p b s t -> p b (s t)")
                        pool.dma_start(dst, src).then_inc(stored[name], 16)

                def pair(n, first):
                    if not first:
                        pool.wait_ge(lora_done, after(n, 2, 0))
                    pool.sem_inc(stores_begun, 1)
                    pool.dma_start(lora_up[:], io["lora_up"][ds(n, 1)].rearrange("a p n -> (a p) n")
                                   ).then_inc(up_landed, 16)
                    if not first:
                        store(n - 1, "SA", raw[:, 1:T + 1])
                    store(n, "R", r)
                    store(n, "B", b)
                    store(n, "K", a)
                    store(n, "V", v[:])
                    store(n, "Q", raw[:, 1:T + 1])
                    store(n, "KK", k)
                    store(n, "BS", s2[:])
                    store(n, "GS", g[:])

                for i in range(2):
                    pool.wait_ge(kv_made, i + 1)
                    pool.dma_start(scr["KVA"][i], raw[:, 1:T + 1]).then_inc(kv_stored, 16)
                pair(0, True)
                with pool.Fori(1, PAIRS) as n:
                    pair(n, False)
                store(PAIRS - 1, "SA", raw[:, 1:T + 1])
                for name in names:
                    pool.wait_ge(stored[name], 16 * PAIRS * (2 if name in ("K", "R") else 1))
                pool.wait_ge(kv_stored, 32)

            @block.scalar
            def _(act):
                def high_half(t, half, first=False):
                    act.wait_ge(w_landed, 32 * t + 16 * (half + 1))
                    if not first:
                        act.wait_ge(w_used[half], t)
                    nc.scalar.activation(w_hi[half][:], w_raw[:], ACT.Copy).then_inc(w_high[half], 1)

                def p(n, name):
                    return par[:, ds(n, 1), PAR.index(name)]

                act.wait_ge(par_landed, 48)
                high_half(0, 0, True)
                for c in range(KC):
                    if c == 2:
                        high_half(0, 1, True)
                    act.wait_ge(x_landed[c % 4], 16 * (c // 4 + 1))
                    if c >= 2:
                        act.wait_ge(x_summed, c - 1)
                    nc.scalar.activation(sq[c % 2][:], x_in[c % 4][:], ACT.Square).then_inc(x_squared, 1)
                    nc.scalar.activation(x_hi[:, c], x_in[c % 4][:], ACT.Copy,
                                         scale=par1[:, c:c + 1]).then_inc(x_high, 1)
                high_half(1, 0)
                high_half(1, 1)
                act.wait_ge(ms_done, 1)
                nc.scalar.activation(rms[:], banks(4), ACT.Sqrt, bias=eps[:, 0:1]).then_inc(rms_root, 1)
                act.wait_ge(lora_ready, 1)
                nc.scalar.activation(lora[0:LORA], lora[0:LORA], ACT.Tanh).then_inc(lora_ready, 1)
                high_half(2, 0)
                high_half(2, 1)

                def pair(n, first):
                    t = TP * n + PRO
                    high_half(t, 0)
                    high_half(t, 1)
                    if not first:
                        act.wait_ge(ga_ready, after(n, 1, 0))
                        nc.scalar.activation(s1[:], raw[:, 1:T + 1], ACT.Sigmoid).then_inc(ga_sig, 1)
                        act.wait_ge(made["SA"], after(n, 1, 0))
                    act.wait_ge(lora_done, after(n, 2, 1))
                    nc.scalar.activation(s1[:], banks(4), ACT.Sigmoid, bias=p(n, "w0")).then_inc(sigma_w, 1)
                    act.wait_ge(lora_done, after(n, 2, 2))
                    if not first:
                        act.wait_ge(stored["K"], after(n, 32, 0))
                    nc.scalar.activation(a[:], banks(6), ACT.Sigmoid, bias=p(n, "a0")).then_inc(sigma_a, 1)
                    high_half(t + 1, 0)
                    act.wait_ge(summed, after(n, 1, 1))
                    nc.scalar.activation(decay[:, :, 1:C + 1], s2[:].rearrange("p (c t) -> p c t", t=C),
                                         ACT.Exp, scale=-DECAY).then_inc(exps, 1)
                    nc.scalar.activation(grow[:], s2[:], ACT.Exp, scale=DECAY).then_inc(exps, 1)
                    high_half(t + 1, 1)
                    high_half(t + 2, 0)
                    high_half(t + 2, 1)
                    act.wait_ge(k_ready, after(n, 1, 1))
                    act.wait_ge(exps, after(n, 2, 2))
                    nc.scalar.activation(s2[:], k[:], ACT.Square, scale=p(n, "k_k")).then_inc(squares, 1)
                    for i in (3, 4):
                        high_half(t + i, 0)
                        high_half(t + i, 1)
                    act.wait_ge(g_ready, after(n, 1, 1))
                    act.wait_ge(norm_done, after(n, 2, 1))
                    nc.scalar.activation(s2[:], g[:], ACT.Sigmoid).then_inc(gate_sig, 1)
                    high_half(t + 5, 0)
                    high_half(t + 5, 1)

                pair(0, True)
                with act.Fori(1, PAIRS) as n:
                    pair(n, False)
                act.wait_ge(ga_ready, PAIRS)
                nc.scalar.activation(s1[:], raw[:, 1:T + 1], ACT.Sigmoid).then_inc(ga_sig, 1)

            @block.vector
            def _(dve):
                count = [0, 0]

                def then(ins):
                    ins.then_inc(steps, 1)
                    count[1] += 1
                    dve.wait_ge(steps, count[0] + count[1])

                def low_half(t, half):
                    dve.wait_ge(w_high[half], t + 1)
                    nc.vector.tensor_tensor(w_lo[half][:], w_raw[:], w_hi[half][:].bitcast(F32),
                                            ALU.subtract).then_inc(w_ready[half], 1)

                def p(n, name):
                    return par[:, ds(n, 1), PAR.index(name)]

                def read_tile(t, dst, scale=None):
                    dve.wait_ge(tile_done, t + 1)
                    src = banks(2 * _parity(t))
                    if scale is None:
                        ins = nc.vector.tensor_tensor(dst, src, rms[:], ALU.mult)
                    else:
                        ins = nc.vector.scalar_tensor_tensor(dst, src, scale, rms[:], ALU.mult, ALU.mult)
                    then(ins)
                    dve.sem_inc(tile_read, 1)

                def _parity(t):
                    return parity[0]

                parity = [0]

                def tile(t, par_, dst, scale=None):
                    parity[0] = par_
                    read_tile(t, dst, scale)

                def shift(dst, mu):
                    then(nc.vector.tensor_tensor(dst, raw[:, 0:T], raw[:, 1:T + 1], ALU.subtract))
                    return nc.vector.scalar_tensor_tensor(dst, dst, mu, raw[:, 1:T + 1],
                                                          ALU.mult, ALU.add)

                then(nc.vector.memset(keep[:], 1))
                then(nc.vector.memset(keep[:].rearrange("p (c t) -> p c t", t=C)[:, :, 0:1], 0))
                then(nc.vector.memset(raw[:, 0:1], 0.0))
                then(nc.vector.memset(decay[:, :, 0:1], 1.0))
                then(nc.vector.memset(eps[:], RMS_EPS))
                low_half(0, 0)
                dve.wait_ge(par_landed, 48)
                for c in range(KC):
                    if c == 2:
                        low_half(0, 1)
                    dve.wait_ge(x_high, c + 1)
                    nc.vector.scalar_tensor_tensor(x_lo[:, c], x_in[c % 4][:], par1[:, c:c + 1],
                                                   x_hi[:, c].bitcast(F32), ALU.mult, ALU.subtract
                                                   ).then_inc(x_ready, 1)
                    dve.wait_ge(x_squared, c + 1)
                    if c == 0:
                        ins = nc.vector.tensor_copy(acc[:], sq[0][:])
                    else:
                        dve.wait_ge(x_summed, c)
                        ins = nc.vector.tensor_tensor(acc[:], acc[:], sq[c % 2][:], ALU.add)
                    ins.then_inc(x_summed, 1)
                low_half(1, 0)
                low_half(1, 1)
                dve.wait_ge(rms_root, 1)
                then(nc.vector.reciprocal(rms[:], rms[:]))
                tile(0, 0, raw[:, 1:T + 1])
                shift(lora[:], par1[:, KC:KC + 1]).then_inc(lora_ready, 1)
                low_half(2, 0)
                low_half(2, 1)
                dve.wait_ge(lora_ready, 1)
                tile(1, 1, raw[:, 1:T + 1])
                dve.sem_inc(kv_made, 1)

                def pair(n, first):
                    t = TP * n + PRO
                    low_half(t, 0)
                    low_half(t, 1)
                    if first:
                        dve.wait_ge(kv_stored, 16)
                        tile(t - 1, 0, raw[:, 1:T + 1])
                        dve.sem_inc(kv_made, 1)
                        dve.wait_ge(kv_stored, 32)
                    else:
                        dve.wait_ge(stored["Q"], after(n, 16, 0))
                        tile(t - 1, 0, raw[:, 1:T + 1])
                        dve.wait_ge(stored["BS"], after(n, 16, 0))
                        dve.sem_inc(ga_ready, 1)
                        dve.wait_ge(ga_sig, after(n, 1, 0))
                        then(nc.vector.tensor_tensor(raw[:, 1:T + 1], raw[:, 1:T + 1], s1[:], ALU.mult))
                        dve.sem_inc(made["SA"], 1)
                    dve.wait_ge(sigma_w, after(n, 1, 1))
                    if first:
                        dve.wait_ge(ms_done, 1)
                    then(nc.vector.tensor_tensor_scan(s2[:], keep[:], s1[:], 0.0, ALU.mult, ALU.add))
                    dve.sem_inc(summed, 1)
                    low_half(t + 1, 0)
                    low_half(t + 1, 1)
                    if not first:
                        dve.wait_ge(stored["SA"], after(n, 16, 0))
                        dve.wait_ge(stored["R"], after(n, 32, 0))
                    tile(t, 1, raw[:, 1:T + 1])
                    then(shift(r[:], p(n, "mu_r")))
                    low_half(t + 2, 0)
                    low_half(t + 2, 1)
                    tile(t + 1, 0, raw[:, 1:T + 1])
                    if not first:
                        dve.wait_ge(stored["KK"], after(n, 16, 0))
                        dve.wait_ge(stored["B"], after(n, 16, 0))
                    then(shift(k[:], p(n, "mu_k")))
                    dve.sem_inc(k_ready, 1)
                    dve.wait_ge(exps, after(n, 2, 2))
                    nc.vector.tensor_copy(pc_all[:, ds(n, 1)].rearrange("p a c -> p (a c)"),
                                          decay[:, :, C])
                    dve.wait_ge(sigma_a, after(n, 1, 1))
                    then(nc.vector.scalar_tensor_tensor(b[:], k[:], p(n, "k_k"), a[:], ALU.mult, ALU.mult))
                    then(nc.vector.tensor_tensor(b[:], b[:], grow[:], ALU.mult))
                    dve.sem_inc(made["B"], 1)
                    then(nc.vector.tensor_scalar(a[:], a[:], 1.0, p(n, "k_a"), ALU.subtract, ALU.mult))
                    then(nc.vector.scalar_tensor_tensor(a[:], a[:], 1.0, k[:], ALU.add, ALU.mult))
                    then(nc.vector.scalar_tensor_tensor(s1[:], r[:], p(n, "r_k"), a[:], ALU.mult, ALU.mult))
                    dve.sem_inc(rkr_ready, 1)
                    low_half(t + 3, 0)
                    then(nc.vector.tensor_tensor(a[:], a[:], grow[:], ALU.mult))
                    dve.sem_inc(made["K"], 1)
                    then(nc.vector.tensor_tensor(r[:].rearrange("p (c t) -> p c t", t=C),
                                                 r[:].rearrange("p (c t) -> p c t", t=C),
                                                 decay[:, :, 1:C + 1], ALU.mult))
                    dve.sem_inc(made["R"], 1)
                    low_half(t + 3, 1)
                    tile(t + 2, 1, raw[:, 1:T + 1])
                    if not first:
                        dve.wait_ge(stored["V"], after(n, 16, 0))
                    then(shift(v[:], p(n, "mu_v")))
                    dve.sem_inc(made["V"], 1)
                    dve.wait_ge(norm_done, after(n, 2, 1))
                    then(nc.vector.tensor_scalar(inv2[:], psum[:, 4, 0:2 * NB], 1e-24, None, ALU.max))
                    then(nc.vector.reciprocal(inv2[:], inv2[:]))
                    spread = grow[:].rearrange("p (b d) -> p b d", d=HD)
                    then(nc.vector.tensor_copy(spread, inv2[:].unsqueeze(2).broadcast_to([P, 2 * NB, HD])))
                    dve.sem_inc(inv_ready, 1)
                    low_half(t + 4, 0)
                    low_half(t + 4, 1)
                    tile(t + 3, 0, raw[:, 1:T + 1])
                    if not first:
                        dve.wait_ge(stored["GS"], after(n, 16, 0))
                    then(shift(g[:], p(n, "mu_g")))
                    dve.sem_inc(g_ready, 1)
                    low_half(t + 5, 0)
                    dve.wait_ge(norm_done, after(n, 2, 2))
                    then(nc.vector.scalar_tensor_tensor(k[:], k[:], p(n, "k_k"), banks(4),
                                                        ALU.mult, ALU.mult))
                    dve.sem_inc(kk_read, 1)
                    then(nc.vector.tensor_tensor(k[:].rearrange("p (c t) -> p c t", t=C),
                                                 k[:].rearrange("p (c t) -> p c t", t=C),
                                                 decay[:, :, 0:C], ALU.mult))
                    dve.sem_inc(made["KK"], 1)
                    dve.wait_ge(gate_sig, after(n, 1, 1))
                    then(nc.vector.tensor_tensor(g[:], g[:], s2[:], ALU.mult))
                    dve.wait_ge(bonus_done, after(n, 1, 1))
                    then(nc.vector.tensor_tensor(s2[:], v[:], banks(6), ALU.mult))
                    dve.sem_inc(bonus_read, 1)
                    then(nc.vector.scalar_tensor_tensor(s2[:], s2[:], p(n, "bias"), g[:], ALU.add, ALU.mult))
                    dve.sem_inc(made["BS"], 1)
                    then(nc.vector.tensor_scalar(g[:], g[:], p(n, "gain"), None, ALU.mult))
                    dve.sem_inc(made["GS"], 1)
                    low_half(t + 5, 1)
                    tile(t + 4, 1, raw[:, 1:T + 1], scale=HD ** -0.5)
                    dve.sem_inc(made["Q"], 1)

                pair_start = count[1]
                pair(0, True)
                count[0], per = count[1], None
                per = count[1] - pair_start + 1
                base = count[1]
                with dve.Fori(1, PAIRS) as n:
                    count[0], count[1] = base + (n - 1) * per, 0
                    pair(n, False)
                    assert count[1] == per, (count, per)
                count[0], count[1] = base + (PAIRS - 1) * per, 0
                dve.wait_ge(stored["Q"], 16 * PAIRS)
                tile(TILES - 1, 0, raw[:, 1:T + 1])
                dve.sem_inc(ga_ready, 1)
                dve.wait_ge(ga_sig, PAIRS)
                then(nc.vector.tensor_tensor(raw[:, 1:T + 1], raw[:, 1:T + 1], s1[:], ALU.mult))
                dve.sem_inc(made["SA"], 1)

            @block.tensor
            def _(pe):
                def project(t, parity, pace=False, reuse=True):
                    if reuse:
                        pe.wait_ge(tile_read, t - 1)
                    for half in range(2):
                        pe.wait_ge(w_ready[half], t + 1)
                        for kk in range(KH):
                            c = half * KH + kk
                            if pace:
                                pe.wait_ge(x_ready, c + 1)
                            cols = slice(kk * P, (kk + 1) * P)
                            for wt, xt in ((w_hi, x_hi), (w_hi, x_lo), (w_lo, x_hi)):
                                for h in range(2):
                                    mm = nc.tensor.matmul(
                                        psum[:, 2 * parity + h], wt[half][:, cols],
                                        xt[:, c, h * HALF:(h + 1) * HALF],
                                        start=(c == 0 and wt is w_hi and xt is x_hi),
                                        stop=(c == KC - 1 and wt is w_lo))
                        mm.then_inc(w_used[half], 1)
                    pe.wait_ge(w_used[1], t + 1)
                    pe.sem_inc(tile_done, 1)

                def const(name):
                    return cst[:, slice(*CONSTS[name])]

                project(0, 0, pace=True, reuse=False)
                pe.wait_ge(x_summed, KC)
                for h in range(2):
                    mm = nc.tensor.matmul(psum[:, 4 + h], const("mean"), acc[:, h * HALF:(h + 1) * HALF],
                                          start=True, stop=True)
                mm.then_inc(ms_done, 1)
                project(1, 1, reuse=False)
                project(2, 0)

                def pair(n, first):
                    t = TP * n + PRO
                    pe.wait_ge(up_landed, after(n, 16, 16))
                    if first:
                        pe.wait_ge(lora_ready, 2)
                        pe.wait_ge(rms_root, 1)
                    else:
                        pe.wait_ge(kk_read, after(n, 1, 0))
                        pe.wait_ge(bonus_read, after(n, 1, 0))
                    for i in range(2):
                        rows = slice(i * LORA, (i + 1) * LORA)
                        for h in range(2):
                            mm = nc.tensor.matmul(psum[:, 4 + 2 * i + h], lora_up[rows, :],
                                                  lora[rows, h * HALF:(h + 1) * HALF],
                                                  start=True, stop=True)
                        mm.then_inc(lora_done, 1)
                    project(t, 1)
                    project(t + 1, 0)
                    project(t + 2, 1)
                    pe.wait_ge(squares, after(n, 1, 1))
                    pe.wait_ge(sigma_w, after(n, 1, 1))
                    for b_ in range(NB):
                        mm = nc.tensor.matmul(psum[:, 4, 2 * b_:2 * b_ + 2], s2[:, b_ * P:(b_ + 1) * P],
                                              const("head_of"), start=True, stop=True)
                    mm.then_inc(norm_done, 1)
                    project(t + 3, 0)
                    pe.wait_ge(inv_ready, after(n, 1, 1))
                    for b_ in range(NB):
                        mm = nc.tensor.matmul(banks(4)[:, b_ * P:(b_ + 1) * P],
                                              grow[:, b_ * P:(b_ + 1) * P], const("ident"),
                                              start=True, stop=True)
                    mm.then_inc(norm_done, 1)
                    pe.wait_ge(rkr_ready, after(n, 1, 1))
                    pe.wait_ge(sigma_a, after(n, 1, 1))
                    for h in range(2):
                        mm = nc.tensor.matmul(psum[:, 6 + h], const("same_head"),
                                              s1[:, h * HALF:(h + 1) * HALF], start=True, stop=True)
                    mm.then_inc(bonus_done, 1)
                    project(t + 4, 1)
                    project(t + 5, 0)

                pair(0, True)
                with pe.Fori(1, PAIRS) as n:
                    pair(n, False)


def stage_b(nc, io, scr, pc_all, cst):
    with ExitStack() as ctx:
        def sb(name, shape, dt=F32):
            return ctx.enter_context(nc.sbuf_tensor("b_" + name, shape, dt))

        def sem(name):
            return ctx.enter_context(nc.semaphore("b_" + name))

        kb = sb("kb", [P, PAIRS, 4 * C])
        qr = sb("qr", [P, PAIRS, 4 * C])
        qr_s = sb("qr_s", [P, PAIRS, 4 * C])
        vt = sb("vt", [P, PAIRS, BT])
        gs = sb("gs", [P, PAIRS, BT])
        bs = sb("bs", [P, PAIRS, BT])
        q = sb("q", [P, PAIRS, BT])
        sa = sb("sa", [P, PAIRS, BT])
        kw = sb("kw", [P, 2, 2 * BT])
        vw = sb("vw", [P, 2 * BT])
        va = sb("va", [P, 2, P])
        am = sb("am", [P, HEADS, 4 * C])
        kbt = sb("kbt", [P, 2, PAIRS, P])
        uv = sb("uv", [P, 2, HEADS, HD])
        x16 = sb("x16", [P, HEADS, 2, P])
        x32 = sb("x32", [P, HEADS, P])
        xt = sb("xt", [P, HEADS, P])
        ym = sb("ym", [P, HEADS, P])
        sub_l = sb("sub_l", [P, SUB, SUB])
        sub_x = sb("sub_x", [P, 2, SUB, SUB])
        sub_t = sb("sub_t", [P, SUB * SUB])
        state = sb("state", [P, PAIRS, 2, HD])
        state_d = sb("state_d", [P, PAIRS, HD])
        fresh = sb("fresh", [P, PAIRS, HD])
        zs = sb("zs", [P, HEADS, HD])
        y = sb("y", [P, HEADS, HD])
        ysq = sb("ysq", [P, HEADS, HD])
        stat = sb("stat", [P, 2, HEADS])
        mix = sb("mix", [P, PAIRS, P])
        mix_a = sb("mix_a", [P, PAIRS, P])
        score = [sb(f"score{i}", [P, 4, 2 * BT]) for i in range(2)]
        pt = [sb(f"pt{i}", [P, 2, 4 * P]) for i in range(2)]
        o = sb("o", [P, HEADS, HD])
        sinks = sb("sinks", [P, HEADS])
        top = sb("top", [P, 4, HEADS])
        part = sb("part", [P, HEADS])
        neg_sinks = sb("neg_sinks", [P, HEADS])
        sub_ident = sb("sub_ident", [P, SUB, SUB])
        eps = sb("eps", [P, 1])
        psum = ctx.enter_context(nc.psum_tensor("psum_b", [P, 8, HALF], F32))

        loads = ("kb", "qr", "qr_s", "vt", "gs", "bs", "q", "sa", "kw", "vw")
        landed = {x: sem(f"landed_{x}") for x in loads}
        sinks_landed = sem("sinks_landed")
        l_out, l_in, x_out, x_in = sem("l_out"), sem("l_in"), sem("x_out"), sem("x_in")
        sub_done = sem("sub_done")
        pool_steps = sem("pool_steps")
        u_zero = sem("u_zero")
        decayed = sem("decayed")
        a_full, a_read = sem("a_full"), sem("a_read")
        t_full, t_read = sem("t_full"), sem("t_read")
        va_full, va_read = sem("va_full"), sem("va_read")
        s_full, s_read = sem("s_full"), sem("s_read")
        p_ready = sem("p_ready")
        pt_full, pt_read = sem("pt_full"), sem("pt_read")
        o_full, o_read = sem("o_full"), sem("o_read")
        ot_full, ot_read = sem("ot_full"), sem("ot_read")
        lev_full, lev_read = sem("lev_full"), sem("lev_read")
        z_full, z_read = sem("z_full"), sem("z_read")
        u_full, u_read = sem("u_full"), sem("u_read")
        f_full, state_read, state_new = sem("f_full"), sem("state_read"), sem("state_new")
        y_full, y_read = sem("y_full"), sem("y_read")
        y_centred, y_squared, y_var, y_root, y_norm = (sem("y_centred"), sem("y_squared"),
                                                       sem("y_var"), sem("y_root"), sem("y_norm"))
        yt_full, yt_read = sem("yt_full"), sem("yt_read")
        negmax = sem("negmax")
        mix_ready, mix_stored = sem("mix_ready"), sem("mix_stored")
        mixa_ready, mixa_stored = sem("mixa_ready"), sem("mixa_stored")
        steps = sem("dve_steps")
        inited = sem("inited")
        apart = sem("apart")

        def const(name):
            return cst[:, slice(*CONSTS[name])]

        def many(ap, n):
            return ap.unsqueeze(1).broadcast_to([P, n, ap.shape[1]])

        def sides(c):
            u = C if c == 0 else 0
            return slice(u, u + C), slice(C - u, 2 * C - u)

        def quad_head(i, hh):
            return 4 * i + 2 * (hh % 2) + hh // 2

        KK = {0: 2 * C, 1: C}
        R = {0: 0, 1: 3 * C}
        GROUPS = 4

        def inversion_order():
            order = [("Y", 0), ("Y", 1)]
            for g in range(GROUPS):
                order += [("D", g), ("DT", g)]
                if g + 2 < GROUPS:
                    order.append(("Y", g + 2))
            order += [("Y2", 0), ("Y2", 1)]
            for g in range(GROUPS):
                order.append(("DT2", g))
                if g + 2 < GROUPS:
                    order.append(("Y2", g + 2))
            return order

        ORDER = inversion_order()
        LEV = len(ORDER)
        LEV_BANK = {"Y": (2, 3), "D": (4, 5), "DT": (6, 7), "Y2": (2, 3), "DT2": (4, 5)}

        def lev_bank(i):
            kind, g = ORDER[i]
            return LEV_BANK[kind][g % 2]

        def lev_before(i):
            before = [j for j in range(i) if lev_bank(j) == lev_bank(i)]
            return before[-1] if before else None

        with nc.Block() as block:
            @block.sync
            def _(sp):
                def load(n, name, dst, src):
                    sp.dma_start(dst, src).then_inc(landed[name], 16)

                def need(semaphore, value):
                    sp.wait_ge(semaphore, value)
                    sp.sem_inc(apart, 1)

                def whole(name, n):
                    return scr[name][ds(n, 1)].rearrange("a p j t -> (a p) j t")

                def whole4(name, n):
                    return scr[name][ds(n, 1)].rearrange("a p j s t -> (a p) j (s t)")

                def round_(n, first):
                    if not first:
                        need(a_full, after(n, 16, 0))
                        need(t_full, after(n, 8, 0))
                    load(n, "kb", kb[:], whole4("KB", n))
                    load(n, "qr", qr[:], whole4("QR", n))
                    load(n, "vt", vt[:], whole("V", n))
                    if not first:
                        need(s_full, after(n, 8, 0))
                        need(va_full, after(n, 1, 0))
                    load(n, "q", q[:], whole("Q", n))
                    if first:
                        window, cols = slice(0, BT), slice(BT, 2 * BT)
                    else:
                        window, cols = ds((n - 1) * BT, 2 * BT), slice(0, 2 * BT)
                    for i in range(2):
                        load(n, "kw", kw[i * HD:(i + 1) * HD, :, cols],
                             scr["KVA"][0, :, window].rearrange("(h d) t -> d h t", h=2))
                    load(n, "vw", vw[:, cols], scr["KVA"][1, :, window])
                    if not first:
                        need(ot_read, after(n, 2, 0))
                    load(n, "sa", sa[:], whole("SA", n))
                    if not first:
                        need(z_full, after(n, 4, 0))
                    load(n, "qr_s", qr_s[:], whole4("QR", n))
                    need(a_read, after(n, 16, 16))
                    if not first:
                        need(l_in, after(n, 16, 0))
                    for i in range(P // SUB):
                        rows = slice(i * SUB, (i + 1) * SUB)
                        sp.dma_start(scr["L"][i].rearrange("h s t -> s h t"),
                                     am[rows, :, C + i * SUB:C + (i + 1) * SUB]).then_inc(l_out, 16)
                    need(l_out, after(n, 8 * 16, 8 * 16))
                    if not first:
                        need(sub_done, after(n, 1, 0))
                    sp.dma_start(sub_l[:], scr["L"].rearrange("i h s t -> (i h) s t")).then_inc(l_in, 16)
                    if not first:
                        need(mix_ready, after(n, 1, 0))
                    load(n, "gs", gs[:], whole("GS", n))
                    load(n, "bs", bs[:], whole("BS", n))
                    need(sub_done, after(n, 1, 1))
                    sp.dma_start(scr["X"].rearrange("i h a s t -> (i h) a s t"), sub_x[:]).then_inc(x_out, 16)
                    need(x_out, after(n, 16, 16))
                    if first:
                        need(inited, 1)
                    else:
                        need(lev_full, after(n, LEV, 0))
                        need(lev_read, after(n, LEV, 0))
                    for i in range(P // SUB):
                        rows = slice(i * SUB, (i + 1) * SUB)
                        sp.dma_start(x16[rows, :, :, i * SUB:(i + 1) * SUB].rearrange("s h a t -> s (h a) t"),
                                     scr["X"][i].rearrange("h a s t -> s (h a) t")).then_inc(x_in, 16)

                sp.dma_start(sinks[:], io["sinks"]).then_inc(sinks_landed, 16)
                round_(0, True)
                with sp.Fori(1, NB) as n:
                    round_(n, False)

            @block.gpsimd
            def _(pool):
                count = [0, 0]

                def then(ins):
                    ins.then_inc(pool_steps, 1)
                    count[1] += 1
                    pool.wait_ge(pool_steps, count[0] + count[1])

                def round_(n, first):
                    if not first:
                        pool.wait_ge(f_full, after(n, 2, 0))
                        pool.wait_ge(y_full, after(n, 4, 0))
                        pool.sem_inc(apart, 1)
                    for c in range(2):
                        us, _ = sides(c)
                        ins = nc.gpsimd.memset(uv[us, c], 0.0)
                    then(ins)
                    pool.sem_inc(u_zero, 1)
                    pool.wait_ge(l_in, after(n, 16, 16))
                    if not first:
                        pool.wait_ge(x_out, after(n, 16, 0))
                    pool.sem_inc(apart, 1)
                    then(nc.gpsimd.tensor_copy(sub_x[:, 0], sub_ident[:]))
                    for s in range(SUB - 1):
                        below, width = SUB - 1 - s, s + 1
                        left = sub_l[:, s, s + 1:].unsqueeze(2).broadcast_to([P, below, width])
                        right = sub_x[:, 0, s, 0:width].unsqueeze(1).broadcast_to([P, below, width])
                        t = sub_t[:, 0:below * width].rearrange("p (r c) -> p r c", c=width)
                        then(nc.gpsimd.tensor_tensor(t, left, right, ALU.mult))
                        rows = sub_x[:, 0, s + 1:, 0:width]
                        then(nc.gpsimd.tensor_tensor(rows, rows, t, ALU.subtract))
                    pool.sem_inc(apart, 1)
                    then(nc.gpsimd.tensor_copy(sub_x[:, 1], sub_x[:, 0].rearrange("p s t -> p t s")))
                    pool.sem_inc(sub_done, 1)
                    for c in range(2):
                        if c == 0:
                            if not first:
                                pool.wait_ge(state_new, after(n, 2, 0))
                        else:
                            pool.wait_ge(state_new, after(n, 2, 1))
                        pc = pc_all[:, :, ds(2 * n + c, 1)]
                        for i in range(2):
                            half = slice(i * HD, (i + 1) * HD)
                            then(nc.gpsimd.tensor_tensor(state_d[half], state[half, :, i],
                                                         pc[half].broadcast_to([HD, PAIRS, HD]), ALU.mult))
                        pool.sem_inc(decayed, 1)

                then(nc.gpsimd.memset(sub_ident[:], 0.0))
                then(nc.gpsimd.affine_select(sub_ident[:], sub_ident[:], pattern=[[1, SUB], [-1, SUB]],
                                             compare_op=ALU.not_equal, fill=1.0, base=0,
                                             channel_multiplier=0))
                then(nc.gpsimd.memset(sub_x[:], 0.0))
                then(nc.gpsimd.memset(state[:], 0.0))
                then(nc.gpsimd.memset(x16[:], 0.0))
                pool.sem_inc(inited, 1)
                before = count[1]
                round_(0, True)
                per = count[1] - before
                base = count[1]
                with pool.Fori(1, NB) as n:
                    count[0], count[1] = base + (n - 1) * per, 0
                    round_(n, False)
                    assert count[1] == per

            @block.scalar
            def _(act):
                def copy(dst, src, scale=1.0):
                    return nc.scalar.activation(dst, src, ACT.Copy, scale=scale)

                def exponentials(n, first, i):
                    lo = BT if first else 0
                    act.wait_ge(negmax, after(n, 4, i + 1))
                    for hh in range(4):
                        at = 4 * i + hh
                        s = score[i % 2][:, hh, lo:]
                        nc.scalar.activation(s, s, ACT.Exp, bias=top[:, 1, at:at + 1],
                                             accum_out=top[:, 2, at:at + 1])
                    heads = slice(4 * i, 4 * i + 4)
                    nc.scalar.activation(top[:, 3, heads], part[:, heads], ACT.Exp).then_inc(p_ready, 1)

                def turned(n, i):
                    for m in range(2):
                        act.wait_ge(pt_full, after(n, 8, 2 * i + m + 1))
                        w = pt_width[0]
                        copy(pt[i % 2][:, m, 0:w], psum[:, 4 + m, 0:w]).then_inc(pt_read, 1)

                pt_width = [0]

                def mix_out(n, group):
                    return scr["MIX"][ds(n, 1), :, group * PAIRS:(group + 1) * PAIRS].rearrange(
                        "b p k t -> (b p) k t")

                def round_(n, first):
                    pt_width[0] = 2 * P if first else 4 * P
                    for j in range(PAIRS):
                        act.wait_ge(t_full, after(n, 8, j + 1))
                        if j == 0:
                            act.wait_ge(u_zero, after(n, 1, 1))
                        bank = psum[:, 4 + j % 2]
                        copy(kbt[:, :, j], bank[:, 0:2 * P].rearrange("p (c k) -> p c k", c=2))
                        for c in range(2):
                            _, vs = sides(c)
                            ins = copy(uv[vs, c, 2 * j:2 * j + 2].rearrange("p h d -> p (h d)"),
                                       bank[vs, 2 * P:3 * P])
                        ins.then_inc(t_read, 1)
                    act.wait_ge(va_full, after(n, 1, 1))
                    if first:
                        copy(va[:, 1], psum[:, 4, P:2 * P]).then_inc(va_read, 1)
                    else:
                        copy(va[:].rearrange("p w d -> p (w d)"), psum[:, 4, 0:2 * P]).then_inc(va_read, 1)
                    exponentials(n, first, 0)
                    for i in range(1, 4):
                        exponentials(n, first, i)
                        turned(n, i - 1)
                    turned(n, 3)
                    act.wait_ge(mixa_ready, after(n, 1, 1))
                    act.dma_start(mix_out(n, 1), mix_a[:]).then_inc(mixa_stored, 16)
                    if not first:
                        act.wait_ge(mix_ready, after(n, 1, 0))
                        act.dma_start(mix_out(n - 1, 0), mix[:]).then_inc(mix_stored, 16)
                    for c in range(2):
                        us, vs = sides(c)
                        for i in range(2):
                            act.wait_ge(z_full, after(n, 4, 2 * c + i + 1))
                            z = psum[us, 6 + i].rearrange("p (h d) -> p h d", d=HD)
                            copy(zs[us, 8 * i:8 * i + 8], z, scale=-1.0).then_inc(z_read, 1)
                        for i in range(2):
                            act.wait_ge(y_full, after(n, 4, 2 * c + i + 1))
                            src = psum[vs, 6 + i].rearrange("p (h d) -> p h d", d=HD)
                            copy(y[vs, 8 * i:8 * i + 8], src).then_inc(y_read, 1)
                    act.wait_ge(y_centred, after(n, 1, 1))
                    nc.scalar.activation(ysq[:], y[:], ACT.Square).then_inc(y_squared, 1)
                    act.wait_ge(y_var, after(n, 1, 1))
                    nc.scalar.activation(stat[:, 1], stat[:, 1], ACT.Sqrt, bias=eps[:, 0:1],
                                         scale=1.0 / HD).then_inc(y_root, 1)

                act.wait_ge(inited, 2)
                round_(0, True)
                with act.Fori(1, NB) as n:
                    round_(n, False)
                act.wait_ge(mix_ready, NB)
                act.dma_start(mix_out(NB - 1, 0), mix[:]).then_inc(mix_stored, 16)
                act.wait_ge(mix_stored, 16 * (NB + 1))
                act.wait_ge(mixa_stored, 16 * NB)

            @block.vector
            def _(dve):
                count = [0, 0]

                def then(ins):
                    ins.then_inc(steps, 1)
                    count[1] += 1
                    dve.wait_ge(steps, count[0] + count[1])

                def gated(n):
                    dve.wait_ge(landed["gs"], after(n, 16, 0))
                    dve.wait_ge(landed["bs"], after(n, 16, 0))
                    dve.wait_ge(mix_stored, after(n, 16, 0))
                    for i in range(2):
                        dve.wait_ge(yt_full, after(n - 1, 2, i + 1))
                        js = slice(4 * i, 4 * i + 4)
                        then(nc.vector.tensor_tensor(mix[:, js], psum[:, 6 + i].rearrange("p (j t) -> p j t", t=BT),
                                                     gs[:, js], ALU.mult))
                        dve.sem_inc(yt_read, 1)
                    then(nc.vector.tensor_tensor(mix[:], mix[:], bs[:], ALU.add))
                    dve.sem_inc(mix_ready, 1)

                def softmax_scores(n, first, i):
                    lo = BT if first else 0
                    w = 2 * BT - lo
                    for par_ in range(2):
                        dve.wait_ge(s_full, after(n, 8, 2 * i + par_ + 1))
                        for jj in range(2):
                            hh = 2 * par_ + jj
                            slope = 2.0 ** (-8.0 * (quad_head(i, hh) + 1) / HEADS)
                            src = psum[:, 2 * (i % 2) + par_, jj * w:(jj + 1) * w]
                            ins = nc.vector.scalar_tensor_tensor(
                                score[i % 2][:, hh, lo:], const("dist")[:, lo:], -slope, src,
                                ALU.mult, ALU.add)
                    then(ins)
                    dve.sem_inc(s_read, 1)
                    heads = slice(4 * i, 4 * i + 4)
                    then(nc.vector.tensor_reduce(top[:, 0, heads], score[i % 2][:, :, lo:], AX, ALU.max))
                    then(nc.vector.scalar_tensor_tensor(top[:, 1, heads], top[:, 0, heads], -1.0,
                                                        neg_sinks[:, heads], ALU.mult, ALU.min))
                    then(nc.vector.tensor_tensor(part[:, heads], top[:, 1, heads], neg_sinks[:, heads],
                                                 ALU.subtract))
                    dve.sem_inc(negmax, 1)

                def outputs(n, i):
                    heads = slice(4 * i, 4 * i + 4)
                    dve.wait_ge(p_ready, after(n, 4, i + 1))
                    then(nc.vector.tensor_tensor(part[:, heads], top[:, 2, heads], top[:, 3, heads], ALU.add))
                    then(nc.vector.reciprocal(part[:, heads], part[:, heads]))
                    dve.wait_ge(o_full, after(n, 4, i + 1))
                    then(nc.vector.tensor_tensor(
                        o[:, heads].rearrange("p (b a) d -> p a b d", a=2),
                        psum[:, 6 + i % 2, 0:4 * HD].rearrange("p (a b d) -> p a b d", a=2, b=2),
                        part[:, heads].rearrange("p (a b) -> p a b", a=2).unsqueeze(3)
                        .broadcast_to([P, 2, 2, HD]), ALU.mult))
                    dve.sem_inc(o_read, 1)

                def round_(n, first):
                    for h in range(HEADS):
                        dve.wait_ge(a_full, after(n, 16, h + 1))
                        if h == 0 and not first:
                            dve.wait_ge(l_out, after(n, 8 * 16, 0))
                        bank = 2 * ((h // 2) % 2) + h % 2
                        then(nc.vector.tensor_tensor(am[:, h], psum[:, bank, 0:4 * C], const("amask"), ALU.mult))
                        dve.sem_inc(a_read, 1)
                    if not first:
                        gated(n)
                    softmax_scores(n, first, 0)
                    softmax_scores(n, first, 1)
                    outputs(n, 0)
                    softmax_scores(n, first, 2)
                    outputs(n, 1)
                    softmax_scores(n, first, 3)
                    outputs(n, 2)
                    outputs(n, 3)
                    dve.wait_ge(landed["sa"], after(n, 16, 16))
                    if not first:
                        dve.wait_ge(mixa_stored, after(n, 16, 0))
                    for i in range(2):
                        js = slice(4 * i, 4 * i + 4)
                        dve.wait_ge(ot_full, after(n, 2, i + 1))
                        then(nc.vector.tensor_tensor(mix_a[:, js], psum[:, i].rearrange("p (j t) -> p j t", t=BT),
                                                     sa[:, js], ALU.mult))
                        dve.sem_inc(ot_read, 1)
                    dve.sem_inc(mixa_ready, 1)
                    for i, (kind, g) in enumerate(ORDER):
                        hs = slice(4 * g, 4 * g + 4)
                        dve.wait_ge(lev_full, after(n, LEV, i + 1))
                        src = psum[:, lev_bank(i)].rearrange("p (h t) -> p h t", t=P)
                        if kind in ("Y", "Y2"):
                            mask = const("m16" if kind == "Y" else "m32")
                            ins = nc.vector.tensor_tensor(ym[:, hs], src, many(mask, 4), ALU.mult)
                        elif kind == "D":
                            ins = nc.vector.tensor_tensor(x32[:, hs], x16[:, hs, 0], src, ALU.subtract)
                        elif kind == "DT":
                            ins = nc.vector.tensor_tensor(xt[:, hs], x16[:, hs, 1], src, ALU.subtract)
                        else:
                            ins = nc.vector.tensor_tensor(xt[:, hs], xt[:, hs], src, ALU.subtract)
                        then(ins)
                        dve.sem_inc(lev_read, 1)
                    for c in range(2):
                        us, _ = sides(c)
                        for i in range(2):
                            dve.wait_ge(u_full, after(n, 4, 2 * c + i + 1))
                            then(nc.vector.tensor_copy(uv[us, c, 8 * i:8 * i + 8].rearrange("p h d -> p (h d)"),
                                                       psum[us, i]))
                            dve.sem_inc(u_read, 1)
                        pc = pc_all[:, :, ds(2 * n + c, 1)]
                        dve.wait_ge(f_full, after(n, 2, c + 1))
                        then(nc.vector.tensor_tensor(fresh[:], psum[:, 2 + c].rearrange("p (j d) -> p j d", d=HD),
                                                     pc.broadcast_to([P, PAIRS, HD]), ALU.mult))
                        dve.sem_inc(state_read, 1)
                        dve.wait_ge(decayed, after(n, 2, c + 1))
                        for i in range(2):
                            half = slice(i * HD, (i + 1) * HD)
                            then(nc.vector.tensor_tensor(state[half, :, i], state_d[half], fresh[half], ALU.add))
                        dve.sem_inc(state_new, 1)
                    dve.wait_ge(y_read, after(n, 4, 4))
                    then(nc.vector.tensor_reduce(stat[:, 0], y[:], AX, ALU.add))
                    then(nc.vector.tensor_scalar(stat[:, 0], stat[:, 0], -1.0 / HD, None, ALU.mult))
                    then(nc.vector.tensor_tensor(y[:], y[:], stat[:, 0].unsqueeze(2).broadcast_to([P, HEADS, HD]),
                                                 ALU.add))
                    dve.sem_inc(y_centred, 1)
                    dve.wait_ge(y_squared, after(n, 1, 1))
                    then(nc.vector.tensor_reduce(stat[:, 1], ysq[:], AX, ALU.add))
                    dve.sem_inc(y_var, 1)
                    dve.wait_ge(y_root, after(n, 1, 1))
                    then(nc.vector.reciprocal(stat[:, 1], stat[:, 1]))
                    then(nc.vector.tensor_tensor(y[:], y[:], stat[:, 1].unsqueeze(2).broadcast_to([P, HEADS, HD]),
                                                 ALU.mult))
                    dve.sem_inc(y_norm, 1)

                then(nc.vector.memset(eps[:], LNX_EPS))
                dve.sem_inc(inited, 1)
                dve.sem_inc(mix_stored, 16)
                dve.wait_ge(sinks_landed, 16)
                then(nc.vector.tensor_scalar(neg_sinks[:], sinks[:], -1.0, None, ALU.mult))
                before = count[1]
                round_(0, True)
                per = count[1] - before + 3
                base = count[1]
                with dve.Fori(1, NB) as n:
                    count[0], count[1] = base + (n - 1) * per, 0
                    round_(n, False)
                    assert count[1] == per, (count, per)
                count[0], count[1] = base + (NB - 1) * per, 0
                gated(NB)

            @block.tensor
            def _(pe):
                ident = const("ident")

                def turn(dst, src):
                    return nc.tensor.transpose(dst, src, ident)

                def turn_y(n):
                    pe.wait_ge(y_norm, after(n, 1, 0))
                    pe.wait_ge(y_read, after(n, 4, 0))
                    for i in range(2):
                        for jj in range(4):
                            j = 4 * i + jj
                            mm = turn(psum[:, 6 + i, jj * P:(jj + 1) * P],
                                      y[:, 2 * j:2 * j + 2].rearrange("p h d -> p (h d)"))
                        mm.then_inc(yt_full, 1)

                def scores(n, first, i):
                    lo = BT if first else 0
                    w = 2 * BT - lo
                    if i >= 2:
                        pe.wait_ge(s_read, after(n, 4, i - 1))
                    for par_ in range(2):
                        rows = slice(par_ * HD, (par_ + 1) * HD)
                        for jj in range(2):
                            j = 2 * i + jj
                            mm = nc.tensor.matmul(psum[:, 2 * (i % 2) + par_, jj * w:(jj + 1) * w], q[rows, j],
                                                  kw[rows, j // 4, lo:], start=True, stop=True)
                        mm.then_inc(s_full, 1)

                def turn_p(n, first, i):
                    pe.wait_ge(p_ready, after(n, 4, i + 1))
                    for m in range(2):
                        if i == 0:
                            pe.wait_ge(va_read, after(n, 1, 1))
                        else:
                            pe.wait_ge(pt_read, after(n, 8, 2 * i + m - 1))
                        at = 0
                        for hh in (2 * m, 2 * m + 1):
                            for wnd in ((1,) if first else (0, 1)):
                                mm = turn(psum[:, 4 + m, at:at + P], score[i % 2][:, hh, wnd * BT:(wnd + 1) * BT])
                                at += P
                        mm.then_inc(pt_full, 1)

                def values(n, first, i):
                    pe.wait_ge(pt_read, after(n, 8, 2 * i + 2))
                    if i >= 2:
                        pe.wait_ge(o_read, after(n, 4, i - 1))
                    elif not first:
                        pe.wait_ge(yt_read, after(n, 2, 0))
                    kv = i // 2
                    wnds = (1,) if first else (0, 1)
                    for hh in range(4):
                        for x, wnd in enumerate(wnds):
                            at = (hh % 2) * len(wnds) * P + x * P
                            mm = nc.tensor.matmul(psum[:, 6 + i % 2, hh * HD:(hh + 1) * HD],
                                                  pt[i % 2][:, hh // 2, at:at + P],
                                                  va[:, wnd, kv * HD:(kv + 1) * HD],
                                                  start=(x == 0), stop=(x == len(wnds) - 1))
                    mm.then_inc(o_full, 1)

                def round_(n, first):
                    pe.wait_ge(landed["kb"], after(n, 16, 16))
                    pe.wait_ge(landed["qr"], after(n, 16, 16))
                    pe.wait_ge(landed["vt"], after(n, 16, 16))
                    if not first:
                        pe.wait_ge(state_read, after(n, 2, 0))
                        pe.wait_ge(u_read, after(n, 4, 0))
                    for j in range(PAIRS):
                        for par_ in range(2):
                            h = 2 * j + par_
                            rows = slice(par_ * HD, (par_ + 1) * HD)
                            bank = 2 * (j % 2) + par_
                            if j >= 2:
                                pe.wait_ge(a_read, after(n, 16, h - 3))
                            for c in range(2):
                                dst = psum[:, bank, 0:4 * C].rearrange("p (s t) -> p s t", t=C)[:, c::2]
                                mm = nc.tensor.matmul(dst, kb[rows, j, c * P:(c + 1) * P],
                                                      qr[rows, j, c * P:(c + 1) * P], start=True, stop=True)
                            mm.then_inc(a_full, 1)
                        bank = psum[:, 4 + j % 2]
                        if j >= 2:
                            pe.wait_ge(t_read, after(n, 8, j - 1))
                        for c in range(2):
                            turn(bank[:, c * P:(c + 1) * P], kb[:, j, c * P:(c + 1) * P])
                        turn(bank[:, 2 * P:3 * P], vt[:, j]).then_inc(t_full, 1)
                    if not first:
                        turn_y(n)
                    pe.wait_ge(landed["vw"], after(n, 16, 16))
                    pe.wait_ge(landed["q"], after(n, 16, 16))
                    pe.wait_ge(landed["kw"], after(n, 32, 32))
                    pe.wait_ge(t_read, after(n, 8, 8))
                    if first:
                        turn(psum[:, 4, P:2 * P], vw[:, BT:]).then_inc(va_full, 1)
                    else:
                        turn(psum[:, 4, 0:P], vw[:, 0:BT])
                        turn(psum[:, 4, P:2 * P], vw[:, BT:]).then_inc(va_full, 1)
                    pe.wait_ge(a_read, after(n, 16, 16))
                    scores(n, first, 0)
                    scores(n, first, 1)
                    turn_p(n, first, 0)
                    values(n, first, 0)
                    for i in (2, 3):
                        scores(n, first, i)
                        turn_p(n, first, i - 1)
                        values(n, first, i - 1)
                    turn_p(n, first, 3)
                    values(n, first, 3)
                    pe.wait_ge(s_read, after(n, 4, 4))
                    for i in range(2):
                        pe.wait_ge(o_read, after(n, 4, 2 * i + 2))
                        for jj in range(4):
                            j = 4 * i + jj
                            mm = turn(psum[:, i, jj * P:(jj + 1) * P],
                                      o[:, 2 * j:2 * j + 2].rearrange("p h d -> p (h d)"))
                        mm.then_inc(ot_full, 1)
                    pe.wait_ge(x_in, after(n, 8 * 16, 8 * 16))
                    pe.wait_ge(pt_read, after(n, 8, 8))
                    done = {}
                    for i, (kind, g) in enumerate(ORDER):
                        needs = {"Y": [], "D": [("Y", g)], "DT": [("Y", g)], "Y2": [("D", g), ("DT", g)],
                                 "DT2": [("Y2", g), ("DT", g)]}[kind]
                        needs = [done[x] for x in needs] + [lev_before(i)]
                        needs = [x for x in needs if x is not None]
                        if needs:
                            pe.wait_ge(lev_read, after(n, LEV, max(needs) + 1))
                        done[(kind, g)] = i
                        for hh in range(4):
                            h = 4 * g + hh
                            lhs, rhs = {
                                "Y": (am[:, h, C:3 * C], x16[:, h, 0]),
                                "D": (x16[:, h, 1], ym[:, h]),
                                "DT": (ym[:, h], x16[:, h, 1]),
                                "Y2": (am[:, h, C:3 * C], x32[:, h]),
                                "DT2": (ym[:, h], xt[:, h]),
                            }[kind]
                            mm = nc.tensor.matmul(psum[:, lev_bank(i), hh * P:(hh + 1) * P], lhs, rhs,
                                                  start=True, stop=True)
                        mm.then_inc(lev_full, 1)
                    pe.wait_ge(landed["qr_s"], after(n, 16, 16))
                    pe.wait_ge(lev_read, after(n, LEV, LEV))
                    pe.wait_ge(ot_read, after(n, 2, 2))
                    for c in range(2):
                        us, vs = sides(c)
                        cols = slice(c * P, (c + 1) * P)
                        if c == 0:
                            if first:
                                pe.wait_ge(inited, 2)
                            else:
                                pe.wait_ge(state_new, after(n, 2, 0))
                        else:
                            pe.wait_ge(state_new, after(n, 2, 1))
                        for i in range(2):
                            if c == 1:
                                pe.wait_ge(y_read, after(n, 4, i + 1))
                            for jj in range(4):
                                j = 4 * i + jj
                                nc.tensor.matmul(psum[:, 6 + i, jj * P:(jj + 1) * P], qr_s[:, j, cols],
                                                 state[:, j].rearrange("p h d -> p (h d)"),
                                                 start=(jj == 0), stop=False, skip_group_check=True)
                            for hh in range(8):
                                h = 8 * i + hh
                                mm = nc.tensor.matmul(psum[us, 6 + i, hh * HD:(hh + 1) * HD],
                                                      am[:, h, KK[c]:KK[c] + C], uv[:, c, h],
                                                      start=False, stop=False, skip_group_check=True)
                            mm.then_inc(z_full, 1)
                        for i in range(2):
                            pe.wait_ge(z_read, after(n, 4, 2 * c + i + 1))
                            if c == 1:
                                pe.wait_ge(u_read, after(n, 4, i + 1))
                            pe.sem_inc(apart, 1)
                            for hh in range(8):
                                h = 8 * i + hh
                                mm = nc.tensor.matmul(psum[us, i, hh * HD:(hh + 1) * HD], xt[us, h, us],
                                                      zs[us, h], start=True, stop=True)
                            mm.then_inc(u_full, 1)
                        for i in range(2):
                            pe.wait_ge(u_read, after(n, 4, 2 * c + i + 1))
                            for hh in range(8):
                                h = 8 * i + hh
                                half = slice((h % 2) * HD, (h % 2 + 1) * HD)
                                mm = nc.tensor.matmul(psum[half, 2 + c, (h // 2) * HD:(h // 2 + 1) * HD],
                                                      kbt[:, c, h // 2, half], uv[:, c, h],
                                                      start=True, stop=True, skip_group_check=True)
                        mm.then_inc(f_full, 1)
                        for i in range(2):
                            for hh in range(8):
                                h = 8 * i + hh
                                mm = nc.tensor.matmul(psum[vs, 6 + i, hh * HD:(hh + 1) * HD],
                                                      am[:, h, R[c]:R[c] + C], uv[:, c, h],
                                                      start=False, stop=(hh == 7), skip_group_check=True)
                            mm.then_inc(y_full, 1)

                pe.wait_ge(inited, 2)
                round_(0, True)
                with pe.Fori(1, NB) as n:
                    round_(n, False)
                turn_y(NB)


def stage_c(nc, io, scr, cst):
    with ExitStack() as ctx:
        def sb(name, shape, dt=F32):
            return ctx.enter_context(nc.sbuf_tensor("c_" + name, shape, dt))

        def sem(name):
            return ctx.enter_context(nc.semaphore("c_" + name))

        m_in = [sb(f"m_in{i}", [P, HALF]) for i in range(4)]
        m_hi = sb("m_hi", [P, 2, KC, HALF], F32R)
        m_lo = sb("m_lo", [P, 2, KC, HALF], F32R)
        w_raw = sb("w_raw", [P, KH * P])
        w_hi = [sb(f"w_hi{i}", [P, KH * P], F32R) for i in range(2)]
        w_lo = [sb(f"w_lo{i}", [P, KH * P], F32R) for i in range(2)]
        x_in = sb("x_in", [P, HALF])
        xn = sb("xn", [P, KC, HALF])
        sq = sb("sq", [P, HALF])
        acc = sb("acc", [P, HALF])
        rms = sb("rms", [P, HALF])
        gain = sb("gain", [P, KC])
        eps = sb("eps", [P, 1])
        psum = ctx.enter_context(nc.psum_tensor("psum_c", [P, 8, HALF], F32))

        gain_landed = sem("gain_landed")
        m_landed = [sem(f"m_landed{i}") for i in range(4)]
        m_high, m_ready = sem("m_high"), sem("m_ready")
        w_landed = sem("w_landed")
        w_high = [sem(f"w_high{i}") for i in range(2)]
        w_ready = [sem(f"w_ready{i}") for i in range(2)]
        w_used = [sem(f"w_used{i}") for i in range(2)]
        x_landed = sem("x_landed")
        tile_done, tile_read = sem("tile_done"), sem("tile_read")
        squared, summed, gained = sem("squared"), sem("summed"), sem("gained")
        mean_done, rooted, rms_ready = sem("mean_done"), sem("rooted"), sem("rms_ready")
        scaled_pool, scaled_dve = sem("scaled_pool"), sem("scaled_dve")
        out_stored = [sem(f"out_stored{i}") for i in range(3)]
        inited = sem("inited")

        BY_DVE = 10
        LAST = 2 * KC - 1

        with nc.Block() as block:
            @block.sync
            def _(sp):
                def load_half(s, t, half, first=False):
                    if half == 1:
                        sp.wait_ge(w_ready[0], s + 1)
                    elif not first:
                        sp.wait_ge(w_ready[1], s)
                    sp.dma_start(w_raw[:], io["w_out"][ds(t, 1), half].rearrange("a p n -> (a p) n")
                                 ).then_inc(w_landed, 16)

                def load_x(s, t, h, first=False):
                    if not first:
                        sp.wait_ge(tile_read, s)
                    sp.dma_start(x_in[:], io["x_t"][ds(t, 1), :, h * HALF:(h + 1) * HALF]
                                 .rearrange("a p n -> (a p) n")).then_inc(x_landed, 16)

                def load_mix(i):
                    h, c = divmod(i, KC)
                    if i >= 4:
                        sp.wait_ge(m_ready, i - 3)
                    src = scr["MIX"][h * NB // 2:(h + 1) * NB // 2, :, c].rearrange("b p t -> p b t")
                    sp.dma_start(m_in[i % 4][:].rearrange("p (b t) -> p b t", t=BT), src
                                 ).then_inc(m_landed[i % 4], 16)

                sp.dma_start(gain[:], io["final_gain"]).then_inc(gain_landed, 16)
                for i in range(4):
                    load_mix(i)
                load_half(0, 0, 0, True)
                for i in range(4, KC):
                    load_mix(i)
                load_half(0, 0, 1)
                load_x(0, 0, 0, True)
                for i in range(KC, 2 * KC):
                    load_mix(i)
                for h in range(2):
                    if h == 1:
                        for half in range(2):
                            load_half(KC, 0, half)
                        load_x(KC, 0, 1)
                    with sp.Fori(1, KC) as t:
                        for half in range(2):
                            load_half(h * KC + t, t, half)
                        load_x(h * KC + t, t, h)

            @block.scalar
            def _(act):
                def high_half(s, half, first=False):
                    act.wait_ge(w_landed, 32 * s + 16 * (half + 1))
                    if not first:
                        act.wait_ge(w_used[half], s)
                    nc.scalar.activation(w_hi[half][:], w_raw[:], ACT.Copy).then_inc(w_high[half], 1)

                def mix_high(i):
                    h, c = divmod(i, KC)
                    act.wait_ge(m_landed[i % 4], 16 * (i // 4 + 1))
                    nc.scalar.activation(m_hi[:, h, c], m_in[i % 4][:], ACT.Copy).then_inc(m_high, 1)

                def square(s, t, first=False):
                    act.wait_ge(tile_read, s + 1)
                    if not first:
                        act.wait_ge(summed, s)
                    tile = xn[:, ds(t, 1)].rearrange("p a t -> p (a t)")
                    nc.scalar.activation(sq[:], tile, ACT.Square).then_inc(squared, 1)
                    act.wait_ge(squared, s + 1)
                    nc.scalar.activation(tile, tile, ACT.Copy, scale=gain[:, ds(t, 1)]).then_inc(gained, 1)

                def root(h):
                    act.wait_ge(mean_done, h + 1)
                    nc.scalar.activation(rms[:], psum[:, 4], ACT.Sqrt, bias=eps[:, 0:1]).then_inc(rooted, 1)

                act.wait_ge(inited, 1)
                act.wait_ge(gain_landed, 16)
                high_half(0, 0, True)
                for i in range(KC):
                    mix_high(i)
                high_half(0, 1, True)
                for i in range(KC, 2 * KC):
                    mix_high(i)
                for h in range(2):
                    s = h * KC
                    if h == 1:
                        high_half(s, 0)
                        high_half(s, 1)
                        square(s - 1, KC - 1)
                        root(0)
                    high_half(s + 1, 0)
                    high_half(s + 1, 1)
                    square(s, 0, first=(h == 0))
                    with act.Fori(2, KC) as t:
                        high_half(s + t, 0)
                        high_half(s + t, 1)
                        square(s + t - 1, t - 1)
                square(LAST, KC - 1)
                root(1)

            @block.vector
            def _(dve):
                def low_half(s, half):
                    dve.wait_ge(w_high[half], s + 1)
                    nc.vector.tensor_tensor(w_lo[half][:], w_raw[:], w_hi[half][:].bitcast(F32),
                                            ALU.subtract).then_inc(w_ready[half], 1)

                def mix_low(i):
                    h, c = divmod(i, KC)
                    dve.wait_ge(m_high, i + 1)
                    nc.vector.tensor_tensor(m_lo[:, h, c], m_in[i % 4][:], m_hi[:, h, c].bitcast(F32),
                                            ALU.subtract).then_inc(m_ready, 1)

                def add(s, t, bank, h):
                    dve.wait_ge(tile_done, s + 1)
                    dve.wait_ge(x_landed, 16 * (s + 1))
                    if h == 1:
                        dve.wait_ge(out_stored[0 if isinstance(t, int) and t == 0 else 1], 16 * KC // 2)
                    nc.vector.tensor_tensor(xn[:, ds(t, 1)].rearrange("p a t -> p (a t)"), psum[:, bank],
                                            x_in[:], ALU.add).then_inc(tile_read, 1)

                def invert(h):
                    dve.wait_ge(rooted, h + 1)
                    nc.vector.reciprocal(rms[:], rms[:]).then_inc(rms_ready, 1)

                nc.vector.memset(eps[:], RMS_EPS).then_inc(inited, 1)
                low_half(0, 0)
                for i in range(KC):
                    mix_low(i)
                low_half(0, 1)
                for i in range(KC, 2 * KC):
                    mix_low(i)
                for h in range(2):
                    s = h * KC
                    if h == 1:
                        low_half(s, 0)
                        low_half(s, 1)
                        add(s - 1, KC - 1, 1, 0)
                        invert(0)
                    low_half(s + 1, 0)
                    low_half(s + 1, 1)
                    add(s, 0, 0, h)
                    with dve.Fori(1, KC // 2) as m:
                        for i in range(2):
                            low_half(s + 2 * m + i, 0)
                            low_half(s + 2 * m + i, 1)
                            add(s + 2 * m + i - 1, 2 * m + i - 1, 1 - i, h)
                add(LAST, KC - 1, 1, 1)
                invert(1)
                dve.wait_ge(rms_ready, 2)
                dve.wait_ge(gained, 2 * KC)
                for t in range(BY_DVE):
                    nc.vector.tensor_tensor(xn[:, t], xn[:, t], rms[:], ALU.mult).then_inc(scaled_dve, 1)

            @block.gpsimd
            def _(pool):
                def accumulate(s, first=False):
                    pool.wait_ge(squared, s + 1)
                    if first:
                        ins = nc.gpsimd.tensor_copy(acc[:], sq[:])
                    else:
                        pool.wait_ge(summed, s)
                        ins = nc.gpsimd.tensor_tensor(acc[:], acc[:], sq[:], ALU.add)
                    ins.then_inc(summed, 1)

                def scale(tiles):
                    for t in tiles:
                        nc.gpsimd.tensor_tensor(xn[:, t], xn[:, t], rms[:], ALU.mult).then_inc(scaled_pool, 1)

                def store(h, t):
                    pool.dma_start(io["out"][t, :, h * HALF:(h + 1) * HALF], xn[:, t]
                                   ).then_inc(out_stored[2 if h else t // (KC // 2)], 16)

                def scale_and_store(h, tiles, done):
                    scale(tiles)
                    for t in tiles:
                        done += 1
                        pool.wait_ge(scaled_pool, done)
                        store(h, t)
                    return done

                accumulate(0, True)
                with pool.Fori(1, KC) as t:
                    accumulate(t)
                pool.wait_ge(mean_done, 1)
                pool.wait_ge(rms_ready, 1)
                pool.wait_ge(gained, KC)
                done = scale_and_store(0, range(0, KC // 2), 0)
                accumulate(KC, True)
                done = scale_and_store(0, range(KC // 2, KC), done)
                with pool.Fori(KC + 1, 2 * KC) as s:
                    accumulate(s)
                pool.wait_ge(rms_ready, 2)
                pool.wait_ge(gained, 2 * KC)
                scale(range(BY_DVE, KC))
                for t in range(BY_DVE):
                    pool.wait_ge(scaled_dve, t + 1)
                    store(1, t)
                for t in range(BY_DVE, KC):
                    done += 1
                    pool.wait_ge(scaled_pool, done)
                    store(1, t)
                for i in range(2):
                    pool.wait_ge(out_stored[i], 16 * KC // 2)
                pool.wait_ge(out_stored[2], 16 * KC)

            @block.tensor
            def _(pe):
                def project(s, bank, h, pace=False, between=None):
                    if between is not None or not pace:
                        pe.wait_ge(tile_read, s - 1)
                    for half in range(2):
                        pe.wait_ge(w_ready[half], s + 1)
                        for kk in range(KH):
                            c = half * KH + kk
                            if pace:
                                pe.wait_ge(m_ready, h * KC + c + 1)
                            cols = slice(kk * P, (kk + 1) * P)
                            for wt, mt in ((w_hi, m_hi), (w_hi, m_lo), (w_lo, m_hi)):
                                mm = nc.tensor.matmul(psum[:, bank], wt[half][:, cols], mt[:, h, c],
                                                      start=(c == 0 and wt is w_hi and mt is m_hi),
                                                      stop=(c == KC - 1 and wt is w_lo))
                        mm.then_inc(w_used[half], 1)
                        if half == 0 and between is not None:
                            between()
                    pe.wait_ge(w_used[1], s + 1)
                    pe.sem_inc(tile_done, 1)

                def mean(h):
                    pe.wait_ge(summed, (h + 1) * KC)
                    nc.tensor.matmul(psum[:, 4], cst[:, slice(*CONSTS["mean"])], acc[:],
                                     start=True, stop=True).then_inc(mean_done, 1)

                for h in range(2):
                    s = h * KC
                    if h == 0:
                        project(0, 0, 0, pace=True)
                        pe.wait_ge(m_ready, KC)
                        project(1, 1, 0, pace=True)
                    else:
                        pe.wait_ge(m_ready, 2 * KC)
                        project(s, 0, 1, between=lambda: mean(0))
                        project(s + 1, 1, 1)
                    with pe.Fori(1, KC // 2) as m:
                        project(s + 2 * m, 0, h)
                        project(s + 2 * m + 1, 1, h)
                mean(1)


SCRATCH = {
    "KB": (NB, P, PAIRS, 4, C), "QR": (NB, P, PAIRS, 4, C),
    "V": (NB, P, PAIRS, BT), "GS": (NB, P, PAIRS, BT), "BS": (NB, P, PAIRS, BT),
    "Q": (NB, P, PAIRS, BT), "SA": (NB, P, PAIRS, BT),
    "KVA": (2, P, T), "MIX": (NB, P, KC, BT),
    "L": (P // SUB, HEADS, SUB, SUB), "X": (P // SUB, HEADS, 2, SUB, SUB),
}


def layout(inputs):
    a = {n: np.asarray(v) for n, v in inputs.items()}

    def tiles(w, starts):
        w = w.reshape(2, KH, P, -1)
        w = np.stack([w[..., s:s + P] for s in starts])
        return np.ascontiguousarray(w.transpose(0, 1, 3, 2, 4)).reshape(len(starts), 2, P, KH * P)

    def channels(v, n):
        return np.asarray(v).reshape(n, P).T

    att = RWKV_COLS
    starts = [3 * RW, att + AW, att + AW + KVW]
    for j in range(PAIRS):
        starts += [j * P, RW + j * P, 2 * RW + j * P, 3 * RW + 2 * LORA + j * P,
                   att + j * P, att + AW + 2 * KVW + j * P]
    mu = a["mu_rwkv"][0]
    per = {"mu_r": mu[:RW], "mu_k": mu[RW:2 * RW], "mu_v": mu[2 * RW:3 * RW],
           "mu_g": mu[3 * RW + 2 * LORA:], "w0": a["w0"], "a0": a["a0"], "k_k": a["k_k"],
           "k_a": a["k_a"], "r_k": a["r_k"], "gain": a["lnx_gain"], "bias": a["lnx_bias"]}
    par = np.stack([channels(per[n], PAIRS) for n in PAR], axis=2)
    lora_up = np.concatenate([a["w_up"][0], a["a_up"][0]]).reshape(2 * LORA, PAIRS, P).transpose(1, 0, 2)
    quads = [4 * i + 2 * (hh % 2) + hh // 2 for i in range(HEADS // 4) for hh in range(4)]
    x_t = np.ascontiguousarray(a["x"][0].T).reshape(KC, P, T)
    out = {
        "x_t": x_t,
        "w_in": tiles(a["w_in"][0], starts),
        "w_out": tiles(a["w_out"][0], range(0, D, P)),
        "par": par,
        "par1": np.concatenate([channels(a["norm_gain"][0], KC), mu[3 * RW:3 * RW + 2 * LORA, None]], axis=1),
        "final_gain": channels(a["final_gain"], KC),
        "sinks": np.broadcast_to(a["attn_sinks"][0, quads], (P, HEADS)),
        "lora_up": lora_up,
        "consts": constants(),
    }
    return {n: np.ascontiguousarray(v) for n, v in out.items()}


def program(nc, io, scr):
    with ExitStack() as ctx:
        pc_all = ctx.enter_context(nc.sbuf_tensor("pc_all", [P, PAIRS, NC_], F32))
        cst = ctx.enter_context(nc.sbuf_tensor("cst", [P, CONST_COLS], F32))
        stage_a(nc, io, scr, pc_all, cst)
        stage_b(nc, io, scr, pc_all, cst)
        stage_c(nc, io, scr, cst)


def kernel(**inputs):
    from concourse import bacc
    from concourse.bass_utils import run_bass_kernel_spmd

    nc = bacc.Bacc("TRN2", target_bir_lowering=False, num_devices=1)
    arrays = {f"in_{name}": a for name, a in layout(inputs).items()}
    io = {name: nc.dram_tensor(f"in_{name}", arrays[f"in_{name}"].shape, F32, kind="ExternalInput").ap()
          for name in (n[3:] for n in arrays)}
    scr = {name: nc.dram_tensor(f"scratch_{name}", shape, F32).ap() for name, shape in SCRATCH.items()}
    io["out"] = nc.dram_tensor("out", (KC, P, T), F32, kind="ExternalOutput").ap()
    program(nc, io, scr)
    r = run_bass_kernel_spmd(nc, [arrays], core_ids=[0])
    return np.ascontiguousarray(np.asarray(r.results[0]["out"]).reshape(D, T).T)[None]
```

```python
import math
from contextlib import ExitStack

import concourse.bass as bass
import numpy as np
from concourse import mybir
from concourse.bass import ds

F32 = mybir.dt.float32
F32R = mybir.dt.float32r
U8 = mybir.dt.uint8
ALU = mybir.AluOpType
ACT = mybir.ActivationFunctionType
AX = mybir.AxisListType.X

P = 128
T = 1024
D = 2048
KC = D // P
HD = 64
PAIRS = 8
HEADS = 2 * PAIRS
LORA = 64
RW = PAIRS * P
AW = PAIRS * P
KVW = 2 * HD
RWKV_COLS = 4 * RW + 2 * LORA
TILES = (RWKV_COLS + 2 * AW + 2 * KVW) // P
C = 64
BT = 128
NB = T // BT
NC_ = T // C
SUB = 16
HALF = T // 2
KH = KC // 2
POOL_STEPS = 39
DVE_STEPS = 73
DECAY = math.exp(-0.5)
RMS_EPS = 1e-5
LNX_EPS = 64e-5

PAR = ["mu_r", "mu_k", "mu_v", "mu_g", "w0", "a0", "k_k", "k_a", "r_k", "gain", "bias"]
NPAR = len(PAR)
CONSTS = {}
_at = 0
for _name, _w in (("ident", 128), ("same_head", 128), ("mean", 128), ("amask", 256), ("m16", 128),
                  ("m32", 128), ("dist", 256), ("head_of", 2)):
    CONSTS[_name] = (_at, _at + _w)
    _at += _w
CONST_COLS = _at


def constants():
    r = np.arange(128)[:, None]
    c = np.arange(128)[None, :]
    t = {}
    t["ident"] = (r == c)
    t["same_head"] = (r // HD == c // HD)
    t["mean"] = np.full((128, 128), 1.0 / D)
    s, u = r % C, np.arange(C)[None, :]
    t["amask"] = np.concatenate([s <= u, s < u, s < u, s <= u], axis=1)
    for m in (16, 32):
        t[f"m{m}"] = (r // (2 * m) == c // (2 * m)) & (r % (2 * m) >= m) & (c % (2 * m) < m)
    key = np.arange(2 * BT)[None, :]
    d = BT + r - key
    t["dist"] = np.where((d >= 0) & (d < BT), d, 1e33)
    t["head_of"] = (r // HD == np.arange(2)[None, :])
    return np.concatenate([t[n].astype(np.float32) for n in CONSTS], axis=1)


def after(n, per, k):
    return n * per + k


def stage_a(nc, io, scr, pc_all, consts):
    with ExitStack() as ctx:
        def sb(name, shape, dt=F32):
            return ctx.enter_context(nc.sbuf_tensor("a_" + name, shape, dt))

        semaphores = []

        def sem(name):
            semaphores.append(nc.alloc_semaphore(name))
            return semaphores[-1]

        x_hi = sb("x_hi", [P, KC, T], F32R)
        x_lo = sb("x_lo", [P, KC, T], F32R)
        w_raw = sb("w_raw", [P, KH * P])
        w_hi = [sb(f"w_hi{i}", [P, KH * P], F32R) for i in range(2)]
        w_lo = [sb(f"w_lo{i}", [P, KH * P], F32R) for i in range(2)]
        rms = sb("rms", [P, T])
        keep = sb("keep", [P, T], U8)
        lora = sb("lora", [P, T])
        raw = sb("raw", [P, T + 1])
        r = sb("r", [P, T])
        k = sb("k", [P, T])
        v = sb("v", [P, T])
        g = sb("g", [P, T])
        s1 = sb("s1", [P, T])
        s2 = sb("s2", [P, T])
        a = sb("a", [P, T])
        b = sb("b", [P, T])
        decay = sb("decay", [P, NC_, C + 1])
        grow = sb("grow", [P, T])
        par = sb("par", [P, PAIRS, NPAR])
        par1 = sb("par1", [P, KC + 1])
        lora_up = sb("lora_up", [P, P])
        inv2 = sb("inv2", [P, 2 * NB])
        eps = sb("eps", [P, 1])
        cst = consts
        x_in = [r, k, v, g]
        sq = [s1, s2]
        acc = a
        psum = ctx.enter_context(nc.psum_tensor("psum_a", [P, 8, HALF], F32))

        def banks(i):
            return psum[:, i:i + 2, :].rearrange("p b t -> p (b t)")

        par_landed = sem("a_par_landed")
        x_landed = [sem(f"a_x_landed{i}") for i in range(4)]
        x_squared = sem("a_x_squared")
        x_high = sem("a_x_high")
        x_ready = sem("a_x_ready")
        x_summed = sem("a_x_summed")
        ms_done = sem("a_ms_done")
        rms_root = sem("a_rms_root")
        w_landed = sem("a_w_landed")
        w_high = [sem(f"a_w_high{i}") for i in range(2)]
        w_ready = [sem(f"a_w_ready{i}") for i in range(2)]
        w_used = [sem(f"a_w_used{i}") for i in range(2)]
        tile_done = sem("a_tile_done")
        tile_read = sem("a_tile_read")
        up_landed = sem("a_up_landed")
        lora_ready = sem("a_lora_ready")
        lora_done = sem("a_lora_done")
        norm_done = sem("a_norm_done")
        sigma_w = sem("a_sigma_w")
        sigma_a = sem("a_sigma_a")
        summed = sem("a_summed")
        exps = sem("a_exps")
        squares = sem("a_squares")
        k_ready = sem("a_k_ready")
        inv_ready = sem("a_inv_ready")
        inv_spread = sem("a_inv_spread")
        rkr_ready = sem("a_rkr_ready")
        bonus_done = sem("a_bonus_done")
        g_ready = sem("a_g_ready")
        gate_sig = sem("a_gate_sig")
        ga_ready = sem("a_ga_ready")
        ga_sig = sem("a_ga_sig")
        kk_read = sem("a_kk_read")
        bonus_read = sem("a_bonus_read")
        names = ["R", "KK", "K", "B", "V", "GS", "BS", "Q", "SA"]
        made = {x: sem(f"a_made_{x}") for x in names}
        stored = {x: sem(f"a_stored_{x}") for x in names}
        stores_begun = sem("a_stores_begun")
        kv_made = sem("a_kv_made")
        kv_stored = sem("a_kv_stored")
        steps = sem("a_dve_steps")

        PRO = 3
        TP = 6

        with nc.Block() as block:
            @block.sync
            def _(sp):
                def load_half(t, half, first):
                    if not first:
                        if half == 0:
                            sp.wait_ge(w_ready[1], t)
                        else:
                            sp.wait_ge(w_ready[0], t + 1)
                    elif half == 1:
                        sp.wait_ge(w_ready[0], 1)
                    sp.dma_start(w_raw[:], io["w_in"][ds(t, 1), half].rearrange("a p n -> (a p) n")
                                 ).then_inc(w_landed, 16)

                sp.dma_start(par1[:], io["par1"]).then_inc(par_landed, 16)
                sp.dma_start(cst[:], io["consts"]).then_inc(par_landed, 16)
                sp.dma_start(par[:], io["par"]).then_inc(par_landed, 16)
                load_half(0, 0, True)
                for c in range(KC):
                    if c == 2:
                        load_half(0, 1, True)
                    if c >= 4:
                        sp.wait_ge(x_ready, c - 3)
                        sp.wait_ge(x_squared, c - 3)
                    sp.dma_start(x_in[c % 4][:], io["x_t"][c]).then_inc(x_landed[c % 4], 16)
                with sp.Fori(1, TILES) as t:
                    load_half(t, 0, False)
                    load_half(t, 1, False)

            @block.gpsimd
            def _(pool):
                def store(n, name, src):
                    pool.wait_ge(made[name], after(n, 1, 1))
                    pool.sem_inc(stores_begun, 1)
                    if name in ("K", "B", "R", "KK"):
                        dst = scr["KB" if name in ("K", "B") else "QR"]
                        dst = dst[:, :, ds(n, 1)].rearrange("b p j s t -> p (b j) s t")
                        src = src[:].rearrange("p (b s t) -> p b s t", b=NB, s=2)
                        dst = dst[:, :, 0:4:3, :] if name in ("K", "R") else dst[:, :, 1:3, :]
                    else:
                        dst = scr[name][:, :, ds(n, 1)].rearrange("b p j t -> p (b j) t")
                        src = src.rearrange("p (b t) -> p b t", b=NB)
                    if name in ("K", "R"):
                        for c in range(2):
                            pool.dma_start(dst[:, :, c], src[:, :, c]).then_inc(stored[name], 16)
                    else:
                        if name in ("KK", "B"):
                            dst = dst.rearrange("p b s t -> p b (s t)")
                            src = src.rearrange("p b s t -> p b (s t)")
                        pool.dma_start(dst, src).then_inc(stored[name], 16)

                def pair(n, first):
                    if not first:
                        pool.wait_ge(lora_done, after(n, 2, 0))
                    pool.sem_inc(stores_begun, 1)
                    pool.dma_start(lora_up[:], io["lora_up"][ds(n, 1)].rearrange("a p n -> (a p) n")
                                   ).then_inc(up_landed, 16)
                    if not first:
                        store(n - 1, "SA", raw[:, 1:T + 1])
                    store(n, "R", r)
                    store(n, "B", b)
                    store(n, "K", a)
                    store(n, "V", v[:])
                    store(n, "Q", raw[:, 1:T + 1])
                    store(n, "KK", k)
                    store(n, "BS", s2[:])
                    store(n, "GS", g[:])

                for i in range(2):
                    pool.wait_ge(kv_made, i + 1)
                    pool.dma_start(scr["KVA"][i], raw[:, 1:T + 1]).then_inc(kv_stored, 16)
                pair(0, True)
                with pool.Fori(1, PAIRS) as n:
                    pair(n, False)
                store(PAIRS - 1, "SA", raw[:, 1:T + 1])
                for name in names:
                    pool.wait_ge(stored[name], 16 * PAIRS * (2 if name in ("K", "R") else 1))
                pool.wait_ge(kv_stored, 32)

            @block.scalar
            def _(act):
                def high_half(t, half, first=False):
                    act.wait_ge(w_landed, 32 * t + 16 * (half + 1))
                    if not first:
                        act.wait_ge(w_used[half], t)
                    nc.scalar.activation(w_hi[half][:], w_raw[:], ACT.Copy).then_inc(w_high[half], 1)

                def p(n, name):
                    return par[:, ds(n, 1), PAR.index(name)]

                act.wait_ge(par_landed, 48)
                high_half(0, 0, True)
                for c in range(KC):
                    if c == 2:
                        high_half(0, 1, True)
                    act.wait_ge(x_landed[c % 4], 16 * (c // 4 + 1))
                    if c >= 2:
                        act.wait_ge(x_summed, c - 1)
                    nc.scalar.activation(sq[c % 2][:], x_in[c % 4][:], ACT.Square).then_inc(x_squared, 1)
                    nc.scalar.activation(x_hi[:, c], x_in[c % 4][:], ACT.Copy,
                                         scale=par1[:, c:c + 1]).then_inc(x_high, 1)
                high_half(1, 0)
                high_half(1, 1)
                act.wait_ge(ms_done, 1)
                nc.scalar.activation(rms[:], banks(4), ACT.Sqrt, bias=eps[:, 0:1]).then_inc(rms_root, 1)
                act.wait_ge(lora_ready, 1)
                nc.scalar.activation(lora[0:LORA], lora[0:LORA], ACT.Tanh).then_inc(lora_ready, 1)
                high_half(2, 0)
                high_half(2, 1)

                def pair(n, first):
                    t = TP * n + PRO
                    high_half(t, 0)
                    high_half(t, 1)
                    if not first:
                        act.wait_ge(ga_ready, after(n, 1, 0))
                        nc.scalar.activation(s1[:], raw[:, 1:T + 1], ACT.Sigmoid).then_inc(ga_sig, 1)
                        act.wait_ge(made["SA"], after(n, 1, 0))
                    act.wait_ge(lora_done, after(n, 2, 1))
                    nc.scalar.activation(s1[:], banks(4), ACT.Sigmoid, bias=p(n, "w0")).then_inc(sigma_w, 1)
                    act.wait_ge(lora_done, after(n, 2, 2))
                    if not first:
                        act.wait_ge(stored["K"], after(n, 32, 0))
                    nc.scalar.activation(a[:], banks(6), ACT.Sigmoid, bias=p(n, "a0")).then_inc(sigma_a, 1)
                    high_half(t + 1, 0)
                    act.wait_ge(summed, after(n, 1, 1))
                    nc.scalar.activation(decay[:, :, 1:C + 1], s2[:].rearrange("p (c t) -> p c t", t=C),
                                         ACT.Exp, scale=-DECAY).then_inc(exps, 1)
                    nc.scalar.activation(grow[:], s2[:], ACT.Exp, scale=DECAY).then_inc(exps, 1)
                    high_half(t + 1, 1)
                    high_half(t + 2, 0)
                    high_half(t + 2, 1)
                    act.wait_ge(k_ready, after(n, 1, 1))
                    act.wait_ge(exps, after(n, 2, 2))
                    nc.scalar.activation(s2[:], k[:], ACT.Square, scale=p(n, "k_k")).then_inc(squares, 1)
                    for i in (3, 4):
                        high_half(t + i, 0)
                        high_half(t + i, 1)
                    act.wait_ge(g_ready, after(n, 1, 1))
                    act.wait_ge(norm_done, after(n, 2, 1))
                    nc.scalar.activation(s2[:], g[:], ACT.Sigmoid).then_inc(gate_sig, 1)
                    high_half(t + 5, 0)
                    high_half(t + 5, 1)

                pair(0, True)
                with act.Fori(1, PAIRS) as n:
                    pair(n, False)
                act.wait_ge(ga_ready, PAIRS)
                nc.scalar.activation(s1[:], raw[:, 1:T + 1], ACT.Sigmoid).then_inc(ga_sig, 1)

            @block.vector
            def _(dve):
                count = [0, 0]

                def then(ins):
                    ins.then_inc(steps, 1)
                    count[1] += 1
                    dve.wait_ge(steps, count[0] + count[1])

                def low_half(t, half):
                    dve.wait_ge(w_high[half], t + 1)
                    nc.vector.tensor_tensor(w_lo[half][:], w_raw[:], w_hi[half][:].bitcast(F32),
                                            ALU.subtract).then_inc(w_ready[half], 1)

                def p(n, name):
                    return par[:, ds(n, 1), PAR.index(name)]

                def read_tile(t, dst, scale=None):
                    dve.wait_ge(tile_done, t + 1)
                    src = banks(2 * _parity(t))
                    if scale is None:
                        ins = nc.vector.tensor_tensor(dst, src, rms[:], ALU.mult)
                    else:
                        ins = nc.vector.scalar_tensor_tensor(dst, src, scale, rms[:], ALU.mult, ALU.mult)
                    then(ins)
                    dve.sem_inc(tile_read, 1)

                def _parity(t):
                    return parity[0]

                parity = [0]

                def tile(t, par_, dst, scale=None):
                    parity[0] = par_
                    read_tile(t, dst, scale)

                def shift(dst, mu):
                    then(nc.vector.tensor_tensor(dst, raw[:, 0:T], raw[:, 1:T + 1], ALU.subtract))
                    return nc.vector.scalar_tensor_tensor(dst, dst, mu, raw[:, 1:T + 1],
                                                          ALU.mult, ALU.add)

                then(nc.vector.memset(keep[:], 1))
                then(nc.vector.memset(keep[:].rearrange("p (c t) -> p c t", t=C)[:, :, 0:1], 0))
                then(nc.vector.memset(raw[:, 0:1], 0.0))
                then(nc.vector.memset(decay[:, :, 0:1], 1.0))
                then(nc.vector.memset(eps[:], RMS_EPS))
                low_half(0, 0)
                dve.wait_ge(par_landed, 48)
                for c in range(KC):
                    if c == 2:
                        low_half(0, 1)
                    dve.wait_ge(x_high, c + 1)
                    nc.vector.scalar_tensor_tensor(x_lo[:, c], x_in[c % 4][:], par1[:, c:c + 1],
                                                   x_hi[:, c].bitcast(F32), ALU.mult, ALU.subtract
                                                   ).then_inc(x_ready, 1)
                    dve.wait_ge(x_squared, c + 1)
                    if c == 0:
                        ins = nc.vector.tensor_copy(acc[:], sq[0][:])
                    else:
                        dve.wait_ge(x_summed, c)
                        ins = nc.vector.tensor_tensor(acc[:], acc[:], sq[c % 2][:], ALU.add)
                    ins.then_inc(x_summed, 1)
                low_half(1, 0)
                low_half(1, 1)
                dve.wait_ge(rms_root, 1)
                then(nc.vector.reciprocal(rms[:], rms[:]))
                tile(0, 0, raw[:, 1:T + 1])
                shift(lora[:], par1[:, KC:KC + 1]).then_inc(lora_ready, 1)
                low_half(2, 0)
                low_half(2, 1)
                dve.wait_ge(lora_ready, 1)
                tile(1, 1, raw[:, 1:T + 1])
                dve.sem_inc(kv_made, 1)

                def pair(n, first):
                    t = TP * n + PRO
                    low_half(t, 0)
                    low_half(t, 1)
                    if first:
                        dve.wait_ge(kv_stored, 16)
                        tile(t - 1, 0, raw[:, 1:T + 1])
                        dve.sem_inc(kv_made, 1)
                        dve.wait_ge(kv_stored, 32)
                    else:
                        dve.wait_ge(stored["Q"], after(n, 16, 0))
                        tile(t - 1, 0, raw[:, 1:T + 1])
                        dve.wait_ge(stored["BS"], after(n, 16, 0))
                        dve.sem_inc(ga_ready, 1)
                        dve.wait_ge(ga_sig, after(n, 1, 0))
                        then(nc.vector.tensor_tensor(raw[:, 1:T + 1], raw[:, 1:T + 1], s1[:], ALU.mult))
                        dve.sem_inc(made["SA"], 1)
                    dve.wait_ge(sigma_w, after(n, 1, 1))
                    if first:
                        dve.wait_ge(ms_done, 1)
                    then(nc.vector.tensor_tensor_scan(s2[:], keep[:], s1[:], 0.0, ALU.mult, ALU.add))
                    dve.sem_inc(summed, 1)
                    low_half(t + 1, 0)
                    low_half(t + 1, 1)
                    if not first:
                        dve.wait_ge(stored["SA"], after(n, 16, 0))
                        dve.wait_ge(stored["R"], after(n, 32, 0))
                    tile(t, 1, raw[:, 1:T + 1])
                    then(shift(r[:], p(n, "mu_r")))
                    low_half(t + 2, 0)
                    low_half(t + 2, 1)
                    tile(t + 1, 0, raw[:, 1:T + 1])
                    if not first:
                        dve.wait_ge(stored["KK"], after(n, 16, 0))
                        dve.wait_ge(stored["B"], after(n, 16, 0))
                    then(shift(k[:], p(n, "mu_k")))
                    dve.sem_inc(k_ready, 1)
                    dve.wait_ge(exps, after(n, 2, 2))
                    nc.vector.tensor_copy(pc_all[:, ds(n, 1)].rearrange("p a c -> p (a c)"),
                                          decay[:, :, C])
                    dve.wait_ge(sigma_a, after(n, 1, 1))
                    then(nc.vector.scalar_tensor_tensor(b[:], k[:], p(n, "k_k"), a[:], ALU.mult, ALU.mult))
                    then(nc.vector.tensor_tensor(b[:], b[:], grow[:], ALU.mult))
                    dve.sem_inc(made["B"], 1)
                    then(nc.vector.tensor_scalar(a[:], a[:], 1.0, p(n, "k_a"), ALU.subtract, ALU.mult))
                    then(nc.vector.scalar_tensor_tensor(a[:], a[:], 1.0, k[:], ALU.add, ALU.mult))
                    then(nc.vector.scalar_tensor_tensor(s1[:], r[:], p(n, "r_k"), a[:], ALU.mult, ALU.mult))
                    dve.sem_inc(rkr_ready, 1)
                    low_half(t + 3, 0)
                    then(nc.vector.tensor_tensor(a[:], a[:], grow[:], ALU.mult))
                    dve.sem_inc(made["K"], 1)
                    then(nc.vector.tensor_tensor(r[:].rearrange("p (c t) -> p c t", t=C),
                                                 r[:].rearrange("p (c t) -> p c t", t=C),
                                                 decay[:, :, 1:C + 1], ALU.mult))
                    dve.sem_inc(made["R"], 1)
                    low_half(t + 3, 1)
                    tile(t + 2, 1, raw[:, 1:T + 1])
                    if not first:
                        dve.wait_ge(stored["V"], after(n, 16, 0))
                    then(shift(v[:], p(n, "mu_v")))
                    dve.sem_inc(made["V"], 1)
                    dve.wait_ge(norm_done, after(n, 2, 1))
                    then(nc.vector.tensor_scalar(inv2[:], psum[:, 4, 0:2 * NB], 1e-24, None, ALU.max))
                    then(nc.vector.reciprocal(inv2[:], inv2[:]))
                    spread = grow[:].rearrange("p (b d) -> p b d", d=HD)
                    then(nc.vector.tensor_copy(spread, inv2[:].unsqueeze(2).broadcast_to([P, 2 * NB, HD])))
                    dve.sem_inc(inv_ready, 1)
                    low_half(t + 4, 0)
                    low_half(t + 4, 1)
                    tile(t + 3, 0, raw[:, 1:T + 1])
                    if not first:
                        dve.wait_ge(stored["GS"], after(n, 16, 0))
                    then(shift(g[:], p(n, "mu_g")))
                    dve.sem_inc(g_ready, 1)
                    low_half(t + 5, 0)
                    dve.wait_ge(norm_done, after(n, 2, 2))
                    then(nc.vector.scalar_tensor_tensor(k[:], k[:], p(n, "k_k"), banks(4),
                                                        ALU.mult, ALU.mult))
                    dve.sem_inc(kk_read, 1)
                    then(nc.vector.tensor_tensor(k[:].rearrange("p (c t) -> p c t", t=C),
                                                 k[:].rearrange("p (c t) -> p c t", t=C),
                                                 decay[:, :, 0:C], ALU.mult))
                    dve.sem_inc(made["KK"], 1)
                    dve.wait_ge(gate_sig, after(n, 1, 1))
                    then(nc.vector.tensor_tensor(g[:], g[:], s2[:], ALU.mult))
                    dve.wait_ge(bonus_done, after(n, 1, 1))
                    then(nc.vector.tensor_tensor(s2[:], v[:], banks(6), ALU.mult))
                    dve.sem_inc(bonus_read, 1)
                    then(nc.vector.scalar_tensor_tensor(s2[:], s2[:], p(n, "bias"), g[:], ALU.add, ALU.mult))
                    dve.sem_inc(made["BS"], 1)
                    then(nc.vector.tensor_scalar(g[:], g[:], p(n, "gain"), None, ALU.mult))
                    dve.sem_inc(made["GS"], 1)
                    low_half(t + 5, 1)
                    tile(t + 4, 1, raw[:, 1:T + 1], scale=HD ** -0.5)
                    dve.sem_inc(made["Q"], 1)

                pair_start = count[1]
                pair(0, True)
                count[0], per = count[1], None
                per = count[1] - pair_start + 1
                base = count[1]
                with dve.Fori(1, PAIRS) as n:
                    count[0], count[1] = base + (n - 1) * per, 0
                    pair(n, False)
                    assert count[1] == per, (count, per)
                count[0], count[1] = base + (PAIRS - 1) * per, 0
                dve.wait_ge(stored["Q"], 16 * PAIRS)
                tile(TILES - 1, 0, raw[:, 1:T + 1])
                dve.sem_inc(ga_ready, 1)
                dve.wait_ge(ga_sig, PAIRS)
                then(nc.vector.tensor_tensor(raw[:, 1:T + 1], raw[:, 1:T + 1], s1[:], ALU.mult))
                dve.sem_inc(made["SA"], 1)

            @block.tensor
            def _(pe):
                def project(t, parity, pace=False, reuse=True):
                    if reuse:
                        pe.wait_ge(tile_read, t - 1)
                    for half in range(2):
                        pe.wait_ge(w_ready[half], t + 1)
                        for kk in range(KH):
                            c = half * KH + kk
                            if pace:
                                pe.wait_ge(x_ready, c + 1)
                            cols = slice(kk * P, (kk + 1) * P)
                            for wt, xt in ((w_hi, x_hi), (w_hi, x_lo), (w_lo, x_hi)):
                                for h in range(2):
                                    mm = nc.tensor.matmul(
                                        psum[:, 2 * parity + h], wt[half][:, cols],
                                        xt[:, c, h * HALF:(h + 1) * HALF],
                                        start=(c == 0 and wt is w_hi and xt is x_hi),
                                        stop=(c == KC - 1 and wt is w_lo))
                        mm.then_inc(w_used[half], 1)
                    pe.wait_ge(w_used[1], t + 1)
                    pe.sem_inc(tile_done, 1)

                def const(name):
                    return cst[:, slice(*CONSTS[name])]

                project(0, 0, pace=True, reuse=False)
                pe.wait_ge(x_summed, KC)
                for h in range(2):
                    mm = nc.tensor.matmul(psum[:, 4 + h], const("mean"), acc[:, h * HALF:(h + 1) * HALF],
                                          start=True, stop=True)
                mm.then_inc(ms_done, 1)
                project(1, 1, reuse=False)
                project(2, 0)

                def pair(n, first):
                    t = TP * n + PRO
                    pe.wait_ge(up_landed, after(n, 16, 16))
                    if first:
                        pe.wait_ge(lora_ready, 2)
                        pe.wait_ge(rms_root, 1)
                    else:
                        pe.wait_ge(kk_read, after(n, 1, 0))
                        pe.wait_ge(bonus_read, after(n, 1, 0))
                    for i in range(2):
                        rows = slice(i * LORA, (i + 1) * LORA)
                        for h in range(2):
                            mm = nc.tensor.matmul(psum[:, 4 + 2 * i + h], lora_up[rows, :],
                                                  lora[rows, h * HALF:(h + 1) * HALF],
                                                  start=True, stop=True)
                        mm.then_inc(lora_done, 1)
                    project(t, 1)
                    project(t + 1, 0)
                    project(t + 2, 1)
                    pe.wait_ge(squares, after(n, 1, 1))
                    pe.wait_ge(sigma_w, after(n, 1, 1))
                    for b_ in range(NB):
                        mm = nc.tensor.matmul(psum[:, 4, 2 * b_:2 * b_ + 2], s2[:, b_ * P:(b_ + 1) * P],
                                              const("head_of"), start=True, stop=True)
                    mm.then_inc(norm_done, 1)
                    project(t + 3, 0)
                    pe.wait_ge(inv_ready, after(n, 1, 1))
                    for b_ in range(NB):
                        mm = nc.tensor.matmul(banks(4)[:, b_ * P:(b_ + 1) * P],
                                              grow[:, b_ * P:(b_ + 1) * P], const("ident"),
                                              start=True, stop=True)
                    mm.then_inc(norm_done, 1)
                    pe.wait_ge(rkr_ready, after(n, 1, 1))
                    pe.wait_ge(sigma_a, after(n, 1, 1))
                    for h in range(2):
                        mm = nc.tensor.matmul(psum[:, 6 + h], const("same_head"),
                                              s1[:, h * HALF:(h + 1) * HALF], start=True, stop=True)
                    mm.then_inc(bonus_done, 1)
                    project(t + 4, 1)
                    project(t + 5, 0)

                pair(0, True)
                with pe.Fori(1, PAIRS) as n:
                    pair(n, False)
        return semaphores


def stage_b(nc, io, scr, pc_all, cst, used=()):
    with ExitStack() as ctx:
        def sb(name, shape, dt=F32):
            return ctx.enter_context(nc.sbuf_tensor("b_" + name, shape, dt))

        def sem(name):
            return ctx.enter_context(nc.semaphore("b_" + name))

        kb = sb("kb", [P, PAIRS, 4 * C])
        qr = sb("qr", [P, PAIRS, 4 * C])
        qr_s = sb("qr_s", [P, PAIRS, 4 * C])
        vt = sb("vt", [P, PAIRS, BT])
        gs = sb("gs", [P, PAIRS, BT])
        bs = sb("bs", [P, PAIRS, BT])
        q = sb("q", [P, PAIRS, BT])
        sa = sb("sa", [P, PAIRS, BT])
        kw = sb("kw", [P, 2, 2 * BT])
        vw = sb("vw", [P, 2 * BT])
        va = sb("va", [P, 2, P])
        am2 = [sb(f"am{i}", [P, HEADS, 4 * C]) for i in range(2)]
        kbt = sb("kbt", [P, 2, PAIRS, P])
        uv = sb("uv", [P, 2, HEADS, HD])
        x16 = sb("x16", [P, HEADS, 2, P])
        x32 = sb("x32", [P, HEADS, P])
        xt = sb("xt", [P, HEADS, P])
        ym = sb("ym", [P, HEADS, P])
        sub_l = sb("sub_l", [P, SUB, SUB])
        sub_x = sb("sub_x", [P, 2, SUB, SUB])
        sub_t = sb("sub_t", [P, SUB * SUB])
        sub_ident = sb("sub_ident", [P, SUB, SUB])
        state = sb("state", [P, PAIRS, 2, HD])
        state_d = sb("state_d", [P, PAIRS, HD])
        fresh = sb("fresh", [P, PAIRS, HD])
        zs = sb("zs", [P, HEADS, HD])
        y = sb("y", [P, HEADS, HD])
        ysq = sb("ysq", [P, HEADS, HD])
        stat = sb("stat", [P, 2, HEADS])
        mix = sb("mix", [P, PAIRS, P])
        mix_a = sb("mix_a", [P, PAIRS, P])
        score = [sb(f"score{i}", [P, 4, 2 * BT]) for i in range(2)]
        pt = sb("pt", [P, 2, 4 * P])
        o = sb("o", [P, HEADS, HD])
        sinks = sb("sinks", [P, HEADS])
        neg_sinks = sb("neg_sinks", [P, HEADS])
        top = sb("top", [P, 4, HEADS])
        part = sb("part", [P, HEADS])
        eps = sb("eps", [P, 1])
        psum = ctx.enter_context(nc.psum_tensor("psum_b", [P, 8, HALF], F32))
        SCORE, PRODUCT, TURNED_P, U, F, ZY = (0, 1), (2, 3), (2, 3), 4, 5, (6, 7)
        OUT = ((U, 0), (F, 0), (U, 0), (F, 0))

        loads = ("kb", "qr", "qr_s", "vt", "gs", "bs", "q", "sa", "kw", "vw")
        landed = {x: sem(f"landed_{x}") for x in loads}
        sinks_landed = sem("sinks_landed")
        l_out, l_in, x_out, x_in = sem("l_out"), sem("l_in"), sem("x_out"), sem("x_in")
        sub_done = sem("sub_done")
        pool_steps = sem("pool_steps")
        u_zero = sem("u_zero")
        decayed = sem("decayed")
        a_full, a_read = sem("a_full"), sem("a_read")
        t_full, t_read = sem("t_full"), sem("t_read")
        va_full, va_read = sem("va_full"), sem("va_read")
        s_full, s_read = sem("s_full"), sem("s_read")
        p_ready = sem("p_ready")
        pt_full, pt_read = sem("pt_full"), sem("pt_read")
        o_full, o_read = sem("o_full"), sem("o_read")
        ot_full, ot_read = sem("ot_full"), sem("ot_read")
        lev_full, lev_read = sem("lev_full"), sem("lev_read")
        z_full, z_read = sem("z_full"), sem("z_read")
        u_full, u_read = sem("u_full"), sem("u_read")
        f_full, state_read, state_new = sem("f_full"), sem("state_read"), sem("state_new")
        y_full, y_read = sem("y_full"), sem("y_read")
        y_mean, y_centred, y_squared, y_var, y_root, y_rstd, y_norm = (
            sem("y_mean"), sem("y_centred"), sem("y_squared"), sem("y_var"), sem("y_root"),
            sem("y_rstd"), sem("y_norm"))
        yt_full, yt_read = sem("yt_full"), sem("yt_read")
        negmax = sem("negmax")
        mix_ready, mix_stored = sem("mix_ready"), sem("mix_stored")
        mixa_ready, mixa_stored = sem("mixa_ready"), sem("mixa_stored")
        steps = sem("dve_steps")
        inited = sem("inited")
        apart = sem("apart")

        def const(name):
            return cst[:, slice(*CONSTS[name])]

        def many(ap, n):
            return ap.unsqueeze(1).broadcast_to([P, n, ap.shape[1]])

        def sides(c):
            u = C if c == 0 else 0
            return slice(u, u + C), slice(C - u, 2 * C - u)

        def quad_head(i, hh):
            return 4 * i + 2 * (hh % 2) + hh // 2

        KK = {0: 2 * C, 1: C}
        R = {0: 0, 1: 3 * C}
        GROUPS = 4

        def inversion_order():
            order = [("Y", 0), ("Y", 1)]
            for g in range(GROUPS):
                order += [("D", g), ("DT", g)]
                if g + 2 < GROUPS:
                    order.append(("Y", g + 2))
            order += [("Y2", 0), ("Y2", 1)]
            for g in range(GROUPS):
                order.append(("DT2", g))
                if g + 2 < GROUPS:
                    order.append(("Y2", g + 2))
            return order

        ORDER = inversion_order()
        LEV = len(ORDER)
        LEV_BANK = {"Y": (0, 1), "D": (2, 3), "DT": (6, 7), "Y2": (0, 1), "DT2": (2, 3)}

        def lev_bank(i):
            kind, g = ORDER[i]
            return LEV_BANK[kind][g % 2]

        def lev_before(i):
            before = [j for j in range(i) if lev_bank(j) == lev_bank(i)]
            return before[-1] if before else None

        with nc.Block() as block:
            def rounds(engine, round_, count=None):
                round_(0, 0, True, False)
                base = count[0] + count[1] if count else 0
                with engine.Fori(0, NB // 2 - 1) as m:
                    if count:
                        count[0], count[1] = base + m * (2 * count[2]), 0
                    round_(2 * m + 1, 1, False, False)
                    round_(2 * m + 2, 0, False, False)
                    if count:
                        assert count[1] == 2 * count[2], count
                if count:
                    count[0], count[1] = base + (NB - 2) * count[2], 0
                round_(NB - 1, 1, False, True)

            @block.sync
            def _(sp):
                def load(n, name, dst, src):
                    sp.dma_start(dst, src).then_inc(landed[name], 16)

                def need(semaphore, value):
                    sp.wait_ge(semaphore, value)
                    sp.sem_inc(apart, 1)

                def whole(name, n):
                    return scr[name][ds(n, 1)].rearrange("a p j t -> (a p) j t")

                def whole4(name, n):
                    return scr[name][ds(n, 1)].rearrange("a p j s t -> (a p) j (s t)")

                def load_recurrence(n):
                    load(n, "kb", kb[:], whole4("KB", n))
                    load(n, "qr", qr[:], whole4("QR", n))
                    load(n, "vt", vt[:], whole("V", n))

                def load_attention(n, first=False):
                    load(n, "q", q[:], whole("Q", n))
                    if first:
                        window, cols = slice(0, BT), slice(BT, 2 * BT)
                    else:
                        window, cols = ds((n - 1) * BT, 2 * BT), slice(0, 2 * BT)
                    for i in range(2):
                        load(n, "kw", kw[i * HD:(i + 1) * HD, :, cols],
                             scr["KVA"][0, :, window].rearrange("(h d) t -> d h t", h=2))
                    load(n, "vw", vw[:, cols], scr["KVA"][1, :, window])

                def blocks_out(n, parity, first=False):
                    need(a_read, after(n, 8, 8))
                    if not first:
                        need(l_in, after(n, 16, 0))
                    for i in range(P // SUB):
                        rows = slice(i * SUB, (i + 1) * SUB)
                        sp.dma_start(scr["L"][i].rearrange("h s t -> s h t"),
                                     am2[parity][rows, :, C + i * SUB:C + (i + 1) * SUB]).then_inc(l_out, 16)
                    need(l_out, after(n, 8 * 16, 8 * 16))
                    if not first:
                        need(sub_done, after(n, 1, 0))
                    sp.dma_start(sub_l[:], scr["L"].rearrange("i h s t -> (i h) s t")).then_inc(l_in, 16)

                def blocks_back(n, first=False):
                    need(sub_done, after(n, 1, 1))
                    sp.dma_start(scr["X"].rearrange("i h a s t -> (i h) a s t"), sub_x[:]).then_inc(x_out, 16)
                    need(x_out, after(n, 16, 16))
                    if first:
                        need(inited, 1)
                    else:
                        need(lev_full, after(n, LEV, 0))
                        need(lev_read, after(n, LEV, 0))
                    for i in range(P // SUB):
                        rows = slice(i * SUB, (i + 1) * SUB)
                        sp.dma_start(x16[rows, :, :, i * SUB:(i + 1) * SUB].rearrange("s h a t -> s (h a) t"),
                                     scr["X"][i].rearrange("h a s t -> s (h a) t")).then_inc(x_in, 16)

                def round_(n, parity, first, last):
                    if not last:
                        need(t_full, after(n, 8, 8))
                        load_recurrence(n + 1)
                    if not first:
                        need(mix_ready, after(n, 1, 0))
                    load(n, "gs", gs[:], whole("GS", n))
                    load(n, "bs", bs[:], whole("BS", n))
                    if not last:
                        blocks_out(n + 1, 1 - parity)
                        need(z_full, after(n, 4, 4))
                        load(n + 1, "qr_s", qr_s[:], whole4("QR", n + 1))
                        blocks_back(n + 1)
                        need(s_full, after(n, 8, 8))
                        need(va_full, after(n, 1, 1))
                        load_attention(n + 1)
                        need(ot_read, after(n, 2, 2))
                        load(n + 1, "sa", sa[:], whole("SA", n + 1))

                load_recurrence(0)
                sp.dma_start(sinks[:], io["sinks"]).then_inc(sinks_landed, 16)
                load_attention(0, True)
                load(0, "qr_s", qr_s[:], whole4("QR", 0))
                load(0, "sa", sa[:], whole("SA", 0))
                blocks_out(0, 0, True)
                blocks_back(0, True)
                rounds(sp, round_)

            @block.gpsimd
            def _(pool):
                count = [0, 0, POOL_STEPS]

                def then(ins):
                    ins.then_inc(pool_steps, 1)
                    count[1] += 1
                    pool.wait_ge(pool_steps, count[0] + count[1])

                def inverses(n, first=False):
                    pool.wait_ge(l_in, after(n, 16, 16))
                    if not first:
                        pool.wait_ge(x_out, after(n, 16, 0))
                    pool.sem_inc(apart, 1)
                    then(nc.gpsimd.tensor_copy(sub_x[:, 0], sub_ident[:]))
                    for s in range(SUB - 1):
                        below, width = SUB - 1 - s, s + 1
                        left = sub_l[:, s, s + 1:].unsqueeze(2).broadcast_to([P, below, width])
                        right = sub_x[:, 0, s, 0:width].unsqueeze(1).broadcast_to([P, below, width])
                        t = sub_t[:, 0:below * width].rearrange("p (r c) -> p r c", c=width)
                        then(nc.gpsimd.tensor_tensor(t, left, right, ALU.mult))
                        rows = sub_x[:, 0, s + 1:, 0:width]
                        then(nc.gpsimd.tensor_tensor(rows, rows, t, ALU.subtract))
                    pool.sem_inc(apart, 1)
                    then(nc.gpsimd.tensor_copy(sub_x[:, 1], sub_x[:, 0].rearrange("p s t -> p t s")))
                    pool.sem_inc(sub_done, 1)

                def head_norm(n):
                    spread = [P, HEADS, HD]
                    pool.wait_ge(y_mean, after(n, 1, 0))
                    then(nc.gpsimd.tensor_tensor(y[:], y[:], stat[:, 0].unsqueeze(2).broadcast_to(spread), ALU.add))
                    pool.sem_inc(y_centred, 1)
                    pool.wait_ge(y_rstd, after(n, 1, 0))
                    then(nc.gpsimd.tensor_tensor(y[:], y[:], stat[:, 1].unsqueeze(2).broadcast_to(spread), ALU.mult))
                    pool.sem_inc(y_norm, 1)

                def round_(n, parity, first, last):
                    if not first:
                        pool.wait_ge(f_full, after(n, 2, 0))
                        pool.wait_ge(y_full, after(n, 4, 0))
                        pool.sem_inc(apart, 1)
                    for c in range(2):
                        us, _ = sides(c)
                        ins = nc.gpsimd.memset(uv[us, c], 0.0)
                    then(ins)
                    pool.sem_inc(u_zero, 1)
                    for c in range(2):
                        if c == 0 and not first:
                            pool.wait_ge(state_new, after(n, 2, 0))
                        if c == 1:
                            if not first:
                                head_norm(n)
                            pool.wait_ge(state_new, after(n, 2, 1))
                        pc = pc_all[:, :, ds(2 * n + c, 1)]
                        for i in range(2):
                            half = slice(i * HD, (i + 1) * HD)
                            then(nc.gpsimd.tensor_tensor(state_d[half], state[half, :, i],
                                                         pc[half].broadcast_to([HD, PAIRS, HD]), ALU.mult))
                        pool.sem_inc(decayed, 1)
                    if not last:
                        inverses(n + 1)

                then(nc.gpsimd.memset(sub_ident[:], 0.0))
                then(nc.gpsimd.affine_select(sub_ident[:], sub_ident[:], pattern=[[1, SUB], [-1, SUB]],
                                             compare_op=ALU.not_equal, fill=1.0, base=0,
                                             channel_multiplier=0))
                then(nc.gpsimd.memset(sub_x[:], 0.0))
                then(nc.gpsimd.memset(state[:], 0.0))
                then(nc.gpsimd.memset(x16[:], 0.0))
                pool.sem_inc(inited, 1)
                inverses(0, True)
                rounds(pool, round_, count)
                head_norm(NB)
                if used:
                    nc.clear_and_free_semaphores(used)

            @block.scalar
            def _(act):
                def copy(dst, src, scale=1.0):
                    return nc.scalar.activation(dst, src, ACT.Copy, scale=scale)

                def exponentials(n, first, i):
                    lo = BT if first else 0
                    act.wait_ge(negmax, after(n, 4, i + 1))
                    for hh in range(4):
                        at = 4 * i + hh
                        s = score[i % 2][:, hh, lo:]
                        nc.scalar.activation(s, s, ACT.Exp, bias=top[:, 1, at:at + 1],
                                             accum_out=top[:, 2, at:at + 1])
                    heads = slice(4 * i, 4 * i + 4)
                    nc.scalar.activation(top[:, 3, heads], part[:, heads], ACT.Exp).then_inc(p_ready, 1)

                def turned_p(n, first, i):
                    w = 2 * P if first else 4 * P
                    for m in range(2):
                        act.wait_ge(pt_full, after(n, 8, 2 * i + m + 1))
                        copy(pt[:, m, 0:w], psum[:, TURNED_P[m], 0:w]).then_inc(pt_read, 1)

                def mix_out(n, group):
                    return scr["MIX"][ds(n, 1), :, group * PAIRS:(group + 1) * PAIRS].rearrange(
                        "b p k t -> (b p) k t")

                def turned(n, j):
                    act.wait_ge(t_full, after(n, 8, j + 1))
                    bank = psum[:, 4 + j % 2]
                    copy(kbt[:, :, j], bank[:, 0:2 * P].rearrange("p (c k) -> p c k", c=2))
                    for c in range(2):
                        _, vs = sides(c)
                        ins = copy(uv[vs, c, 2 * j:2 * j + 2].rearrange("p h d -> p (h d)"),
                                   bank[vs, 2 * P:3 * P])
                    ins.then_inc(t_read, 1)

                def negative_z(n, c):
                    us, _ = sides(c)
                    for i in range(2):
                        act.wait_ge(z_full, after(n, 4, 2 * c + i + 1))
                        z = psum[us, ZY[i]].rearrange("p (h d) -> p h d", d=HD)
                        copy(zs[us, 8 * i:8 * i + 8], z, scale=-1.0).then_inc(z_read, 1)

                def rows_out(n, c):
                    _, vs = sides(c)
                    for i in range(2):
                        act.wait_ge(y_full, after(n, 4, 2 * c + i + 1))
                        src = psum[vs, ZY[i]].rearrange("p (h d) -> p h d", d=HD)
                        copy(y[vs, 8 * i:8 * i + 8], src).then_inc(y_read, 1)

                def squares(n):
                    act.wait_ge(y_centred, after(n, 1, 0))
                    nc.scalar.activation(ysq[:], y[:], ACT.Square).then_inc(y_squared, 1)

                def roots(n):
                    act.wait_ge(y_var, after(n, 1, 0))
                    nc.scalar.activation(stat[:, 1], stat[:, 1], ACT.Sqrt, bias=eps[:, 0:1],
                                         scale=1.0 / HD).then_inc(y_root, 1)

                def round_(n, parity, first, last):
                    act.wait_ge(u_zero, after(n, 1, 1))
                    for j in range(PAIRS):
                        turned(n, j)
                        if j == 4 and not first:
                            squares(n)
                    if not first:
                        roots(n)
                    act.wait_ge(va_full, after(n, 1, 1))
                    if first:
                        copy(va[:, 1], psum[:, TURNED_P[0], P:2 * P]).then_inc(va_read, 1)
                    else:
                        copy(va[:].rearrange("p w d -> p (w d)"), psum[:, TURNED_P[0], 0:2 * P]).then_inc(va_read, 1)
                    exponentials(n, first, 0)
                    negative_z(n, 0)
                    exponentials(n, first, 1)
                    rows_out(n, 0)
                    turned_p(n, first, 0)
                    negative_z(n, 1)
                    turned_p(n, first, 1)
                    exponentials(n, first, 2)
                    turned_p(n, first, 2)
                    exponentials(n, first, 3)
                    rows_out(n, 1)
                    turned_p(n, first, 3)
                    if not first:
                        act.wait_ge(mix_ready, after(n, 1, 0))
                        act.dma_start(mix_out(n - 1, 0), mix[:]).then_inc(mix_stored, 16)
                    act.wait_ge(mixa_ready, after(n, 1, 1))
                    act.dma_start(mix_out(n, 1), mix_a[:]).then_inc(mixa_stored, 16)

                act.wait_ge(inited, 2)
                rounds(act, round_)
                squares(NB)
                roots(NB)
                act.wait_ge(mix_ready, NB)
                act.dma_start(mix_out(NB - 1, 0), mix[:]).then_inc(mix_stored, 16)
                act.wait_ge(mix_stored, 16 * (NB + 1))
                act.wait_ge(mixa_stored, 16 * NB)

            @block.vector
            def _(dve):
                count = [0, 0, DVE_STEPS]

                def then(ins):
                    ins.then_inc(steps, 1)
                    count[1] += 1
                    dve.wait_ge(steps, count[0] + count[1])

                def mean(n):
                    dve.wait_ge(y_read, after(n, 4, 0))
                    then(nc.vector.tensor_reduce(stat[:, 0], y[:], AX, ALU.add))
                    then(nc.vector.tensor_scalar(stat[:, 0], stat[:, 0], -1.0 / HD, None, ALU.mult))
                    dve.sem_inc(y_mean, 1)

                def variance(n):
                    dve.wait_ge(y_squared, after(n, 1, 0))
                    then(nc.vector.tensor_reduce(stat[:, 1], ysq[:], AX, ALU.add))
                    dve.sem_inc(y_var, 1)

                def deviation(n):
                    dve.wait_ge(y_root, after(n, 1, 0))
                    then(nc.vector.reciprocal(stat[:, 1], stat[:, 1]))
                    dve.sem_inc(y_rstd, 1)

                def gated(n):
                    dve.wait_ge(landed["gs"], after(n, 16, 0))
                    dve.wait_ge(landed["bs"], after(n, 16, 0))
                    dve.wait_ge(mix_stored, after(n, 16, 0))
                    for i in range(2):
                        dve.wait_ge(yt_full, after(n - 1, 2, i + 1))
                        js = slice(4 * i, 4 * i + 4)
                        then(nc.vector.tensor_tensor(mix[:, js], psum[:, 4 + i].rearrange("p (j t) -> p j t", t=BT),
                                                     gs[:, js], ALU.mult))
                        dve.sem_inc(yt_read, 1)
                    then(nc.vector.tensor_tensor(mix[:], mix[:], bs[:], ALU.add))
                    dve.sem_inc(mix_ready, 1)

                def softmax_scores(n, first, i):
                    lo = BT if first else 0
                    w = 2 * BT - lo
                    for par_ in range(2):
                        dve.wait_ge(s_full, after(n, 8, 2 * i + par_ + 1))
                        for jj in range(2):
                            hh = 2 * par_ + jj
                            slope = 2.0 ** (-8.0 * (quad_head(i, hh) + 1) / HEADS)
                            src = psum[:, SCORE[par_], jj * w:(jj + 1) * w]
                            ins = nc.vector.scalar_tensor_tensor(
                                score[i % 2][:, hh, lo:], const("dist")[:, lo:], -slope, src,
                                ALU.mult, ALU.add)
                    then(ins)
                    dve.sem_inc(s_read, 1)
                    heads = slice(4 * i, 4 * i + 4)
                    then(nc.vector.tensor_reduce(top[:, 0, heads], score[i % 2][:, :, lo:], AX, ALU.max))
                    then(nc.vector.scalar_tensor_tensor(top[:, 1, heads], top[:, 0, heads], -1.0,
                                                        neg_sinks[:, heads], ALU.mult, ALU.min))
                    then(nc.vector.tensor_tensor(part[:, heads], top[:, 1, heads], neg_sinks[:, heads],
                                                 ALU.subtract))
                    dve.sem_inc(negmax, 1)

                def outputs(n, i):
                    heads = slice(4 * i, 4 * i + 4)
                    dve.wait_ge(p_ready, after(n, 4, i + 1))
                    then(nc.vector.tensor_tensor(part[:, heads], top[:, 2, heads], top[:, 3, heads], ALU.add))
                    then(nc.vector.reciprocal(part[:, heads], part[:, heads]))
                    dve.wait_ge(o_full, after(n, 4, i + 1))
                    bank, at = OUT[i]
                    then(nc.vector.tensor_tensor(
                        o[:, heads].rearrange("p (b a) d -> p a b d", a=2),
                        psum[:, bank, at:at + 4 * HD].rearrange("p (a b d) -> p a b d", a=2, b=2),
                        part[:, heads].rearrange("p (a b) -> p a b", a=2).unsqueeze(3)
                        .broadcast_to([P, 2, 2, HD]), ALU.mult))
                    dve.sem_inc(o_read, 1)

                def masked(n, parity, g):
                    for par_ in range(2):
                        dve.wait_ge(a_full, after(n, 8, 2 * g + par_ + 1))
                        then(nc.vector.tensor_tensor(
                            am2[parity][:, 4 * g + par_:4 * g + 4:2],
                            psum[:, PRODUCT[par_]].rearrange("p (h t) -> p h t", h=2),
                            many(const("amask"), 2), ALU.mult))
                        dve.sem_inc(a_read, 1)

                def level(n, i):
                    kind, g = ORDER[i]
                    hs = slice(4 * g, 4 * g + 4)
                    dve.wait_ge(lev_full, after(n, LEV, i + 1))
                    src = psum[:, lev_bank(i)].rearrange("p (h t) -> p h t", t=P)
                    if kind in ("Y", "Y2"):
                        mask = const("m16" if kind == "Y" else "m32")
                        ins = nc.vector.tensor_tensor(ym[:, hs], src, many(mask, 4), ALU.mult)
                    elif kind == "D":
                        ins = nc.vector.tensor_tensor(x32[:, hs], x16[:, hs, 0], src, ALU.subtract)
                    elif kind == "DT":
                        ins = nc.vector.tensor_tensor(xt[:, hs], x16[:, hs, 1], src, ALU.subtract)
                    else:
                        ins = nc.vector.tensor_tensor(xt[:, hs], xt[:, hs], src, ALU.subtract)
                    then(ins)
                    dve.sem_inc(lev_read, 1)

                def u_rows(n, c):
                    us, vs = sides(c)
                    for i in range(2):
                        dve.wait_ge(u_full, after(n, 4, 2 * c + i + 1))
                        then(nc.vector.tensor_copy(uv[us, c, 8 * i:8 * i + 8].rearrange("p h d -> p (h d)"),
                                                   psum[(us, vs)[i], U]))
                        dve.sem_inc(u_read, 1)

                def new_state(n, c):
                    pc = pc_all[:, :, ds(2 * n + c, 1)]
                    dve.wait_ge(f_full, after(n, 2, c + 1))
                    then(nc.vector.tensor_tensor(fresh[:], psum[:, F].rearrange("p (j d) -> p j d", d=HD),
                                                 pc.broadcast_to([P, PAIRS, HD]), ALU.mult))
                    dve.sem_inc(state_read, 1)
                    dve.wait_ge(decayed, after(n, 2, c + 1))
                    for i in range(2):
                        half = slice(i * HD, (i + 1) * HD)
                        ins = nc.vector.tensor_tensor(state[half, :, i], state_d[half], fresh[half], ALU.add)
                    then(ins)
                    dve.sem_inc(state_new, 1)

                def round_(n, parity, first, last):
                    if not first:
                        mean(n)
                    for i in range(LEV):
                        level(n, i)
                        if not first and i == 11:
                            variance(n)
                        if not first and i == 16:
                            deviation(n)
                    softmax_scores(n, first, 0)
                    if not first:
                        gated(n)
                    if not last:
                        if not first:
                            dve.wait_ge(l_out, after(n, 8 * 16, 0))
                        masked(n + 1, 1 - parity, 0)
                        masked(n + 1, 1 - parity, 1)
                    softmax_scores(n, first, 1)
                    u_rows(n, 0)
                    if not last:
                        masked(n + 1, 1 - parity, 2)
                    new_state(n, 0)
                    if not last:
                        masked(n + 1, 1 - parity, 3)
                    outputs(n, 0)
                    softmax_scores(n, first, 2)
                    u_rows(n, 1)
                    outputs(n, 1)
                    softmax_scores(n, first, 3)
                    new_state(n, 1)
                    outputs(n, 2)
                    outputs(n, 3)
                    dve.wait_ge(landed["sa"], after(n, 16, 16))
                    if not first:
                        dve.wait_ge(mixa_stored, after(n, 16, 0))
                    for i in range(2):
                        js = slice(4 * i, 4 * i + 4)
                        dve.wait_ge(ot_full, after(n, 2, i + 1))
                        then(nc.vector.tensor_tensor(mix_a[:, js], psum[:, ZY[i]].rearrange("p (j t) -> p j t", t=BT),
                                                     sa[:, js], ALU.mult))
                        dve.sem_inc(ot_read, 1)
                    dve.sem_inc(mixa_ready, 1)

                then(nc.vector.memset(eps[:], LNX_EPS))
                dve.sem_inc(inited, 1)
                dve.sem_inc(mix_stored, 16)
                dve.wait_ge(sinks_landed, 16)
                then(nc.vector.tensor_scalar(neg_sinks[:], sinks[:], -1.0, None, ALU.mult))
                for g in range(GROUPS):
                    masked(0, 0, g)
                rounds(dve, round_, count)
                mean(NB)
                variance(NB)
                deviation(NB)
                gated(NB)

            @block.tensor
            def _(pe):
                ident = const("ident")

                def turn(dst, src):
                    return nc.tensor.transpose(dst, src, ident)

                def turn_rows(n, j):
                    if j >= 2:
                        pe.wait_ge(t_read, after(n, 8, j - 1))
                    bank = psum[:, 4 + j % 2]
                    for c in range(2):
                        turn(bank[:, c * P:(c + 1) * P], kb[:, j, c * P:(c + 1) * P])
                    turn(bank[:, 2 * P:3 * P], vt[:, j]).then_inc(t_full, 1)

                def turn_y(n):
                    pe.wait_ge(y_norm, after(n, 1, 0))
                    for i in range(2):
                        for jj in range(4):
                            j = 4 * i + jj
                            mm = turn(psum[:, 4 + i, jj * P:(jj + 1) * P],
                                      y[:, 2 * j:2 * j + 2].rearrange("p h d -> p (h d)"))
                        mm.then_inc(yt_full, 1)

                def scores(n, first, i):
                    lo = BT if first else 0
                    w = 2 * BT - lo
                    if i >= 1:
                        pe.wait_ge(s_read, after(n, 4, i))
                    for par_ in range(2):
                        rows = slice(par_ * HD, (par_ + 1) * HD)
                        for jj in range(2):
                            j = 2 * i + jj
                            mm = nc.tensor.matmul(psum[:, SCORE[par_], jj * w:(jj + 1) * w], q[rows, j],
                                                  kw[rows, j // 4, lo:], start=True, stop=True)
                        mm.then_inc(s_full, 1)

                def turn_p(n, first, i, m):
                    pe.wait_ge(p_ready, after(n, 4, i + 1))
                    if i >= 1:
                        pe.wait_ge(pt_read, after(n, 8, 2 * i + m - 1))
                    at = 0
                    for hh in (2 * m, 2 * m + 1):
                        for wnd in ((1,) if first else (0, 1)):
                            mm = turn(psum[:, TURNED_P[m], at:at + P], score[i % 2][:, hh, wnd * BT:(wnd + 1) * BT])
                            at += P
                    mm.then_inc(pt_full, 1)

                def values(n, first, i):
                    kv = i // 2
                    bank, start = OUT[i]
                    wnds = (1,) if first else (0, 1)
                    for hh in range(4):
                        if hh % 2 == 0:
                            pe.wait_ge(pt_read, after(n, 8, 2 * i + hh // 2 + 1))
                        for x, wnd in enumerate(wnds):
                            at = (hh % 2) * len(wnds) * P + x * P
                            out = start + hh * HD
                            mm = nc.tensor.matmul(psum[:, bank, out:out + HD],
                                                  pt[:, hh // 2, at:at + P],
                                                  va[:, wnd, kv * HD:(kv + 1) * HD],
                                                  start=(x == 0), stop=(x == len(wnds) - 1))
                    mm.then_inc(o_full, 1)

                def products(n, g):
                    if g == 0:
                        pe.wait_ge(landed["kb"], after(n, 16, 16))
                        pe.wait_ge(landed["qr"], after(n, 16, 16))
                    else:
                        pe.wait_ge(a_read, after(n, 8, 2 * g))
                    mm = [None, None]
                    for jj in range(2):
                        j = 2 * g + jj
                        for c in range(2):
                            for par_ in range(2):
                                rows = slice(par_ * HD, (par_ + 1) * HD)
                                full = psum[:, PRODUCT[par_], jj * 4 * C:(jj + 1) * 4 * C]
                                dst = full.rearrange("p (s t) -> p s t", t=C)[:, c::2]
                                mm[par_] = nc.tensor.matmul(dst, kb[rows, j, c * P:(c + 1) * P],
                                                            qr[rows, j, c * P:(c + 1) * P],
                                                            start=True, stop=True)
                    for par_ in range(2):
                        mm[par_].then_inc(a_full, 1)

                def inversion(n, am, first):
                    done = {}
                    for i, (kind, g) in enumerate(ORDER):
                        needs = {"Y": [], "D": [("Y", g)], "DT": [("Y", g)], "Y2": [("D", g), ("DT", g)],
                                 "DT2": [("Y2", g), ("DT", g)]}[kind]
                        needs = [done[x] for x in needs] + [lev_before(i)]
                        needs = [x for x in needs if x is not None]
                        if needs:
                            pe.wait_ge(lev_read, after(n, LEV, max(needs) + 1))
                        done[(kind, g)] = i
                        if kind == "DT" and g == 0 and not first:
                            pe.wait_ge(ot_read, after(n, 2, 0))
                        for hh in range(4):
                            h = 4 * g + hh
                            lhs, rhs = {
                                "Y": (am[:, h, C:3 * C], x16[:, h, 0]),
                                "D": (x16[:, h, 1], ym[:, h]),
                                "DT": (ym[:, h], x16[:, h, 1]),
                                "Y2": (am[:, h, C:3 * C], x32[:, h]),
                                "DT2": (ym[:, h], xt[:, h]),
                            }[kind]
                            mm = nc.tensor.matmul(psum[:, lev_bank(i), hh * P:(hh + 1) * P], lhs, rhs,
                                                  start=True, stop=True)
                        mm.then_inc(lev_full, 1)
                        if i < PAIRS:
                            turn_rows(n, i)

                def z(n, c, am):
                    us, _ = sides(c)
                    cols = slice(c * P, (c + 1) * P)
                    if c == 1:
                        pe.wait_ge(state_new, after(n, 2, 1))
                    for i in range(2):
                        if c == 1:
                            pe.wait_ge(y_read, after(n, 4, i + 1))
                        for jj in range(4):
                            j = 4 * i + jj
                            nc.tensor.matmul(psum[:, ZY[i], jj * P:(jj + 1) * P], qr_s[:, j, cols],
                                             state[:, j].rearrange("p h d -> p (h d)"),
                                             start=(jj == 0), stop=False, skip_group_check=True)
                        for hh in range(8):
                            h = 8 * i + hh
                            mm = nc.tensor.matmul(psum[us, ZY[i], hh * HD:(hh + 1) * HD],
                                                  am[:, h, KK[c]:KK[c] + C], uv[:, c, h],
                                                  start=False, stop=False, skip_group_check=True)
                        mm.then_inc(z_full, 1)

                def u(n, c):
                    us, vs = sides(c)
                    for i in range(2):
                        pe.wait_ge(z_read, after(n, 4, 2 * c + i + 1))
                        if c == 1:
                            pe.wait_ge(u_read, after(n, 4, 2))
                            pe.wait_ge(o_read, after(n, 4, 1))
                        pe.sem_inc(apart, 1)
                        for hh in range(8):
                            h = 8 * i + hh
                            mm = nc.tensor.matmul(psum[(us, vs)[i], U, hh * HD:(hh + 1) * HD], xt[us, h, us],
                                                  zs[us, h], start=True, stop=True, skip_group_check=True)
                        mm.then_inc(u_full, 1)

                def f(n, c):
                    if c == 1:
                        pe.wait_ge(o_read, after(n, 4, 2))
                    for i in range(2):
                        pe.wait_ge(u_read, after(n, 4, 2 * c + i + 1))
                        for hh in range(8):
                            h = 8 * i + hh
                            half = slice((h % 2) * HD, (h % 2 + 1) * HD)
                            mm = nc.tensor.matmul(psum[half, F, (h // 2) * HD:(h // 2 + 1) * HD],
                                                  kbt[:, c, h // 2, half], uv[:, c, h],
                                                  start=True, stop=True, skip_group_check=True)
                    mm.then_inc(f_full, 1)

                def rows(n, c, am):
                    _, vs = sides(c)
                    for i in range(2):
                        for hh in range(8):
                            h = 8 * i + hh
                            mm = nc.tensor.matmul(psum[vs, ZY[i], hh * HD:(hh + 1) * HD],
                                                  am[:, h, R[c]:R[c] + C], uv[:, c, h],
                                                  start=False, stop=(hh == 7), skip_group_check=True)
                        mm.then_inc(y_full, 1)

                def round_(n, parity, first, last):
                    am = am2[parity]
                    pe.wait_ge(landed["vt"], after(n, 16, 16))
                    pe.wait_ge(x_in, after(n, 8 * 16, 8 * 16))
                    if first:
                        pe.wait_ge(a_read, 8)
                    else:
                        pe.wait_ge(s_read, after(n, 4, 0))
                        pe.wait_ge(o_read, after(n, 4, 0))
                        pe.wait_ge(pt_read, after(n, 8, 0))
                        pe.wait_ge(y_read, after(n, 4, 0))
                        pe.wait_ge(u_read, after(n, 4, 0))
                        pe.wait_ge(state_read, after(n, 2, 0))
                    inversion(n, am, first)
                    pe.wait_ge(landed["q"], after(n, 16, 16))
                    pe.wait_ge(landed["kw"], after(n, 32, 32))
                    pe.wait_ge(lev_read, after(n, LEV, LEV))
                    scores(n, first, 0)
                    pe.wait_ge(landed["vw"], after(n, 16, 16))
                    if not first:
                        turn(psum[:, TURNED_P[0], 0:P], vw[:, 0:BT])
                    turn(psum[:, TURNED_P[0], P:2 * P], vw[:, BT:]).then_inc(va_full, 1)
                    pe.wait_ge(t_read, after(n, 8, 8))
                    if not first:
                        turn_y(n)
                    pe.wait_ge(va_read, after(n, 1, 1))
                    if not last:
                        products(n + 1, 0)
                    pe.wait_ge(landed["qr_s"], after(n, 16, 16))
                    if first:
                        pe.wait_ge(inited, 2)
                    else:
                        pe.wait_ge(state_new, after(n, 2, 0))
                    z(n, 0, am)
                    if not last:
                        products(n + 1, 1)
                    scores(n, first, 1)
                    if not first:
                        pe.wait_ge(yt_read, after(n, 2, 0))
                    u(n, 0)
                    if not last:
                        products(n + 1, 2)
                    f(n, 0)
                    if not last:
                        products(n + 1, 3)
                    rows(n, 0, am)
                    if not last:
                        pe.wait_ge(a_read, after(n + 1, 8, 8))
                    turn_p(n, first, 0, 0)
                    turn_p(n, first, 0, 1)
                    z(n, 1, am)
                    values(n, first, 0)
                    scores(n, first, 2)
                    turn_p(n, first, 1, 0)
                    turn_p(n, first, 1, 1)
                    u(n, 1)
                    pe.wait_ge(state_read, after(n, 2, 1))
                    values(n, first, 1)
                    scores(n, first, 3)
                    turn_p(n, first, 2, 0)
                    turn_p(n, first, 2, 1)
                    f(n, 1)
                    values(n, first, 2)
                    rows(n, 1, am)
                    turn_p(n, first, 3, 0)
                    turn_p(n, first, 3, 1)
                    pe.wait_ge(state_read, after(n, 2, 2))
                    values(n, first, 3)
                    for i in range(2):
                        pe.wait_ge(y_read, after(n, 4, i + 3))
                        pe.wait_ge(o_read, after(n, 4, 2 * i + 2))
                        for jj in range(4):
                            j = 4 * i + jj
                            mm = turn(psum[:, ZY[i], jj * P:(jj + 1) * P],
                                      o[:, 2 * j:2 * j + 2].rearrange("p h d -> p (h d)"))
                        mm.then_inc(ot_full, 1)

                pe.wait_ge(inited, 2)
                for g in range(GROUPS):
                    products(0, g)
                rounds(pe, round_)
                pe.wait_ge(u_read, 4 * NB)
                pe.wait_ge(state_read, 2 * NB)
                turn_y(NB)


def stage_c(nc, io, scr, cst):
    with ExitStack() as ctx:
        def sb(name, shape, dt=F32):
            return ctx.enter_context(nc.sbuf_tensor("c_" + name, shape, dt))

        def sem(name):
            return ctx.enter_context(nc.semaphore("c_" + name))

        m_in = sb("m_in", [P, HALF])
        m_hi = sb("m_hi", [P, 2, KC, HALF], F32R)
        m_lo = sb("m_lo", [P, 2, KC, HALF], F32R)
        w_raw = [sb(f"w_raw{i}", [P, KH * P]) for i in range(2)]
        w_hi = [sb(f"w_hi{i}", [P, KH * P], F32R) for i in range(2)]
        w_lo = [sb(f"w_lo{i}", [P, KH * P], F32R) for i in range(2)]
        x_in = sb("x_in", [P, HALF])
        xn = sb("xn", [P, KC, HALF])
        sq = sb("sq", [P, HALF])
        acc = sb("acc", [P, HALF])
        rms = sb("rms", [P, HALF])
        gain = sb("gain", [P, KC])
        eps = sb("eps", [P, 1])
        psum = ctx.enter_context(nc.psum_tensor("psum_c", [P, 8, HALF], F32))

        gain_landed = sem("gain_landed")
        m_landed = [sem(f"m_landed{i}") for i in range(KC // 2)]
        m2_landed = sem("m2_landed")
        m_high, m_ready = sem("m_high"), sem("m_ready")
        w_landed = [sem(f"w_landed{i}") for i in range(2)]
        w_high = [sem(f"w_high{i}") for i in range(2)]
        w_ready = [sem(f"w_ready{i}") for i in range(2)]
        w_used = [sem(f"w_used{i}") for i in range(2)]
        x_landed = sem("x_landed")
        tile_done, tile_read = sem("tile_done"), sem("tile_read")
        squared, summed, gained = sem("squared"), sem("summed"), sem("gained")
        mean_done, rooted, rms_ready = sem("mean_done"), sem("rooted"), sem("rms_ready")
        scaled_pool, scaled_dve = sem("scaled_pool"), sem("scaled_dve")
        out_stored = [sem(f"out_stored{i}") for i in range(4)]
        inited = sem("inited")

        BY_DVE = (4, 10)
        GROUP = 2
        LAST = 2 * KC - 1

        with nc.Block() as block:
            @block.sync
            def _(sp):
                def load_half(s, t, half, first=False):
                    if not first:
                        sp.wait_ge(w_ready[half], s)
                    sp.dma_start(w_raw[half][:], io["w_out"][ds(t, 1), half].rearrange("a p n -> (a p) n")
                                 ).then_inc(w_landed[half], 16)

                def load_x(s, t, h, first=False):
                    if not first:
                        sp.wait_ge(tile_read, s)
                    sp.dma_start(x_in[:], io["x_t"][ds(t, 1), :, h * HALF:(h + 1) * HALF]
                                 .rearrange("a p n -> (a p) n")).then_inc(x_landed, 16)

                def load_mix(i):
                    for k in (2 * i, 2 * i + 1):
                        src = scr["MIX"][0:NB // 2, :, k].rearrange("b p t -> p b t")
                        sp.dma_start(xn[:, k].rearrange("p (b t) -> p b t", t=BT), src
                                     ).then_inc(m_landed[i], 16)

                sp.dma_start(gain[:], io["final_gain"]).then_inc(gain_landed, 16)
                def load_mix_2(k):
                    if not isinstance(k, int) or k > 0:
                        sp.wait_ge(m_ready, KC // 2 + k)
                    src = scr["MIX"][NB // 2:, :, ds(k, 1)].rearrange("b p c t -> p (b c) t")
                    sp.dma_start(m_in[:].rearrange("p (b t) -> p b t", t=BT), src).then_inc(m2_landed, 16)

                load_half(0, 0, 0, True)
                for i in range(3):
                    load_mix(i)
                load_half(0, 0, 1, True)
                for i in range(3, KC // 2):
                    load_mix(i)
                load_x(0, 0, 0, True)
                for h in range(2):
                    if h == 1:
                        for half in range(2):
                            load_half(KC, 0, half)
                        load_x(KC, 0, 1)
                        first = 1
                    else:
                        for half in range(2):
                            load_half(1, 1, half)
                        load_mix_2(0)
                        load_mix_2(1)
                        load_x(1, 1, 0)
                        first = 2
                    with sp.Fori(first, KC) as t:
                        for half in range(2):
                            load_half(h * KC + t, t, half)
                        if h == 0:
                            load_mix_2(t)
                        load_x(h * KC + t, t, h)
                for t in range(0, KC, GROUP):
                    if t < BY_DVE[1]:
                        sp.wait_ge(scaled_dve, BY_DVE[0] + t // GROUP + 1)
                    else:
                        sp.wait_ge(scaled_pool, KC - BY_DVE[0] + (t - BY_DVE[1]) // GROUP + 1)
                    sp.dma_start(io["out"][t:t + GROUP, :, HALF:].rearrange("k p n -> p k n"),
                                 xn[:, t:t + GROUP]).then_inc(out_stored[3], 16)
                sp.wait_ge(out_stored[3], 16 * KC // GROUP)

            @block.scalar
            def _(act):
                def high_half(s, half, first=False):
                    act.wait_ge(w_landed[half], 16 * (s + 1))
                    if not first:
                        act.wait_ge(w_used[half], s)
                    nc.scalar.activation(w_hi[half][:], w_raw[half][:], ACT.Copy).then_inc(w_high[half], 1)

                def mix_high(i):
                    act.wait_ge(m_landed[i], 32)
                    two = slice(2 * i, 2 * i + 2)
                    nc.scalar.activation(m_hi[:, 0, two], xn[:, two], ACT.Copy).then_inc(m_high, 1)

                def mix_high_2(k):
                    act.wait_ge(m2_landed, 16 * (k + 1))
                    nc.scalar.activation(m_hi[:, 1, ds(k, 1)].rearrange("p a t -> p (a t)"), m_in[:],
                                         ACT.Copy).then_inc(m_high, 1)

                def square(s, t, first=False):
                    act.wait_ge(tile_read, s + 1)
                    if not first:
                        act.wait_ge(summed, s)
                    tile = xn[:, ds(t, 1)].rearrange("p a t -> p (a t)")
                    nc.scalar.activation(sq[:], tile, ACT.Square).then_inc(squared, 1)
                    act.wait_ge(squared, s + 1)
                    nc.scalar.activation(tile, tile, ACT.Copy, scale=gain[:, ds(t, 1)]).then_inc(gained, 1)

                def root(h):
                    act.wait_ge(mean_done, h + 1)
                    nc.scalar.activation(rms[:], psum[:, 4], ACT.Sqrt, bias=eps[:, 0:1]).then_inc(rooted, 1)

                act.wait_ge(inited, 1)
                act.wait_ge(gain_landed, 16)
                high_half(0, 0, True)
                for i in range(KC // 2):
                    if i == 3:
                        high_half(0, 1, True)
                    mix_high(i)
                for h in range(2):
                    s = h * KC
                    if h == 1:
                        high_half(s, 0)
                        high_half(s, 1)
                        square(s - 1, KC - 1)
                        root(0)
                    high_half(s + 1, 0)
                    high_half(s + 1, 1)
                    if h == 0:
                        mix_high_2(0)
                        mix_high_2(1)
                    square(s, 0, first=(h == 0))
                    with act.Fori(2, KC) as t:
                        high_half(s + t, 0)
                        high_half(s + t, 1)
                        if h == 0:
                            mix_high_2(t)
                        square(s + t - 1, t - 1)
                square(LAST, KC - 1)
                root(1)

            @block.vector
            def _(dve):
                def low_half(s, half):
                    dve.wait_ge(w_high[half], s + 1)
                    nc.vector.tensor_tensor(w_lo[half][:], w_raw[half][:], w_hi[half][:].bitcast(F32),
                                            ALU.subtract).then_inc(w_ready[half], 1)

                def mix_low(i):
                    dve.wait_ge(m_high, i + 1)
                    two = slice(2 * i, 2 * i + 2)
                    nc.vector.tensor_tensor(m_lo[:, 0, two], xn[:, two], m_hi[:, 0, two].bitcast(F32),
                                            ALU.subtract).then_inc(m_ready, 1)

                def mix_low_2(k):
                    dve.wait_ge(m_high, KC // 2 + k + 1)
                    lo, hi = (m[:, 1, ds(k, 1)].rearrange("p a t -> p (a t)") for m in (m_lo, m_hi))
                    nc.vector.tensor_tensor(lo, m_in[:], hi.bitcast(F32), ALU.subtract).then_inc(m_ready, 1)

                def add(s, t, bank, h):
                    dve.wait_ge(tile_done, s + 1)
                    dve.wait_ge(x_landed, 16 * (s + 1))
                    if h == 1:
                        which = min(t, 2) if isinstance(t, int) else 2
                        dve.wait_ge(out_stored[which], 16 * (1, 1, KC - 2)[which])
                    nc.vector.tensor_tensor(xn[:, ds(t, 1)].rearrange("p a t -> p (a t)"), psum[:, bank],
                                            x_in[:], ALU.add).then_inc(tile_read, 1)

                def invert(h):
                    dve.wait_ge(rooted, h + 1)
                    nc.vector.reciprocal(rms[:], rms[:]).then_inc(rms_ready, 1)

                nc.vector.memset(eps[:], RMS_EPS).then_inc(inited, 1)
                low_half(0, 0)
                for i in range(KC // 2):
                    if i == 3:
                        low_half(0, 1)
                    mix_low(i)
                for h in range(2):
                    s = h * KC
                    if h == 1:
                        low_half(s, 0)
                        low_half(s, 1)
                        add(s - 1, KC - 1, 1, 0)
                        invert(0)
                        dve.wait_ge(rms_ready, 1)
                        dve.wait_ge(gained, KC)
                        for t in range(BY_DVE[0]):
                            nc.vector.tensor_tensor(xn[:, t], xn[:, t], rms[:], ALU.mult).then_inc(scaled_dve, 1)
                    low_half(s + 1, 0)
                    low_half(s + 1, 1)
                    if h == 0:
                        mix_low_2(0)
                        mix_low_2(1)
                    add(s, 0, 0, h)
                    if h == 1:
                        low_half(s + 2, 0)
                        low_half(s + 2, 1)
                        add(s + 1, 1, 1, h)
                        low_half(s + 3, 0)
                        low_half(s + 3, 1)
                        add(s + 2, 2, 0, h)
                    with dve.Fori(1 + h, KC // 2) as m:
                        for i in range(2):
                            low_half(s + 2 * m + i, 0)
                            low_half(s + 2 * m + i, 1)
                            if h == 0:
                                mix_low_2(2 * m + i)
                            add(s + 2 * m + i - 1, 2 * m + i - 1, 1 - i, h)
                add(LAST, KC - 1, 1, 1)
                invert(1)
                dve.wait_ge(rms_ready, 2)
                dve.wait_ge(gained, 2 * KC)
                for t in range(0, BY_DVE[1], GROUP):
                    group = xn[:, t:t + GROUP]
                    nc.vector.tensor_tensor(group, group, rms[:].unsqueeze(1).broadcast_to([P, GROUP, HALF]),
                                            ALU.mult).then_inc(scaled_dve, 1)

            @block.gpsimd
            def _(pool):
                def accumulate(s, first=False):
                    pool.wait_ge(squared, s + 1)
                    if first:
                        ins = nc.gpsimd.tensor_copy(acc[:], sq[:])
                    else:
                        pool.wait_ge(summed, s)
                        ins = nc.gpsimd.tensor_tensor(acc[:], acc[:], sq[:], ALU.add)
                    ins.then_inc(summed, 1)

                def scale(t, n=1):
                    group = xn[:, t:t + n]
                    nc.gpsimd.tensor_tensor(group, group, rms[:].unsqueeze(1).broadcast_to([P, n, HALF]),
                                            ALU.mult).then_inc(scaled_pool, 1)

                def store(t):
                    if t < BY_DVE[0]:
                        pool.wait_ge(scaled_dve, t + 1)
                    else:
                        pool.wait_ge(scaled_pool, t - BY_DVE[0] + 1)
                    pool.dma_start(io["out"][t, :, 0:HALF], xn[:, t]).then_inc(out_stored[min(t, 2)], 16)

                accumulate(0, True)
                with pool.Fori(1, KC) as t:
                    accumulate(t)
                pool.wait_ge(mean_done, 1)
                pool.wait_ge(rms_ready, 1)
                pool.wait_ge(gained, KC)
                for t in range(BY_DVE[0]):
                    store(t)
                for t in range(BY_DVE[0], KC // 2):
                    scale(t)
                    store(t)
                accumulate(KC, True)
                for t in range(KC // 2, KC):
                    scale(t)
                    store(t)
                with pool.Fori(KC + 1, 2 * KC) as s:
                    accumulate(s)
                pool.wait_ge(rms_ready, 2)
                pool.wait_ge(gained, 2 * KC)
                for t in range(BY_DVE[1], KC, GROUP):
                    scale(t, GROUP)
                for i, n in enumerate((1, 1, KC - 2)):
                    pool.wait_ge(out_stored[i], 16 * n)

            @block.tensor
            def _(pe):
                def project(s, bank, h, pace=False, between=None):
                    if between is not None or not pace:
                        pe.wait_ge(tile_read, s - 1)
                    for half in range(2):
                        pe.wait_ge(w_ready[half], s + 1)
                        for kk in range(KH):
                            c = half * KH + kk
                            if pace:
                                pe.wait_ge(m_ready, (c // 2 + 1) if h == 0 else KC // 2 + c + 1)
                            cols = slice(kk * P, (kk + 1) * P)
                            for wt, mt in ((w_hi, m_hi), (w_hi, m_lo), (w_lo, m_hi)):
                                mm = nc.tensor.matmul(psum[:, bank], wt[half][:, cols], mt[:, h, c],
                                                      start=(c == 0 and wt is w_hi and mt is m_hi),
                                                      stop=(c == KC - 1 and wt is w_lo))
                        mm.then_inc(w_used[half], 1)
                        if half == 0 and between is not None:
                            between()
                    pe.wait_ge(w_used[1], s + 1)
                    pe.sem_inc(tile_done, 1)

                def mean(h):
                    pe.wait_ge(summed, (h + 1) * KC)
                    nc.tensor.matmul(psum[:, 4], cst[:, slice(*CONSTS["mean"])], acc[:],
                                     start=True, stop=True).then_inc(mean_done, 1)

                for h in range(2):
                    s = h * KC
                    if h == 0:
                        project(0, 0, 0, pace=True)
                        project(1, 1, 0, pace=True)
                    else:
                        project(s, 0, 1, pace=True, between=lambda: mean(0))
                        project(s + 1, 1, 1)
                    with pe.Fori(1, KC // 2) as m:
                        project(s + 2 * m, 0, h)
                        project(s + 2 * m + 1, 1, h)
                mean(1)


SCRATCH = {
    "KB": (NB, P, PAIRS, 4, C), "QR": (NB, P, PAIRS, 4, C),
    "V": (NB, P, PAIRS, BT), "GS": (NB, P, PAIRS, BT), "BS": (NB, P, PAIRS, BT),
    "Q": (NB, P, PAIRS, BT), "SA": (NB, P, PAIRS, BT),
    "KVA": (2, P, T), "MIX": (NB, P, KC, BT),
    "L": (P // SUB, HEADS, SUB, SUB), "X": (P // SUB, HEADS, 2, SUB, SUB),
}


def layout(inputs):
    a = {n: np.asarray(v) for n, v in inputs.items()}

    def tiles(w, starts):
        w = w.reshape(2, KH, P, -1)
        w = np.stack([w[..., s:s + P] for s in starts])
        return np.ascontiguousarray(w.transpose(0, 1, 3, 2, 4)).reshape(len(starts), 2, P, KH * P)

    def channels(v, n):
        return np.asarray(v).reshape(n, P).T

    att = RWKV_COLS
    starts = [3 * RW, att + AW, att + AW + KVW]
    for j in range(PAIRS):
        starts += [j * P, RW + j * P, 2 * RW + j * P, 3 * RW + 2 * LORA + j * P,
                   att + j * P, att + AW + 2 * KVW + j * P]
    mu = a["mu_rwkv"][0]
    per = {"mu_r": mu[:RW], "mu_k": mu[RW:2 * RW], "mu_v": mu[2 * RW:3 * RW],
           "mu_g": mu[3 * RW + 2 * LORA:], "w0": a["w0"], "a0": a["a0"], "k_k": a["k_k"],
           "k_a": a["k_a"], "r_k": a["r_k"], "gain": a["lnx_gain"], "bias": a["lnx_bias"]}
    par = np.stack([channels(per[n], PAIRS) for n in PAR], axis=2)
    lora_up = np.concatenate([a["w_up"][0], a["a_up"][0]]).reshape(2 * LORA, PAIRS, P).transpose(1, 0, 2)
    quads = [4 * i + 2 * (hh % 2) + hh // 2 for i in range(HEADS // 4) for hh in range(4)]
    x_t = np.ascontiguousarray(a["x"][0].T).reshape(KC, P, T)
    out = {
        "x_t": x_t,
        "w_in": tiles(a["w_in"][0], starts),
        "w_out": tiles(a["w_out"][0], range(0, D, P)),
        "par": par,
        "par1": np.concatenate([channels(a["norm_gain"][0], KC), mu[3 * RW:3 * RW + 2 * LORA, None]], axis=1),
        "final_gain": channels(a["final_gain"], KC),
        "sinks": np.broadcast_to(a["attn_sinks"][0, quads], (P, HEADS)),
        "lora_up": lora_up,
        "consts": constants(),
    }
    return {n: np.ascontiguousarray(v) for n, v in out.items()}


def program(nc, io, scr):
    with ExitStack() as ctx:
        pc_all = ctx.enter_context(nc.sbuf_tensor("pc_all", [P, PAIRS, NC_], F32))
        cst = ctx.enter_context(nc.sbuf_tensor("cst", [P, CONST_COLS], F32))
        used = stage_a(nc, io, scr, pc_all, cst)
        stage_b(nc, io, scr, pc_all, cst, used)
        stage_c(nc, io, scr, cst)


def kernel(**inputs):
    from concourse import bacc
    from concourse.bass_utils import run_bass_kernel_spmd

    nc = bacc.Bacc("TRN2", target_bir_lowering=False, num_devices=1)
    arrays = {f"in_{name}": a for name, a in layout(inputs).items()}
    io = {name: nc.dram_tensor(f"in_{name}", arrays[f"in_{name}"].shape, F32, kind="ExternalInput").ap()
          for name in (n[3:] for n in arrays)}
    scr = {name: nc.dram_tensor(f"scratch_{name}", shape, F32).ap() for name, shape in SCRATCH.items()}
    io["out"] = nc.dram_tensor("out", (KC, P, T), F32, kind="ExternalOutput").ap()
    program(nc, io, scr)
    r = run_bass_kernel_spmd(nc, [arrays], core_ids=[0])
    return np.ascontiguousarray(np.asarray(r.results[0]["out"]).reshape(D, T).T)[None]
```

```python
import math
from contextlib import ExitStack

import concourse.bass as bass
import numpy as np
from concourse import mybir
from concourse.bass import ds

F32 = mybir.dt.float32
F32R = mybir.dt.float32r
U8 = mybir.dt.uint8
ALU = mybir.AluOpType
ACT = mybir.ActivationFunctionType
AX = mybir.AxisListType.X

P = 128
T = 1024
D = 2048
KC = D // P
HD = 64
PAIRS = 8
HEADS = 2 * PAIRS
LORA = 64
RW = PAIRS * P
AW = PAIRS * P
KVW = 2 * HD
RWKV_COLS = 4 * RW + 2 * LORA
TILES = (RWKV_COLS + 2 * AW + 2 * KVW) // P
C = 64
BT = 128
NB = T // BT
NC_ = T // C
SUB = 16
HALF = T // 2
KH = KC // 2
POOL_STEPS = 39
DVE_STEPS = 68
DECAY = math.exp(-0.5)
RMS_EPS = 1e-5
LNX_EPS = 64e-5

PAR = ["mu_r", "mu_k", "mu_v", "mu_g", "w0", "a0", "k_k", "k_a", "r_k", "gain", "bias"]
NPAR = len(PAR)
CONSTS = {}
_at = 0
for _name, _w in (("ident", 128), ("same_head", 128), ("mean", 128), ("amask", 256), ("m16", 128),
                  ("m32", 128), ("dist", 256), ("head_of", 2)):
    CONSTS[_name] = (_at, _at + _w)
    _at += _w
CONST_COLS = _at


def constants():
    r = np.arange(128)[:, None]
    c = np.arange(128)[None, :]
    t = {}
    t["ident"] = (r == c)
    t["same_head"] = (r // HD == c // HD)
    t["mean"] = np.full((128, 128), 1.0 / D)
    s, u = r % C, np.arange(C)[None, :]
    t["amask"] = np.concatenate([s <= u, s < u, s < u, s <= u], axis=1)
    for m in (16, 32):
        t[f"m{m}"] = (r // (2 * m) == c // (2 * m)) & (r % (2 * m) >= m) & (c % (2 * m) < m)
    key = np.arange(2 * BT)[None, :]
    d = BT + r - key
    t["dist"] = np.where((d >= 0) & (d < BT), d, 1e33)
    t["head_of"] = (r // HD == np.arange(2)[None, :])
    return np.concatenate([t[n].astype(np.float32) for n in CONSTS], axis=1)


def after(n, per, k):
    return n * per + k


def stage_a(nc, io, scr, pc_all, consts):
    with ExitStack() as ctx:
        def sb(name, shape, dt=F32):
            return ctx.enter_context(nc.sbuf_tensor("a_" + name, shape, dt))

        semaphores = []

        def sem(name):
            semaphores.append(nc.alloc_semaphore(name))
            return semaphores[-1]

        x_hi = sb("x_hi", [P, KC, T], F32R)
        x_lo = sb("x_lo", [P, KC, T], F32R)
        w_raw = sb("w_raw", [P, KH * P])
        w_hi = [sb(f"w_hi{i}", [P, KH * P], F32R) for i in range(2)]
        w_lo = [sb(f"w_lo{i}", [P, KH * P], F32R) for i in range(2)]
        rms = sb("rms", [P, T])
        keep = sb("keep", [P, T], U8)
        lora = sb("lora", [P, T])
        raw = sb("raw", [P, T + 1])
        r = sb("r", [P, T])
        k = sb("k", [P, T])
        v = sb("v", [P, T])
        g = sb("g", [P, T])
        s1 = sb("s1", [P, T])
        s2 = sb("s2", [P, T])
        a = sb("a", [P, T])
        b = sb("b", [P, T])
        decay = sb("decay", [P, NC_, C + 1])
        grow = sb("grow", [P, T])
        par = sb("par", [P, PAIRS, NPAR])
        par1 = sb("par1", [P, KC + 1])
        lora_up = sb("lora_up", [P, P])
        inv2 = sb("inv2", [P, 2 * NB])
        eps = sb("eps", [P, 1])
        cst = consts
        x_in = [r, k, v, g]
        sq = [s1, s2]
        acc, acc_odd = a, b
        psum = ctx.enter_context(nc.psum_tensor("psum_a", [P, 8, HALF], F32))

        def banks(i):
            return psum[:, i:i + 2, :].rearrange("p b t -> p (b t)")

        par1_landed = sem("a_par1_landed")
        par_landed = sem("a_par_landed")
        x_landed = [sem(f"a_x_landed{i}") for i in range(4)]
        x_squared = sem("a_x_squared")
        x_high = sem("a_x_high")
        x_ready = sem("a_x_ready")
        x_summed = sem("a_x_summed")
        x_summed_odd = sem("a_x_summed_odd")
        ms_done = sem("a_ms_done")
        rms_root = sem("a_rms_root")
        inv_rms = sem("a_inv_rms")
        w_landed = sem("a_w_landed")
        w_high = [sem(f"a_w_high{i}") for i in range(2)]
        w_ready = [sem(f"a_w_ready{i}") for i in range(2)]
        w_used = sem("a_w_used")
        tile_done = sem("a_tile_done")
        tile_read = sem("a_tile_read")
        up_landed = sem("a_up_landed")
        lora_ready = sem("a_lora_ready")
        lora_done = sem("a_lora_done")
        norm_done = sem("a_norm_done")
        sigma_w = sem("a_sigma_w")
        sigma_a = sem("a_sigma_a")
        summed = sem("a_summed")
        exps = sem("a_exps")
        squares = sem("a_squares")
        k_ready = sem("a_k_ready")
        inv_ready = sem("a_inv_ready")
        inv_spread = sem("a_inv_spread")
        rkr_ready = sem("a_rkr_ready")
        bonus_done = sem("a_bonus_done")
        g_ready = sem("a_g_ready")
        gate_sig = sem("a_gate_sig")
        ga_ready = sem("a_ga_ready")
        ga_sig = sem("a_ga_sig")
        kk_read = sem("a_kk_read")
        bonus_read = sem("a_bonus_read")
        names = ["R", "KK", "K", "B", "V", "GS", "BS", "Q", "SA"]
        made = {x: sem(f"a_made_{x}") for x in names}
        stored = {x: sem(f"a_stored_{x}") for x in names}
        stores_begun = sem("a_stores_begun")
        kv_made = sem("a_kv_made")
        kv_stored = sem("a_kv_stored")
        steps = sem("a_dve_steps")

        PRO = 3
        TP = 6

        with nc.Block() as block:
            @block.sync
            def _(sp):
                def load_half(t, half, first):
                    if not first:
                        if half == 0:
                            sp.wait_ge(w_ready[1], t)
                        else:
                            sp.wait_ge(w_ready[0], t + 1)
                    elif half == 1:
                        sp.wait_ge(w_ready[0], 1)
                    sp.dma_start(w_raw[:], io["w_in"][ds(t, 1), half].rearrange("a p n -> (a p) n")
                                 ).then_inc(w_landed, 16)

                sp.dma_start(par1[:], io["par1"]).then_inc(par1_landed, 16)
                load_half(0, 0, True)
                for c in range(KC):
                    if c == 2:
                        load_half(0, 1, True)
                    if c == 10:
                        load_half(1, 0, False)
                    if c >= 4:
                        sp.wait_ge(x_ready, c - 3)
                    sp.dma_start(x_in[c % 4][:], io["x_t"][c]).then_inc(x_landed[c % 4], 16)
                sp.dma_start(cst[:], io["consts"]).then_inc(par_landed, 16)
                sp.dma_start(par[:], io["par"]).then_inc(par_landed, 16)
                for c in range(KC):
                    if c == 0:
                        load_half(1, 1, False)
                    if c == 10:
                        load_half(2, 0, False)
                    if c < 4:
                        sp.wait_ge(x_ready, KC - 3 + c)
                    else:
                        sp.wait_ge(x_squared, c - 3)
                    sp.dma_start(x_in[c % 4][:], io["x_t"][c]).then_inc(x_landed[c % 4], 16)
                load_half(2, 1, False)
                with sp.Fori(PRO, TILES) as t:
                    load_half(t, 0, False)
                    load_half(t, 1, False)

            @block.gpsimd
            def _(pool):
                def store(n, name, src):
                    pool.wait_ge(made[name], after(n, 1, 1))
                    pool.sem_inc(stores_begun, 1)
                    if name in ("K", "B", "R", "KK"):
                        dst = scr["KB" if name in ("K", "B") else "QR"]
                        dst = dst[:, :, ds(n, 1)].rearrange("b p j s t -> p (b j) s t")
                        src = src[:].rearrange("p (b s t) -> p b s t", b=NB, s=2)
                        dst = dst[:, :, 0:4:3, :] if name in ("K", "R") else dst[:, :, 1:3, :]
                    else:
                        dst = scr[name][:, :, ds(n, 1)].rearrange("b p j t -> p (b j) t")
                        src = src.rearrange("p (b t) -> p b t", b=NB)
                    if name in ("K", "R"):
                        for c in range(2):
                            pool.dma_start(dst[:, :, c], src[:, :, c]).then_inc(stored[name], 16)
                    else:
                        if name in ("KK", "B"):
                            dst = dst.rearrange("p b s t -> p b (s t)")
                            src = src.rearrange("p b s t -> p b (s t)")
                        pool.dma_start(dst, src).then_inc(stored[name], 16)

                def load_up(n):
                    pool.dma_start(lora_up[:], io["lora_up"][ds(n, 1)].rearrange("a p n -> (a p) n")
                                   ).then_inc(up_landed, 16)

                def pair(n, first):
                    if not first:
                        pool.wait_ge(lora_done, after(n, 2, 0))
                        pool.sem_inc(stores_begun, 1)
                        load_up(n)
                        store(n - 1, "SA", raw[:, 1:T + 1])
                    store(n, "R", r)
                    store(n, "B", b)
                    store(n, "K", a)
                    store(n, "V", v[:])
                    store(n, "Q", raw[:, 1:T + 1])
                    store(n, "KK", k)
                    store(n, "BS", s2[:])
                    store(n, "GS", g[:])

                load_up(0)
                for c in range(1, KC, 2):
                    pool.wait_ge(x_squared, c + 1)
                    if c == 1:
                        ins = nc.gpsimd.tensor_copy(acc_odd[:], sq[1][:])
                    else:
                        pool.wait_ge(x_summed_odd, c // 2)
                        ins = nc.gpsimd.tensor_tensor(acc_odd[:], acc_odd[:], sq[1][:], ALU.add)
                    ins.then_inc(x_summed_odd, 1)
                for i in range(2):
                    pool.wait_ge(kv_made, i + 1)
                    pool.dma_start(scr["KVA"][i], raw[:, 1:T + 1]).then_inc(kv_stored, 16)
                pair(0, True)
                with pool.Fori(1, PAIRS) as n:
                    pair(n, False)
                store(PAIRS - 1, "SA", raw[:, 1:T + 1])
                for name in names:
                    pool.wait_ge(stored[name], 16 * PAIRS * (2 if name in ("K", "R") else 1))
                pool.wait_ge(kv_stored, 32)

            @block.scalar
            def _(act):
                def high_half(t, half, first=False):
                    act.wait_ge(w_landed, 32 * t + 16 * (half + 1))
                    if not first:
                        act.wait_ge(tile_done if half else w_used, t)
                    nc.scalar.activation(w_hi[half][:], w_raw[:], ACT.Copy).then_inc(w_high[half], 1)

                def p(n, name):
                    return par[:, ds(n, 1), PAR.index(name)]

                act.wait_ge(par1_landed, 16)
                high_half(0, 0, True)
                for c in range(KC):
                    if c == 2:
                        high_half(0, 1, True)
                    if c == 12:
                        high_half(1, 0)
                    act.wait_ge(x_landed[c % 4], 16 * (c // 4 + 1))
                    nc.scalar.activation(x_hi[:, c], x_in[c % 4][:], ACT.Copy,
                                         scale=par1[:, c:c + 1]).then_inc(x_high, 1)
                for c in range(KC):
                    if c == 3:
                        high_half(1, 1)
                    if c == 12:
                        high_half(2, 0)
                    act.wait_ge(x_landed[c % 4], 16 * ((KC + c) // 4 + 1))
                    if c >= 2:
                        act.wait_ge(x_summed_odd if c % 2 else x_summed, c // 2)
                    nc.scalar.activation(sq[c % 2][:], x_in[c % 4][:], ACT.Square).then_inc(x_squared, 1)
                high_half(2, 1)
                act.wait_ge(ms_done, 1)
                nc.scalar.activation(inv2[:], psum[:, 4, 0:2 * NB], ACT.Sqrt, bias=eps[:, 0:1]
                                     ).then_inc(rms_root, 1)
                act.wait_ge(ms_done, 2)
                nc.scalar.activation(rms[:], banks(4), ACT.Copy).then_inc(rms_root, 1)
                act.wait_ge(lora_ready, 1)
                act.wait_ge(par_landed, 32)
                nc.scalar.activation(lora[0:LORA], lora[0:LORA], ACT.Tanh).then_inc(lora_ready, 1)

                def pair(n, first):
                    t = TP * n + PRO
                    high_half(t, 0)
                    high_half(t, 1)
                    if not first:
                        act.wait_ge(ga_ready, after(n, 1, 0))
                        nc.scalar.activation(s1[:], raw[:, 1:T + 1], ACT.Sigmoid).then_inc(ga_sig, 1)
                        act.wait_ge(made["SA"], after(n, 1, 0))
                    act.wait_ge(lora_done, after(n, 2, 1))
                    nc.scalar.activation(s1[:], banks(4), ACT.Sigmoid, bias=p(n, "w0")).then_inc(sigma_w, 1)
                    act.wait_ge(lora_done, after(n, 2, 2))
                    if not first:
                        act.wait_ge(stored["K"], after(n, 32, 0))
                    nc.scalar.activation(a[:], banks(6), ACT.Sigmoid, bias=p(n, "a0")).then_inc(sigma_a, 1)
                    high_half(t + 1, 0)
                    act.wait_ge(summed, after(n, 1, 1))
                    nc.scalar.activation(decay[:, :, 1:C + 1], s2[:].rearrange("p (c t) -> p c t", t=C),
                                         ACT.Exp, scale=-DECAY).then_inc(exps, 1)
                    nc.scalar.activation(grow[:], s2[:], ACT.Exp, scale=DECAY).then_inc(exps, 1)
                    high_half(t + 1, 1)
                    high_half(t + 2, 0)
                    high_half(t + 2, 1)
                    act.wait_ge(k_ready, after(n, 1, 1))
                    act.wait_ge(exps, after(n, 2, 2))
                    nc.scalar.activation(s2[:], k[:], ACT.Square, scale=p(n, "k_k")).then_inc(squares, 1)
                    for i in (3, 4):
                        high_half(t + i, 0)
                        high_half(t + i, 1)
                    act.wait_ge(g_ready, after(n, 1, 1))
                    act.wait_ge(norm_done, after(n, 2, 1))
                    nc.scalar.activation(s2[:], g[:], ACT.Sigmoid).then_inc(gate_sig, 1)
                    high_half(t + 5, 0)
                    high_half(t + 5, 1)

                pair(0, True)
                with act.Fori(1, PAIRS) as n:
                    pair(n, False)
                act.wait_ge(ga_ready, PAIRS)
                nc.scalar.activation(s1[:], raw[:, 1:T + 1], ACT.Sigmoid).then_inc(ga_sig, 1)

            @block.vector
            def _(dve):
                count = [0, 0]

                def then(ins):
                    ins.then_inc(steps, 1)
                    count[1] += 1
                    dve.wait_ge(steps, count[0] + count[1])

                def low_half(t, half):
                    dve.wait_ge(w_high[half], t + 1)
                    nc.vector.tensor_tensor(w_lo[half][:], w_raw[:], w_hi[half][:].bitcast(F32),
                                            ALU.subtract).then_inc(w_ready[half], 1)

                def p(n, name):
                    return par[:, ds(n, 1), PAR.index(name)]

                def read_tile(t, dst, scale=None):
                    dve.wait_ge(tile_done, t + 1)
                    src = banks(2 * _parity(t))
                    if scale is None:
                        ins = nc.vector.tensor_tensor(dst, src, rms[:], ALU.mult)
                    else:
                        ins = nc.vector.scalar_tensor_tensor(dst, src, scale, rms[:], ALU.mult, ALU.mult)
                    then(ins)
                    dve.sem_inc(tile_read, 1)

                def _parity(t):
                    return parity[0]

                parity = [0]

                def tile(t, par_, dst, scale=None):
                    parity[0] = par_
                    read_tile(t, dst, scale)

                def shift(dst, mu):
                    then(nc.vector.tensor_tensor(dst, raw[:, 0:T], raw[:, 1:T + 1], ALU.subtract))
                    return nc.vector.scalar_tensor_tensor(dst, dst, mu, raw[:, 1:T + 1],
                                                          ALU.mult, ALU.add)

                then(nc.vector.memset(keep[:], 1))
                then(nc.vector.memset(keep[:].rearrange("p (c t) -> p c t", t=C)[:, :, 0:1], 0))
                then(nc.vector.memset(raw[:, 0:1], 0.0))
                then(nc.vector.memset(decay[:, :, 0:1], 1.0))
                then(nc.vector.memset(eps[:], RMS_EPS))
                low_half(0, 0)
                dve.wait_ge(par1_landed, 16)
                for c in range(KC):
                    if c == 2:
                        low_half(0, 1)
                    if c == 13:
                        low_half(1, 0)
                    dve.wait_ge(x_high, c + 1)
                    nc.vector.scalar_tensor_tensor(x_lo[:, c], x_in[c % 4][:], par1[:, c:c + 1],
                                                   x_hi[:, c].bitcast(F32), ALU.mult, ALU.subtract
                                                   ).then_inc(x_ready, 1)
                for c in range(0, KC, 2):
                    if c == 4:
                        low_half(1, 1)
                    if c == 12:
                        low_half(2, 0)
                    dve.wait_ge(x_squared, c + 1)
                    if c == 0:
                        ins = nc.vector.tensor_copy(acc[:], sq[0][:])
                    else:
                        dve.wait_ge(x_summed, c // 2)
                        ins = nc.vector.tensor_tensor(acc[:], acc[:], sq[0][:], ALU.add)
                    ins.then_inc(x_summed, 1)
                dve.wait_ge(x_summed, KC // 2)
                dve.wait_ge(x_summed_odd, KC // 2)
                nc.vector.tensor_tensor(acc[:], acc[:], acc_odd[:], ALU.add).then_inc(x_summed, 1)
                low_half(2, 1)
                dve.wait_ge(rms_root, 1)
                then(nc.vector.reciprocal(inv2[:], inv2[:]))
                then(nc.vector.tensor_copy(grow[:].rearrange("p (b d) -> p b d", d=HD),
                                           inv2[:].unsqueeze(2).broadcast_to([P, 2 * NB, HD])))
                dve.sem_inc(inv_rms, 1)
                dve.wait_ge(rms_root, 2)
                tile(0, 0, raw[:, 1:T + 1])
                shift(lora[:], par1[:, KC:KC + 1]).then_inc(lora_ready, 1)
                dve.wait_ge(lora_ready, 1)
                dve.wait_ge(par_landed, 32)
                tile(1, 1, raw[:, 1:T + 1])
                dve.sem_inc(kv_made, 1)

                def pair(n, first):
                    t = TP * n + PRO
                    low_half(t, 0)
                    low_half(t, 1)
                    if first:
                        dve.wait_ge(kv_stored, 16)
                        tile(t - 1, 3, raw[:, 1:T + 1])
                        dve.sem_inc(kv_made, 1)
                        dve.wait_ge(kv_stored, 32)
                    else:
                        dve.wait_ge(stored["Q"], after(n, 16, 0))
                        tile(t - 1, 0, raw[:, 1:T + 1])
                        dve.wait_ge(stored["BS"], after(n, 16, 0))
                        dve.sem_inc(ga_ready, 1)
                        dve.wait_ge(ga_sig, after(n, 1, 0))
                        then(nc.vector.tensor_tensor(raw[:, 1:T + 1], raw[:, 1:T + 1], s1[:], ALU.mult))
                        dve.sem_inc(made["SA"], 1)
                    dve.wait_ge(sigma_w, after(n, 1, 1))
                    if first:
                        dve.wait_ge(ms_done, 1)
                    then(nc.vector.tensor_tensor_scan(s2[:], keep[:], s1[:], 0.0, ALU.mult, ALU.add))
                    dve.sem_inc(summed, 1)
                    low_half(t + 1, 0)
                    low_half(t + 1, 1)
                    if not first:
                        dve.wait_ge(stored["SA"], after(n, 16, 0))
                        dve.wait_ge(stored["R"], after(n, 32, 0))
                    tile(t, 1, raw[:, 1:T + 1])
                    then(shift(r[:], p(n, "mu_r")))
                    low_half(t + 2, 0)
                    low_half(t + 2, 1)
                    tile(t + 1, 0, raw[:, 1:T + 1])
                    if not first:
                        dve.wait_ge(stored["KK"], after(n, 16, 0))
                        dve.wait_ge(stored["B"], after(n, 16, 0))
                    then(shift(k[:], p(n, "mu_k")))
                    dve.sem_inc(k_ready, 1)
                    dve.wait_ge(exps, after(n, 2, 2))
                    nc.vector.tensor_copy(pc_all[:, ds(n, 1)].rearrange("p a c -> p (a c)"),
                                          decay[:, :, C])
                    dve.wait_ge(sigma_a, after(n, 1, 1))
                    then(nc.vector.scalar_tensor_tensor(b[:], k[:], p(n, "k_k"), a[:], ALU.mult, ALU.mult))
                    then(nc.vector.tensor_tensor(b[:], b[:], grow[:], ALU.mult))
                    dve.sem_inc(made["B"], 1)
                    then(nc.vector.tensor_scalar(a[:], a[:], 1.0, p(n, "k_a"), ALU.subtract, ALU.mult))
                    then(nc.vector.scalar_tensor_tensor(a[:], a[:], 1.0, k[:], ALU.add, ALU.mult))
                    then(nc.vector.scalar_tensor_tensor(s1[:], r[:], p(n, "r_k"), a[:], ALU.mult, ALU.mult))
                    dve.sem_inc(rkr_ready, 1)
                    low_half(t + 3, 0)
                    then(nc.vector.tensor_tensor(a[:], a[:], grow[:], ALU.mult))
                    dve.sem_inc(made["K"], 1)
                    then(nc.vector.tensor_tensor(r[:].rearrange("p (c t) -> p c t", t=C),
                                                 r[:].rearrange("p (c t) -> p c t", t=C),
                                                 decay[:, :, 1:C + 1], ALU.mult))
                    dve.sem_inc(made["R"], 1)
                    low_half(t + 3, 1)
                    tile(t + 2, 1, raw[:, 1:T + 1])
                    if not first:
                        dve.wait_ge(stored["V"], after(n, 16, 0))
                    then(shift(v[:], p(n, "mu_v")))
                    dve.sem_inc(made["V"], 1)
                    dve.wait_ge(norm_done, after(n, 2, 1))
                    then(nc.vector.tensor_scalar(inv2[:], psum[:, 4, 0:2 * NB], 1e-24, None, ALU.max))
                    then(nc.vector.reciprocal(inv2[:], inv2[:]))
                    spread = grow[:].rearrange("p (b d) -> p b d", d=HD)
                    then(nc.vector.tensor_copy(spread, inv2[:].unsqueeze(2).broadcast_to([P, 2 * NB, HD])))
                    dve.sem_inc(inv_ready, 1)
                    low_half(t + 4, 0)
                    low_half(t + 4, 1)
                    tile(t + 3, 0, raw[:, 1:T + 1])
                    if not first:
                        dve.wait_ge(stored["GS"], after(n, 16, 0))
                    then(shift(g[:], p(n, "mu_g")))
                    dve.sem_inc(g_ready, 1)
                    low_half(t + 5, 0)
                    dve.wait_ge(norm_done, after(n, 2, 2))
                    then(nc.vector.scalar_tensor_tensor(k[:], k[:], p(n, "k_k"), banks(4),
                                                        ALU.mult, ALU.mult))
                    dve.sem_inc(kk_read, 1)
                    then(nc.vector.tensor_tensor(k[:].rearrange("p (c t) -> p c t", t=C),
                                                 k[:].rearrange("p (c t) -> p c t", t=C),
                                                 decay[:, :, 0:C], ALU.mult))
                    dve.sem_inc(made["KK"], 1)
                    dve.wait_ge(gate_sig, after(n, 1, 1))
                    then(nc.vector.tensor_tensor(g[:], g[:], s2[:], ALU.mult))
                    dve.wait_ge(bonus_done, after(n, 1, 1))
                    then(nc.vector.tensor_tensor(s2[:], v[:], banks(6), ALU.mult))
                    dve.sem_inc(bonus_read, 1)
                    then(nc.vector.scalar_tensor_tensor(s2[:], s2[:], p(n, "bias"), g[:], ALU.add, ALU.mult))
                    dve.sem_inc(made["BS"], 1)
                    then(nc.vector.tensor_scalar(g[:], g[:], p(n, "gain"), None, ALU.mult))
                    dve.sem_inc(made["GS"], 1)
                    low_half(t + 5, 1)
                    tile(t + 4, 1, raw[:, 1:T + 1], scale=HD ** -0.5)
                    dve.sem_inc(made["Q"], 1)

                pair_start = count[1]
                pair(0, True)
                count[0], per = count[1], None
                per = count[1] - pair_start + 1
                base = count[1]
                with dve.Fori(1, PAIRS) as n:
                    count[0], count[1] = base + (n - 1) * per, 0
                    pair(n, False)
                    assert count[1] == per, (count, per)
                count[0], count[1] = base + (PAIRS - 1) * per, 0
                dve.wait_ge(stored["Q"], 16 * PAIRS)
                tile(TILES - 1, 0, raw[:, 1:T + 1])
                dve.sem_inc(ga_ready, 1)
                dve.wait_ge(ga_sig, PAIRS)
                then(nc.vector.tensor_tensor(raw[:, 1:T + 1], raw[:, 1:T + 1], s1[:], ALU.mult))
                dve.sem_inc(made["SA"], 1)

            @block.tensor
            def _(pe):
                def project(t, parity, pace=False, reuse=True, between={}):
                    if reuse:
                        pe.wait_ge(tile_read, t - 1)
                    for half in range(2):
                        pe.wait_ge(w_ready[half], t + 1)
                        for kk in range(KH):
                            c = half * KH + kk
                            if pace:
                                pe.wait_ge(x_ready, c + 1)
                            if c in between:
                                between[c]()
                            cols = slice(kk * P, (kk + 1) * P)
                            for wt, xt in ((w_hi, x_hi), (w_hi, x_lo), (w_lo, x_hi)):
                                for h in range(2):
                                    mm = nc.tensor.matmul(
                                        psum[:, 2 * parity + h], wt[half][:, cols],
                                        xt[:, c, h * HALF:(h + 1) * HALF],
                                        start=(c == 0 and wt is w_hi and xt is x_hi),
                                        stop=(c == KC - 1 and wt is w_lo))
                        mm.then_inc(tile_done if half else w_used, 1)

                def const(name):
                    return cst[:, slice(*CONSTS[name])]

                project(0, 0, pace=True, reuse=False)
                project(1, 1, reuse=False)

                def mean_squares():
                    pe.wait_ge(x_summed, KC // 2 + 1)
                    pe.wait_ge(par_landed, 32)
                    for b_ in range(NB):
                        mm = nc.tensor.matmul(psum[:, 4, 2 * b_:2 * b_ + 2], acc[:, b_ * P:(b_ + 1) * P],
                                              const("mean")[:, 0:2], start=True, stop=True)
                    mm.then_inc(ms_done, 1)

                def inverse_rms():
                    pe.wait_ge(inv_rms, 1)
                    for b_ in range(NB):
                        mm = nc.tensor.matmul(banks(4)[:, b_ * P:(b_ + 1) * P],
                                              grow[:, b_ * P:(b_ + 1) * P], const("ident"),
                                              start=True, stop=True)
                    mm.then_inc(ms_done, 1)

                project(2, 3, reuse=False, between={8: mean_squares, 12: inverse_rms})

                def pair(n, first):
                    t = TP * n + PRO
                    pe.wait_ge(up_landed, after(n, 16, 16))

                    def lora_product(i):
                        rows = slice(i * LORA, (i + 1) * LORA)
                        for h in range(2):
                            mm = nc.tensor.matmul(psum[:, 4 + 2 * i + h], lora_up[rows, :],
                                                  lora[rows, h * HALF:(h + 1) * HALF],
                                                  start=True, stop=True)
                        mm.then_inc(lora_done, 1)

                    def second_of_first():
                        pe.wait_ge(tile_read, 3)
                        lora_product(1)

                    if first:
                        pe.wait_ge(lora_ready, 2)
                        pe.wait_ge(rms_root, 2)
                        lora_product(0)
                        project(t, 1, between={8: second_of_first})
                    else:
                        pe.wait_ge(kk_read, after(n, 1, 0))
                        pe.wait_ge(bonus_read, after(n, 1, 0))
                        lora_product(0)
                        lora_product(1)
                        project(t, 1)
                    project(t + 1, 0)
                    project(t + 2, 1)
                    pe.wait_ge(squares, after(n, 1, 1))
                    pe.wait_ge(sigma_w, after(n, 1, 1))
                    for b_ in range(NB):
                        mm = nc.tensor.matmul(psum[:, 4, 2 * b_:2 * b_ + 2], s2[:, b_ * P:(b_ + 1) * P],
                                              const("head_of"), start=True, stop=True)
                    mm.then_inc(norm_done, 1)
                    project(t + 3, 0)
                    pe.wait_ge(inv_ready, after(n, 1, 1))
                    for b_ in range(NB):
                        mm = nc.tensor.matmul(banks(4)[:, b_ * P:(b_ + 1) * P],
                                              grow[:, b_ * P:(b_ + 1) * P], const("ident"),
                                              start=True, stop=True)
                    mm.then_inc(norm_done, 1)
                    pe.wait_ge(rkr_ready, after(n, 1, 1))
                    pe.wait_ge(sigma_a, after(n, 1, 1))
                    for h in range(2):
                        mm = nc.tensor.matmul(psum[:, 6 + h], const("same_head"),
                                              s1[:, h * HALF:(h + 1) * HALF], start=True, stop=True)
                    mm.then_inc(bonus_done, 1)
                    project(t + 4, 1)
                    project(t + 5, 0)

                pair(0, True)
                with pe.Fori(1, PAIRS) as n:
                    pair(n, False)
        return semaphores


def stage_b(nc, io, scr, pc_all, cst, used=()):
    with ExitStack() as ctx:
        def sb(name, shape, dt=F32):
            return ctx.enter_context(nc.sbuf_tensor("b_" + name, shape, dt))

        def sem(name):
            return ctx.enter_context(nc.semaphore("b_" + name))

        kb = sb("kb", [P, PAIRS, 4 * C])
        qr = sb("qr", [P, PAIRS, 4 * C])
        qr_s = sb("qr_s", [P, PAIRS, 4 * C])
        vt = sb("vt", [P, PAIRS, BT])
        gs = sb("gs", [P, PAIRS, BT])
        bs = sb("bs", [P, PAIRS, BT])
        q = sb("q", [P, PAIRS, BT])
        sa = sb("sa", [P, PAIRS, BT])
        kw = sb("kw", [P, 2, 2 * BT])
        vw = sb("vw", [P, 2 * BT])
        va = sb("va", [P, 2, P])
        am2 = [sb(f"am{i}", [P, HEADS, 4 * C]) for i in range(2)]
        kbt = sb("kbt", [P, 2, PAIRS, P])
        uv = sb("uv", [P, 2, HEADS, HD])
        x16 = sb("x16", [P, HEADS, 2, P])
        x32 = sb("x32", [P, HEADS, P])
        xt = sb("xt", [P, HEADS, P])
        ym = sb("ym", [P, HEADS, P])
        sub_l = sb("sub_l", [P, SUB, SUB])
        sub_x = sb("sub_x", [P, 2, SUB, SUB])
        sub_t = sb("sub_t", [P, SUB * SUB])
        sub_ident = sb("sub_ident", [P, SUB, SUB])
        state = sb("state", [P, PAIRS, 2, HD])
        state_d = sb("state_d", [P, PAIRS, HD])
        fresh = sb("fresh", [P, PAIRS, HD])
        zs = sb("zs", [P, HEADS, HD])
        y = sb("y", [P, HEADS, HD])
        ysq = sb("ysq", [P, HEADS, HD])
        stat = sb("stat", [P, 2, HEADS])
        mix = sb("mix", [P, PAIRS, P])
        mix_a = sb("mix_a", [P, PAIRS, P])
        score = [sb(f"score{i}", [P, 4, 2 * BT]) for i in range(2)]
        pt = sb("pt", [P, 2, 4 * P])
        o = sb("o", [P, HEADS, HD])
        sinks = sb("sinks", [P, HEADS])
        neg_sinks = sb("neg_sinks", [P, HEADS])
        top = sb("top", [P, 4, HEADS])
        part = sb("part", [P, HEADS])
        eps = sb("eps", [P, 1])
        psum = ctx.enter_context(nc.psum_tensor("psum_b", [P, 8, HALF], F32))
        SCORE, TURNED_P, U, F, ZY = (0, 1), (2, 3), 4, 5, (6, 7)

        def product_banks(n, g):
            at = 2 * g if isinstance(n, int) and n < 2 else 2
            return at, at + 1

        OUT = ((U, 0), (F, 0), (U, 0), (F, 0))

        loads = ("kb", "qr", "qr_s", "vt", "gs", "bs", "q", "sa", "kw", "vw")
        landed = {x: sem(f"landed_{x}") for x in loads}
        early = [[sem(f"early{n}{g}") for g in range(4)] for n in range(2)]
        sinks_landed = sem("sinks_landed")
        l_out, l_in, x_out, x_in = sem("l_out"), sem("l_in"), sem("x_out"), sem("x_in")
        sub_done = sem("sub_done")
        pool_steps = sem("pool_steps")
        u_zero = sem("u_zero")
        decayed = sem("decayed")
        a_full, a_read = sem("a_full"), sem("a_read")
        t_full, t_read = sem("t_full"), sem("t_read")
        va_full, va_read = sem("va_full"), sem("va_read")
        s_full, s_read = sem("s_full"), sem("s_read")
        p_ready = sem("p_ready")
        pt_full, pt_read = sem("pt_full"), sem("pt_read")
        o_full, o_read = sem("o_full"), sem("o_read")
        ot_full, ot_read = sem("ot_full"), sem("ot_read")
        lev_full, lev_read = sem("lev_full"), sem("lev_read")
        x_full, x_read = sem("x_full"), sem("x_read")
        z_full, z_read = sem("z_full"), sem("z_read")
        u_full, u_read = sem("u_full"), sem("u_read")
        f_full, state_read, state_new = sem("f_full"), sem("state_read"), sem("state_new")
        y_full, y_read = sem("y_full"), sem("y_read")
        y_mean, y_centred, y_squared, y_root, y_rstd, y_norm = (
            sem("y_mean"), sem("y_centred"), sem("y_squared"), sem("y_root"), sem("y_rstd"),
            sem("y_norm"))
        yt_full, yt_read = sem("yt_full"), sem("yt_read")
        negmax = sem("negmax")
        mix_ready, mix_stored = sem("mix_ready"), sem("mix_stored")
        mixa_ready, mixa_stored = sem("mixa_ready"), sem("mixa_stored")
        steps = sem("dve_steps")
        inited = sem("inited")
        apart = sem("apart")

        def const(name):
            return cst[:, slice(*CONSTS[name])]

        def many(ap, n):
            return ap.unsqueeze(1).broadcast_to([P, n, ap.shape[1]])

        def sides(c):
            u = C if c == 0 else 0
            return slice(u, u + C), slice(C - u, 2 * C - u)

        def quad_head(i, hh):
            return 4 * i + 2 * (hh % 2) + hh // 2

        def inverses(engine, then, n):
            engine.wait_ge(l_in, after(n, 16, 16))
            if not isinstance(n, int) or n > 0:
                engine.wait_ge(x_out, after(n, 16, 0))
            engine.sem_inc(apart, 1)
            then(engine.tensor_copy(sub_x[:, 0], sub_ident[:]))
            for s in range(SUB - 1):
                below, width = SUB - 1 - s, s + 1
                left = sub_l[:, s, s + 1:].unsqueeze(2).broadcast_to([P, below, width])
                right = sub_x[:, 0, s, 0:width].unsqueeze(1).broadcast_to([P, below, width])
                t = sub_t[:, 0:below * width].rearrange("p (r c) -> p r c", c=width)
                then(engine.tensor_tensor(t, left, right, ALU.mult))
                rows = sub_x[:, 0, s + 1:, 0:width]
                then(engine.tensor_tensor(rows, rows, t, ALU.subtract))
            engine.sem_inc(apart, 1)
            then(engine.tensor_copy(sub_x[:, 1], sub_x[:, 0].rearrange("p s t -> p t s")))
            engine.sem_inc(sub_done, 1)

        KK = {0: 2 * C, 1: C}
        R = {0: 0, 1: 3 * C}
        GROUPS = 4

        ORDER = [("Y", 0), ("Y", 1), ("XT", 0), ("Y", 2), ("XT", 1), ("Y", 3), ("X", 0), ("XT", 2),
                 ("X", 1), ("XT", 3), ("X", 2), ("Y2", 0), ("X", 3), ("Y2", 1), ("XT2", 0), ("Y2", 2),
                 ("XT2", 1), ("Y2", 3), ("XT2", 2), ("XT2", 3)]
        LEVELS = [x for x in ORDER if x[0] != "X"]
        LEV = len(LEVELS)
        LEV_BANK = {"Y": (0, 1), "X": (2, 3), "XT": (6, 7), "Y2": (0, 1), "XT2": (6, 7)}

        def lev_bank(kind, g):
            return LEV_BANK[kind][g % 2]

        def lev_before(i):
            before = [j for j in range(i) if lev_bank(*LEVELS[j]) == lev_bank(*LEVELS[i])]
            return before[-1] if before else None

        with nc.Block() as block:
            def rounds(engine, round_, count=None):
                round_(0, 0, True, False)
                base = count[0] + count[1] if count else 0
                with engine.Fori(0, NB // 2 - 1) as m:
                    if count:
                        count[0], count[1] = base + m * (2 * count[2]), 0
                    round_(2 * m + 1, 1, False, False)
                    round_(2 * m + 2, 0, False, False)
                    if count:
                        assert count[1] == 2 * count[2], count
                if count:
                    count[0], count[1] = base + (NB - 2) * count[2], 0
                round_(NB - 1, 1, False, True)

            @block.sync
            def _(sp):
                def load(n, name, dst, src):
                    sp.dma_start(dst, src).then_inc(landed[name], 16)

                def need(semaphore, value):
                    sp.wait_ge(semaphore, value)
                    sp.sem_inc(apart, 1)

                def whole(name, n):
                    return scr[name][ds(n, 1)].rearrange("a p j t -> (a p) j t")

                def whole4(name, n):
                    return scr[name][ds(n, 1)].rearrange("a p j s t -> (a p) j (s t)")

                def load_recurrence(n):
                    if isinstance(n, int):
                        for g in range(GROUPS):
                            js = slice(2 * g, 2 * g + 2)
                            sp.dma_start(kb[:, js], whole4("KB", n)[:, js]).then_inc(early[n][g], 16)
                            sp.dma_start(qr[:, js], whole4("QR", n)[:, js]).then_inc(early[n][g], 16)
                    else:
                        load(n, "kb", kb[:], whole4("KB", n))
                        load(n, "qr", qr[:], whole4("QR", n))
                    load(n, "vt", vt[:], whole("V", n))

                def load_attention(n, first=False):
                    load(n, "q", q[:], whole("Q", n))
                    if first:
                        window, cols = slice(0, BT), slice(BT, 2 * BT)
                    else:
                        window, cols = ds((n - 1) * BT, 2 * BT), slice(0, 2 * BT)
                    for i in range(2):
                        load(n, "kw", kw[i * HD:(i + 1) * HD, :, cols],
                             scr["KVA"][0, :, window].rearrange("(h d) t -> d h t", h=2))
                    load(n, "vw", vw[:, cols], scr["KVA"][1, :, window])

                def blocks_out(n, parity, first=False):
                    need(a_read, after(n, 8, 8))
                    if not first:
                        need(l_in, after(n, 16, 0))
                    for i in range(P // SUB):
                        rows = slice(i * SUB, (i + 1) * SUB)
                        sp.dma_start(scr["L"][i].rearrange("h s t -> s h t"),
                                     am2[parity][rows, :, C + i * SUB:C + (i + 1) * SUB]).then_inc(l_out, 16)
                    need(l_out, after(n, 8 * 16, 8 * 16))
                    if not first:
                        need(sub_done, after(n, 1, 0))
                    sp.dma_start(sub_l[:], scr["L"].rearrange("i h s t -> (i h) s t")).then_inc(l_in, 16)

                def blocks_back(n, first=False):
                    need(sub_done, after(n, 1, 1))
                    sp.dma_start(scr["X"].rearrange("i h a s t -> (i h) a s t"), sub_x[:]).then_inc(x_out, 16)
                    need(x_out, after(n, 16, 16))
                    if first:
                        need(inited, 1)
                    else:
                        need(lev_full, after(n, LEV, 0))
                        need(lev_read, after(n, LEV, 0))
                    for i in range(P // SUB):
                        rows = slice(i * SUB, (i + 1) * SUB)
                        sp.dma_start(x16[rows, :, :, i * SUB:(i + 1) * SUB].rearrange("s h a t -> s (h a) t"),
                                     scr["X"][i].rearrange("h a s t -> s (h a) t")).then_inc(x_in, 16)

                def round_(n, parity, first, last):
                    if not first and not last:
                        need(t_full, after(n, 8, 8))
                        load_recurrence(n + 1)
                    if not first:
                        need(mix_ready, after(n, 1, 0))
                    load(n, "gs", gs[:], whole("GS", n))
                    load(n, "bs", bs[:], whole("BS", n))
                    if not last:
                        if not first:
                            blocks_out(n + 1, 1 - parity)
                        need(z_full, after(n, 4, 4))
                        load(n + 1, "qr_s", qr_s[:], whole4("QR", n + 1))
                        blocks_back(n + 1)
                        need(s_full, after(n, 8, 8))
                        need(va_full, after(n, 1, 1))
                        load_attention(n + 1)
                        need(ot_read, after(n, 2, 2))
                        load(n + 1, "sa", sa[:], whole("SA", n + 1))

                load_recurrence(0)
                sp.dma_start(sinks[:], io["sinks"]).then_inc(sinks_landed, 16)
                load_attention(0, True)
                load(0, "qr_s", qr_s[:], whole4("QR", 0))
                load(0, "sa", sa[:], whole("SA", 0))
                blocks_out(0, 0, True)
                need(t_full, 8)
                load_recurrence(1)
                blocks_back(0, True)
                blocks_out(1, 1)
                rounds(sp, round_)

            @block.gpsimd
            def _(pool):
                count = [0, 0, POOL_STEPS]

                def then(ins):
                    ins.then_inc(pool_steps, 1)
                    count[1] += 1
                    pool.wait_ge(pool_steps, count[0] + count[1])

                def head_norm(n):
                    spread = [P, HEADS, HD]
                    pool.wait_ge(y_mean, after(n, 1, 0))
                    then(nc.gpsimd.tensor_tensor(y[:], y[:], stat[:, 0].unsqueeze(2).broadcast_to(spread), ALU.add))
                    pool.sem_inc(y_centred, 1)
                    pool.wait_ge(y_rstd, after(n, 1, 0))
                    then(nc.gpsimd.tensor_tensor(y[:], y[:], stat[:, 1].unsqueeze(2).broadcast_to(spread), ALU.mult))
                    pool.sem_inc(y_norm, 1)

                def round_(n, parity, first, last):
                    if not first:
                        pool.wait_ge(f_full, after(n, 2, 0))
                        pool.wait_ge(y_full, after(n, 4, 0))
                        pool.sem_inc(apart, 1)
                    for c in range(2):
                        us, _ = sides(c)
                        ins = nc.gpsimd.memset(uv[us, c], 0.0)
                    then(ins)
                    pool.sem_inc(u_zero, 1)
                    for c in range(2):
                        if c == 0 and not first:
                            pool.wait_ge(state_new, after(n, 2, 0))
                        if c == 1:
                            if first:
                                inverses(pool, then, 1)
                            else:
                                head_norm(n)
                            pool.wait_ge(state_new, after(n, 2, 1))
                        pc = pc_all[:, :, ds(2 * n + c, 1)]
                        for i in range(2):
                            half = slice(i * HD, (i + 1) * HD)
                            then(nc.gpsimd.tensor_tensor(state_d[half], state[half, :, i],
                                                         pc[half].broadcast_to([HD, PAIRS, HD]), ALU.mult))
                        pool.sem_inc(decayed, 1)
                    if not first and not last:
                        inverses(pool, then, n + 1)

                then(nc.gpsimd.memset(sub_ident[:], 0.0))
                then(nc.gpsimd.affine_select(sub_ident[:], sub_ident[:], pattern=[[1, SUB], [-1, SUB]],
                                             compare_op=ALU.not_equal, fill=1.0, base=0,
                                             channel_multiplier=0))
                then(nc.gpsimd.memset(sub_x[:], 0.0))
                then(nc.gpsimd.memset(state[:], 0.0))
                then(nc.gpsimd.memset(x16[:], 0.0))
                pool.sem_inc(inited, 1)
                rounds(pool, round_, count)
                head_norm(NB)
                if used:
                    nc.clear_and_free_semaphores(used)

            @block.scalar
            def _(act):
                def copy(dst, src, scale=1.0):
                    return nc.scalar.activation(dst, src, ACT.Copy, scale=scale)

                def exponentials(n, first, i):
                    lo = BT if first else 0
                    act.wait_ge(negmax, after(n, 4, i + 1))
                    for hh in range(4):
                        at = 4 * i + hh
                        s = score[i % 2][:, hh, lo:]
                        nc.scalar.activation(s, s, ACT.Exp, bias=top[:, 1, at:at + 1],
                                             accum_out=top[:, 2, at:at + 1])
                    heads = slice(4 * i, 4 * i + 4)
                    nc.scalar.activation(top[:, 3, heads], part[:, heads], ACT.Exp).then_inc(p_ready, 1)

                def turned_p(n, first, i):
                    w = 2 * P if first else 4 * P
                    for m in range(2):
                        act.wait_ge(pt_full, after(n, 8, 2 * i + m + 1))
                        copy(pt[:, m, 0:w], psum[:, TURNED_P[m], 0:w]).then_inc(pt_read, 1)

                def mix_out(n, group):
                    return scr["MIX"][ds(n, 1), :, group * PAIRS:(group + 1) * PAIRS].rearrange(
                        "b p k t -> (b p) k t")

                def turned(n, j):
                    act.wait_ge(t_full, after(n, 8, j + 1))
                    bank = psum[:, 4 + j % 2]
                    copy(kbt[:, :, j], bank[:, 0:2 * P].rearrange("p (c k) -> p c k", c=2))
                    for c in range(2):
                        _, vs = sides(c)
                        ins = copy(uv[vs, c, 2 * j:2 * j + 2].rearrange("p h d -> p (h d)"),
                                   bank[vs, 2 * P:3 * P])
                    ins.then_inc(t_read, 1)

                def block_turned_back(n, g):
                    act.wait_ge(x_full, after(n, 4, g + 1))
                    copy(x32[:, 4 * g:4 * g + 4], psum[:, lev_bank("X", g)].rearrange("p (h t) -> p h t", t=P)
                         ).then_inc(x_read, 1)

                def negative_z(n, c):
                    us, _ = sides(c)
                    for i in range(2):
                        act.wait_ge(z_full, after(n, 4, 2 * c + i + 1))
                        z = psum[us, ZY[i]].rearrange("p (h d) -> p h d", d=HD)
                        copy(zs[us, 8 * i:8 * i + 8], z, scale=-1.0).then_inc(z_read, 1)

                def rows_out(n, c):
                    _, vs = sides(c)
                    for i in range(2):
                        act.wait_ge(y_full, after(n, 4, 2 * c + i + 1))
                        src = psum[vs, ZY[i]].rearrange("p (h d) -> p h d", d=HD)
                        copy(y[vs, 8 * i:8 * i + 8], src).then_inc(y_read, 1)

                def squares(n):
                    act.wait_ge(y_centred, after(n, 1, 0))
                    for h in range(HEADS):
                        ins = nc.scalar.activation(ysq[:, h], y[:, h], ACT.Square,
                                                   accum_out=stat[:, 1, h:h + 1])
                    ins.then_inc(y_squared, 1)

                def roots(n):
                    act.wait_ge(y_squared, after(n, 1, 0))
                    nc.scalar.activation(stat[:, 1], stat[:, 1], ACT.Sqrt, bias=eps[:, 0:1],
                                         scale=1.0 / HD).then_inc(y_root, 1)

                def round_(n, parity, first, last):
                    if not first:
                        act.wait_ge(u_zero, after(n, 1, 1))
                    for i, (kind, g) in enumerate(ORDER):
                        if kind == "X":
                            block_turned_back(n, g)
                        if i < PAIRS and not first:
                            turned(n, i)
                        if i == 9 and not first:
                            squares(n)
                    if not first:
                        roots(n)
                    act.wait_ge(va_full, after(n, 1, 1))
                    if first:
                        copy(va[:, 1], psum[:, TURNED_P[0], P:2 * P]).then_inc(va_read, 1)
                    else:
                        copy(va[:].rearrange("p w d -> p (w d)"), psum[:, TURNED_P[0], 0:2 * P]).then_inc(va_read, 1)
                    exponentials(n, first, 0)
                    negative_z(n, 0)
                    rows_out(n, 0)
                    turned_p(n, first, 0)
                    exponentials(n, first, 1)
                    negative_z(n, 1)
                    turned_p(n, first, 1)
                    exponentials(n, first, 2)
                    turned_p(n, first, 2)
                    exponentials(n, first, 3)
                    rows_out(n, 1)
                    turned_p(n, first, 3)
                    if not first:
                        act.wait_ge(mix_ready, after(n, 1, 0))
                        act.dma_start(mix_out(n - 1, 0), mix[:]).then_inc(mix_stored, 16)
                    act.wait_ge(mixa_ready, after(n, 1, 1))
                    act.dma_start(mix_out(n, 1), mix_a[:]).then_inc(mixa_stored, 16)

                act.wait_ge(inited, 2)
                act.wait_ge(u_zero, 1)
                for j in range(PAIRS):
                    turned(0, j)
                rounds(act, round_)
                squares(NB)
                roots(NB)
                act.wait_ge(mix_ready, NB)
                act.dma_start(mix_out(NB - 1, 0), mix[:]).then_inc(mix_stored, 16)
                act.wait_ge(mix_stored, 16 * (NB + 1))
                act.wait_ge(mixa_stored, 16 * NB)

            @block.vector
            def _(dve):
                count = [0, 0, DVE_STEPS]

                def then(ins):
                    ins.then_inc(steps, 1)
                    count[1] += 1
                    dve.wait_ge(steps, count[0] + count[1])

                def mean(n):
                    dve.wait_ge(y_read, after(n, 4, 0))
                    then(nc.vector.tensor_reduce(stat[:, 0], y[:], AX, ALU.add))
                    then(nc.vector.tensor_scalar(stat[:, 0], stat[:, 0], -1.0 / HD, None, ALU.mult))
                    dve.sem_inc(y_mean, 1)

                def deviation(n):
                    dve.wait_ge(y_root, after(n, 1, 0))
                    then(nc.vector.reciprocal(stat[:, 1], stat[:, 1]))
                    dve.sem_inc(y_rstd, 1)

                def gated(n):
                    dve.wait_ge(landed["gs"], after(n, 16, 0))
                    dve.wait_ge(landed["bs"], after(n, 16, 0))
                    dve.wait_ge(mix_stored, after(n, 16, 0))
                    for i in range(2):
                        dve.wait_ge(yt_full, after(n - 1, 2, i + 1))
                        js = slice(4 * i, 4 * i + 4)
                        then(nc.vector.tensor_tensor(mix[:, js], psum[:, 4 + i].rearrange("p (j t) -> p j t", t=BT),
                                                     gs[:, js], ALU.mult))
                        dve.sem_inc(yt_read, 1)
                    then(nc.vector.tensor_tensor(mix[:], mix[:], bs[:], ALU.add))
                    dve.sem_inc(mix_ready, 1)

                def softmax_scores(n, first, i):
                    lo = BT if first else 0
                    w = 2 * BT - lo
                    for par_ in range(2):
                        dve.wait_ge(s_full, after(n, 8, 2 * i + par_ + 1))
                        for jj in range(2):
                            hh = 2 * par_ + jj
                            slope = 2.0 ** (-8.0 * (quad_head(i, hh) + 1) / HEADS)
                            src = psum[:, SCORE[par_], jj * w:(jj + 1) * w]
                            ins = nc.vector.scalar_tensor_tensor(
                                score[i % 2][:, hh, lo:], const("dist")[:, lo:], -slope, src,
                                ALU.mult, ALU.add)
                    then(ins)
                    dve.sem_inc(s_read, 1)
                    heads = slice(4 * i, 4 * i + 4)
                    then(nc.vector.tensor_reduce(top[:, 0, heads], score[i % 2][:, :, lo:], AX, ALU.max))
                    then(nc.vector.scalar_tensor_tensor(top[:, 1, heads], top[:, 0, heads], -1.0,
                                                        neg_sinks[:, heads], ALU.mult, ALU.min))
                    then(nc.vector.tensor_tensor(part[:, heads], top[:, 1, heads], neg_sinks[:, heads],
                                                 ALU.subtract))
                    dve.sem_inc(negmax, 1)

                def outputs(n, i):
                    heads = slice(4 * i, 4 * i + 4)
                    dve.wait_ge(p_ready, after(n, 4, i + 1))
                    then(nc.vector.tensor_tensor(part[:, heads], top[:, 2, heads], top[:, 3, heads], ALU.add))
                    then(nc.vector.reciprocal(part[:, heads], part[:, heads]))
                    dve.wait_ge(o_full, after(n, 4, i + 1))
                    bank, at = OUT[i]
                    then(nc.vector.tensor_tensor(
                        o[:, heads].rearrange("p (b a) d -> p a b d", a=2),
                        psum[:, bank, at:at + 4 * HD].rearrange("p (a b d) -> p a b d", a=2, b=2),
                        part[:, heads].rearrange("p (a b) -> p a b", a=2).unsqueeze(3)
                        .broadcast_to([P, 2, 2, HD]), ALU.mult))
                    dve.sem_inc(o_read, 1)

                def masked(n, parity, g):
                    for par_ in range(2):
                        dve.wait_ge(a_full, after(n, 8, 2 * g + par_ + 1))
                        then(nc.vector.tensor_tensor(
                            am2[parity][:, 4 * g + par_:4 * g + 4:2],
                            psum[:, product_banks(n, g)[par_]].rearrange("p (h t) -> p h t", h=2),
                            many(const("amask"), 2), ALU.mult))
                        dve.sem_inc(a_read, 1)

                def level(n, i):
                    kind, g = LEVELS[i]
                    hs = slice(4 * g, 4 * g + 4)
                    dve.wait_ge(lev_full, after(n, LEV, i + 1))
                    src = psum[:, lev_bank(kind, g)].rearrange("p (h t) -> p h t", t=P)
                    if kind in ("Y", "Y2"):
                        mask = const("m16" if kind == "Y" else "m32")
                        ins = nc.vector.tensor_tensor(ym[:, hs], src, many(mask, 4), ALU.mult)
                    else:
                        old = x16[:, hs, 1] if kind == "XT" else xt[:, hs]
                        ins = nc.vector.tensor_tensor(xt[:, hs], old, src, ALU.subtract)
                    then(ins)
                    dve.sem_inc(lev_read, 1)

                def u_rows(n, c):
                    us, vs = sides(c)
                    for i in range(2):
                        dve.wait_ge(u_full, after(n, 4, 2 * c + i + 1))
                        then(nc.vector.tensor_copy(uv[us, c, 8 * i:8 * i + 8].rearrange("p h d -> p (h d)"),
                                                   psum[(us, vs)[i], U]))
                        dve.sem_inc(u_read, 1)

                def new_state(n, c):
                    pc = pc_all[:, :, ds(2 * n + c, 1)]
                    dve.wait_ge(f_full, after(n, 2, c + 1))
                    then(nc.vector.tensor_tensor(fresh[:], psum[:, F].rearrange("p (j d) -> p j d", d=HD),
                                                 pc.broadcast_to([P, PAIRS, HD]), ALU.mult))
                    dve.sem_inc(state_read, 1)
                    dve.wait_ge(decayed, after(n, 2, c + 1))
                    for i in range(2):
                        half = slice(i * HD, (i + 1) * HD)
                        ins = nc.vector.tensor_tensor(state[half, :, i], state_d[half], fresh[half], ALU.add)
                    then(ins)
                    dve.sem_inc(state_new, 1)

                def round_(n, parity, first, last):
                    for i in range(LEV):
                        level(n, i)
                        if not first and i == 1:
                            mean(n)
                        if not first and i == 15:
                            deviation(n)
                    softmax_scores(n, first, 0)
                    ahead = not first and not last
                    if ahead:
                        dve.wait_ge(l_out, after(n, 8 * 16, 0))
                        masked(n + 1, 1 - parity, 0)
                    if not first:
                        gated(n)
                    if ahead:
                        masked(n + 1, 1 - parity, 1)
                    u_rows(n, 0)
                    if ahead:
                        masked(n + 1, 1 - parity, 2)
                    new_state(n, 0)
                    if ahead:
                        masked(n + 1, 1 - parity, 3)
                    softmax_scores(n, first, 1)
                    outputs(n, 0)
                    softmax_scores(n, first, 2)
                    u_rows(n, 1)
                    outputs(n, 1)
                    softmax_scores(n, first, 3)
                    new_state(n, 1)
                    outputs(n, 2)
                    outputs(n, 3)
                    dve.wait_ge(landed["sa"], after(n, 16, 16))
                    if not first:
                        dve.wait_ge(mixa_stored, after(n, 16, 0))
                    for i in range(2):
                        js = slice(4 * i, 4 * i + 4)
                        dve.wait_ge(ot_full, after(n, 2, i + 1))
                        then(nc.vector.tensor_tensor(mix_a[:, js], psum[:, ZY[i]].rearrange("p (j t) -> p j t", t=BT),
                                                     sa[:, js], ALU.mult))
                        dve.sem_inc(ot_read, 1)
                    dve.sem_inc(mixa_ready, 1)

                then(nc.vector.memset(eps[:], LNX_EPS))
                dve.sem_inc(inited, 1)
                dve.sem_inc(mix_stored, 16)
                dve.wait_ge(sinks_landed, 16)
                then(nc.vector.tensor_scalar(neg_sinks[:], sinks[:], -1.0, None, ALU.mult))
                for g in range(GROUPS):
                    masked(0, 0, g)
                dve.wait_ge(inited, 2)
                inverses(dve, then, 0)
                for g in range(GROUPS):
                    masked(1, 1, g)
                rounds(dve, round_, count)
                mean(NB)
                deviation(NB)
                gated(NB)

            @block.tensor
            def _(pe):
                ident = const("ident")

                def turn(dst, src):
                    return nc.tensor.transpose(dst, src, ident)

                def turn_rows(n, j):
                    if j >= 2:
                        pe.wait_ge(t_read, after(n, 8, j - 1))
                    bank = psum[:, 4 + j % 2]
                    for c in range(2):
                        turn(bank[:, c * P:(c + 1) * P], kb[:, j, c * P:(c + 1) * P])
                    turn(bank[:, 2 * P:3 * P], vt[:, j]).then_inc(t_full, 1)

                def turn_y(n):
                    pe.wait_ge(y_norm, after(n, 1, 0))
                    for i in range(2):
                        for jj in range(4):
                            j = 4 * i + jj
                            mm = turn(psum[:, 4 + i, jj * P:(jj + 1) * P],
                                      y[:, 2 * j:2 * j + 2].rearrange("p h d -> p (h d)"))
                        mm.then_inc(yt_full, 1)

                def scores(n, first, i):
                    lo = BT if first else 0
                    w = 2 * BT - lo
                    if i >= 1:
                        pe.wait_ge(s_read, after(n, 4, i))
                    for par_ in range(2):
                        rows = slice(par_ * HD, (par_ + 1) * HD)
                        for jj in range(2):
                            j = 2 * i + jj
                            mm = nc.tensor.matmul(psum[:, SCORE[par_], jj * w:(jj + 1) * w], q[rows, j],
                                                  kw[rows, j // 4, lo:], start=True, stop=True)
                        mm.then_inc(s_full, 1)

                def turn_p(n, first, i, m):
                    pe.wait_ge(p_ready, after(n, 4, i + 1))
                    if i >= 1:
                        pe.wait_ge(pt_read, after(n, 8, 2 * i + m - 1))
                    at = 0
                    for hh in (2 * m, 2 * m + 1):
                        for wnd in ((1,) if first else (0, 1)):
                            mm = turn(psum[:, TURNED_P[m], at:at + P], score[i % 2][:, hh, wnd * BT:(wnd + 1) * BT])
                            at += P
                    mm.then_inc(pt_full, 1)

                def values(n, first, i):
                    kv = i // 2
                    bank, start = OUT[i]
                    wnds = (1,) if first else (0, 1)
                    for hh in range(4):
                        if hh % 2 == 0:
                            pe.wait_ge(pt_read, after(n, 8, 2 * i + hh // 2 + 1))
                        for x, wnd in enumerate(wnds):
                            at = (hh % 2) * len(wnds) * P + x * P
                            out = start + hh * HD
                            mm = nc.tensor.matmul(psum[:, bank, out:out + HD],
                                                  pt[:, hh // 2, at:at + P],
                                                  va[:, wnd, kv * HD:(kv + 1) * HD],
                                                  start=(x == 0), stop=(x == len(wnds) - 1))
                    mm.then_inc(o_full, 1)

                def products(n, g):
                    if isinstance(n, int):
                        pe.wait_ge(early[n][g], 32)
                    elif g == 0:
                        pe.wait_ge(landed["kb"], after(n - 1, 16, 0))
                        pe.wait_ge(landed["qr"], after(n - 1, 16, 0))
                    else:
                        pe.wait_ge(a_read, after(n, 8, 2 * g))
                    mm = [None, None]
                    for jj in range(2):
                        j = 2 * g + jj
                        for c in range(2):
                            for par_ in range(2):
                                rows = slice(par_ * HD, (par_ + 1) * HD)
                                full = psum[:, product_banks(n, g)[par_], jj * 4 * C:(jj + 1) * 4 * C]
                                dst = full.rearrange("p (s t) -> p s t", t=C)[:, c::2]
                                mm[par_] = nc.tensor.matmul(dst, kb[rows, j, c * P:(c + 1) * P],
                                                            qr[rows, j, c * P:(c + 1) * P],
                                                            start=True, stop=True)
                    for par_ in range(2):
                        mm[par_].then_inc(a_full, 1)

                def inversion(n, am, first):
                    done = {}
                    at = 0
                    for i, (kind, g) in enumerate(ORDER):
                        if kind == "X":
                            pe.wait_ge(lev_read, after(n, LEV, done[("XT", g)] + 1))
                            if g >= 2:
                                pe.wait_ge(x_read, after(n, 4, g - 1))
                        else:
                            needs = {"Y": [], "XT": [("Y", g)], "Y2": [("XT", g)], "XT2": [("Y2", g)]}[kind]
                            needs = [done[x] for x in needs] + [lev_before(at)]
                            needs = [x for x in needs if x is not None]
                            if needs:
                                pe.wait_ge(lev_read, after(n, LEV, max(needs) + 1))
                            if kind == "Y2":
                                pe.wait_ge(x_read, after(n, 4, g + 1))
                            if kind == "XT" and g == 0 and not first:
                                pe.wait_ge(ot_read, after(n, 2, 0))
                            done[(kind, g)] = at
                            at += 1
                        for hh in range(4):
                            h = 4 * g + hh
                            dst = psum[:, lev_bank(kind, g), hh * P:(hh + 1) * P]
                            if kind == "X":
                                mm = turn(dst, xt[:, h])
                            else:
                                lhs, rhs = {
                                    "Y": (am[:, h, C:3 * C], x16[:, h, 0]),
                                    "XT": (ym[:, h], x16[:, h, 1]),
                                    "Y2": (am[:, h, C:3 * C], x32[:, h]),
                                    "XT2": (ym[:, h], xt[:, h]),
                                }[kind]
                                mm = nc.tensor.matmul(dst, lhs, rhs, start=True, stop=True)
                        mm.then_inc(x_full if kind == "X" else lev_full, 1)
                        if i < PAIRS and not first:
                            turn_rows(n, i)

                def z(n, c, am):
                    us, _ = sides(c)
                    cols = slice(c * P, (c + 1) * P)
                    if c == 1:
                        pe.wait_ge(state_new, after(n, 2, 1))
                    for i in range(2):
                        if c == 1:
                            pe.wait_ge(y_read, after(n, 4, i + 1))
                        for jj in range(4):
                            j = 4 * i + jj
                            nc.tensor.matmul(psum[:, ZY[i], jj * P:(jj + 1) * P], qr_s[:, j, cols],
                                             state[:, j].rearrange("p h d -> p (h d)"),
                                             start=(jj == 0), stop=False, skip_group_check=True)
                        for hh in range(8):
                            h = 8 * i + hh
                            mm = nc.tensor.matmul(psum[us, ZY[i], hh * HD:(hh + 1) * HD],
                                                  am[:, h, KK[c]:KK[c] + C], uv[:, c, h],
                                                  start=False, stop=False, skip_group_check=True)
                        mm.then_inc(z_full, 1)

                def u(n, c):
                    us, vs = sides(c)
                    for i in range(2):
                        pe.wait_ge(z_read, after(n, 4, 2 * c + i + 1))
                        if c == 1:
                            pe.wait_ge(u_read, after(n, 4, 2))
                            pe.wait_ge(o_read, after(n, 4, 1))
                        pe.sem_inc(apart, 1)
                        for hh in range(8):
                            h = 8 * i + hh
                            mm = nc.tensor.matmul(psum[(us, vs)[i], U, hh * HD:(hh + 1) * HD], xt[us, h, us],
                                                  zs[us, h], start=True, stop=True, skip_group_check=True)
                        mm.then_inc(u_full, 1)

                def f(n, c):
                    if c == 1:
                        pe.wait_ge(o_read, after(n, 4, 2))
                    for i in range(2):
                        pe.wait_ge(u_read, after(n, 4, 2 * c + i + 1))
                        for hh in range(8):
                            h = 8 * i + hh
                            half = slice((h % 2) * HD, (h % 2 + 1) * HD)
                            mm = nc.tensor.matmul(psum[half, F, (h // 2) * HD:(h // 2 + 1) * HD],
                                                  kbt[:, c, h // 2, half], uv[:, c, h],
                                                  start=True, stop=True, skip_group_check=True)
                    mm.then_inc(f_full, 1)

                def rows(n, c, am):
                    _, vs = sides(c)
                    for i in range(2):
                        for hh in range(8):
                            h = 8 * i + hh
                            mm = nc.tensor.matmul(psum[vs, ZY[i], hh * HD:(hh + 1) * HD],
                                                  am[:, h, R[c]:R[c] + C], uv[:, c, h],
                                                  start=False, stop=(hh == 7), skip_group_check=True)
                        mm.then_inc(y_full, 1)

                def round_(n, parity, first, last):
                    am = am2[parity]
                    ahead = not first and not last
                    pe.wait_ge(landed["vt"], after(n, 16, 16))
                    pe.wait_ge(x_in, after(n, 8 * 16, 8 * 16))
                    if first:
                        pe.wait_ge(a_read, 16)
                    else:
                        pe.wait_ge(s_read, after(n, 4, 0))
                        pe.wait_ge(o_read, after(n, 4, 0))
                        pe.wait_ge(pt_read, after(n, 8, 0))
                        pe.wait_ge(y_read, after(n, 4, 0))
                        pe.wait_ge(u_read, after(n, 4, 0))
                        pe.wait_ge(state_read, after(n, 2, 0))
                    inversion(n, am, first)
                    pe.wait_ge(landed["q"], after(n, 16, 16))
                    pe.wait_ge(landed["kw"], after(n, 32, 32))
                    pe.wait_ge(lev_read, after(n, LEV, LEV))
                    scores(n, first, 0)
                    pe.wait_ge(landed["vw"], after(n, 16, 16))
                    if not first:
                        turn(psum[:, TURNED_P[0], 0:P], vw[:, 0:BT])
                    turn(psum[:, TURNED_P[0], P:2 * P], vw[:, BT:]).then_inc(va_full, 1)
                    pe.wait_ge(t_read, after(n, 8, 8))
                    if not first:
                        turn_y(n)
                    pe.wait_ge(va_read, after(n, 1, 1))
                    if ahead:
                        products(n + 1, 0)
                    pe.wait_ge(landed["qr_s"], after(n, 16, 16))
                    if first:
                        pe.wait_ge(inited, 2)
                    else:
                        pe.wait_ge(state_new, after(n, 2, 0))
                    z(n, 0, am)
                    if ahead:
                        products(n + 1, 1)
                    if not first:
                        pe.wait_ge(yt_read, after(n, 2, 0))
                    u(n, 0)
                    if ahead:
                        products(n + 1, 2)
                    f(n, 0)
                    if ahead:
                        products(n + 1, 3)
                    scores(n, first, 1)
                    rows(n, 0, am)
                    if ahead:
                        pe.wait_ge(a_read, after(n + 1, 8, 8))
                    turn_p(n, first, 0, 0)
                    turn_p(n, first, 0, 1)
                    z(n, 1, am)
                    values(n, first, 0)
                    scores(n, first, 2)
                    turn_p(n, first, 1, 0)
                    turn_p(n, first, 1, 1)
                    u(n, 1)
                    pe.wait_ge(state_read, after(n, 2, 1))
                    values(n, first, 1)
                    scores(n, first, 3)
                    turn_p(n, first, 2, 0)
                    turn_p(n, first, 2, 1)
                    f(n, 1)
                    values(n, first, 2)
                    rows(n, 1, am)
                    turn_p(n, first, 3, 0)
                    turn_p(n, first, 3, 1)
                    pe.wait_ge(state_read, after(n, 2, 2))
                    values(n, first, 3)
                    for i in range(2):
                        pe.wait_ge(y_read, after(n, 4, i + 3))
                        pe.wait_ge(o_read, after(n, 4, 2 * i + 2))
                        for jj in range(4):
                            j = 4 * i + jj
                            mm = turn(psum[:, ZY[i], jj * P:(jj + 1) * P],
                                      o[:, 2 * j:2 * j + 2].rearrange("p h d -> p (h d)"))
                        mm.then_inc(ot_full, 1)

                pe.wait_ge(inited, 2)
                for g in range(GROUPS):
                    products(0, g)
                pe.wait_ge(landed["vt"], 16)
                pe.wait_ge(a_read, 8)
                for j in range(PAIRS):
                    turn_rows(0, j)
                pe.wait_ge(t_read, 8)
                for g in range(GROUPS):
                    products(1, g)
                rounds(pe, round_)
                pe.wait_ge(u_read, 4 * NB)
                pe.wait_ge(state_read, 2 * NB)
                turn_y(NB)


def stage_c(nc, io, scr, cst):
    with ExitStack() as ctx:
        def sb(name, shape, dt=F32):
            return ctx.enter_context(nc.sbuf_tensor("c_" + name, shape, dt))

        def sem(name):
            return ctx.enter_context(nc.semaphore("c_" + name))

        m_in = sb("m_in", [P, HALF])
        m_hi = sb("m_hi", [P, 2, KC, HALF], F32R)
        m_lo = sb("m_lo", [P, 2, KC, HALF], F32R)
        w_raw = [sb(f"w_raw{i}", [P, KH * P]) for i in range(2)]
        w_hi = [sb(f"w_hi{i}", [P, KH * P], F32R) for i in range(2)]
        w_lo = [sb(f"w_lo{i}", [P, KH * P], F32R) for i in range(2)]
        x_in = sb("x_in", [P, HALF])
        xn = sb("xn", [P, KC, HALF])
        sq = sb("sq", [P, HALF])
        acc = sb("acc", [P, HALF])
        rms = sb("rms", [P, HALF])
        gain = sb("gain", [P, KC])
        eps = sb("eps", [P, 1])
        psum = ctx.enter_context(nc.psum_tensor("psum_c", [P, 8, HALF], F32))

        gain_landed = sem("gain_landed")
        m_landed = [sem(f"m_landed{i}") for i in range(KC // 2)]
        m2_landed = sem("m2_landed")
        m_high, m_ready = sem("m_high"), sem("m_ready")
        w_landed = [sem(f"w_landed{i}") for i in range(2)]
        w_high = [sem(f"w_high{i}") for i in range(2)]
        w_ready = [sem(f"w_ready{i}") for i in range(2)]
        w_used = sem("w_used")
        x_landed = sem("x_landed")
        tile_done, tile_read = sem("tile_done"), sem("tile_read")
        squared, summed, gained = sem("squared"), sem("summed"), sem("gained")
        mean_done, rooted, rms_ready = sem("mean_done"), sem("rooted"), sem("rms_ready")
        scaled_pool, scaled_dve = sem("scaled_pool"), sem("scaled_dve")
        out_stored = [sem(f"out_stored{i}") for i in range(4)]
        inited = sem("inited")

        BY_DVE = (4, 10)
        GROUP = 2
        LAST = 2 * KC - 1

        with nc.Block() as block:
            @block.sync
            def _(sp):
                def load_half(s, t, half, first=False):
                    if not first:
                        sp.wait_ge(w_ready[half], s)
                    sp.dma_start(w_raw[half][:], io["w_out"][ds(t, 1), half].rearrange("a p n -> (a p) n")
                                 ).then_inc(w_landed[half], 16)

                def load_x(s, t, h, first=False):
                    if not first:
                        sp.wait_ge(tile_read, s)
                    sp.dma_start(x_in[:], io["x_t"][ds(t, 1), :, h * HALF:(h + 1) * HALF]
                                 .rearrange("a p n -> (a p) n")).then_inc(x_landed, 16)

                def load_mix(i):
                    for k in (2 * i, 2 * i + 1):
                        src = scr["MIX"][0:NB // 2, :, k].rearrange("b p t -> p b t")
                        sp.dma_start(xn[:, k].rearrange("p (b t) -> p b t", t=BT), src
                                     ).then_inc(m_landed[i], 16)

                sp.dma_start(gain[:], io["final_gain"]).then_inc(gain_landed, 16)
                def load_mix_2(k):
                    if not isinstance(k, int) or k > 0:
                        sp.wait_ge(m_ready, KC // 2 + k)
                    src = scr["MIX"][NB // 2:, :, ds(k, 1)].rearrange("b p c t -> p (b c) t")
                    sp.dma_start(m_in[:].rearrange("p (b t) -> p b t", t=BT), src).then_inc(m2_landed, 16)

                load_half(0, 0, 0, True)
                for i in range(3):
                    load_mix(i)
                load_half(0, 0, 1, True)
                for i in range(3, KC // 2):
                    load_mix(i)
                load_x(0, 0, 0, True)
                for h in range(2):
                    if h == 1:
                        for half in range(2):
                            load_half(KC, 0, half)
                        load_x(KC, 0, 1)
                        first = 1
                    else:
                        for half in range(2):
                            load_half(1, 1, half)
                        load_mix_2(0)
                        load_mix_2(1)
                        load_x(1, 1, 0)
                        first = 2
                    with sp.Fori(first, KC) as t:
                        for half in range(2):
                            load_half(h * KC + t, t, half)
                        if h == 0:
                            load_mix_2(t)
                        load_x(h * KC + t, t, h)
                for t in range(0, KC, GROUP):
                    if t < BY_DVE[1]:
                        sp.wait_ge(scaled_dve, BY_DVE[0] + t // GROUP + 1)
                    else:
                        sp.wait_ge(scaled_pool, (KC - BY_DVE[0] + t - BY_DVE[1]) // GROUP + 1)
                    sp.dma_start(io["out"][t:t + GROUP, :, HALF:].rearrange("k p n -> p k n"),
                                 xn[:, t:t + GROUP]).then_inc(out_stored[3], 16)
                sp.wait_ge(out_stored[3], 16 * KC // GROUP)

            @block.scalar
            def _(act):
                def high_half(s, half, first=False):
                    act.wait_ge(w_landed[half], 16 * (s + 1))
                    if not first:
                        act.wait_ge(tile_done if half else w_used, s)
                    nc.scalar.activation(w_hi[half][:], w_raw[half][:], ACT.Copy).then_inc(w_high[half], 1)

                def mix_high(i):
                    act.wait_ge(m_landed[i], 32)
                    two = slice(2 * i, 2 * i + 2)
                    nc.scalar.activation(m_hi[:, 0, two], xn[:, two], ACT.Copy).then_inc(m_high, 1)

                def mix_high_2(k):
                    act.wait_ge(m2_landed, 16 * (k + 1))
                    nc.scalar.activation(m_hi[:, 1, ds(k, 1)].rearrange("p a t -> p (a t)"), m_in[:],
                                         ACT.Copy).then_inc(m_high, 1)

                def square(s, t, first=False):
                    act.wait_ge(tile_read, s + 1)
                    if not first:
                        act.wait_ge(summed, s)
                    tile = xn[:, ds(t, 1)].rearrange("p a t -> p (a t)")
                    nc.scalar.activation(sq[:], tile, ACT.Square).then_inc(squared, 1)
                    act.wait_ge(squared, s + 1)
                    nc.scalar.activation(tile, tile, ACT.Copy, scale=gain[:, ds(t, 1)]).then_inc(gained, 1)

                def root(h):
                    act.wait_ge(mean_done, h + 1)
                    nc.scalar.activation(rms[:], psum[:, 4], ACT.Sqrt, bias=eps[:, 0:1]).then_inc(rooted, 1)

                act.wait_ge(inited, 1)
                act.wait_ge(gain_landed, 16)
                high_half(0, 0, True)
                for i in range(KC // 2):
                    if i == 3:
                        high_half(0, 1, True)
                    mix_high(i)
                for h in range(2):
                    s = h * KC
                    if h == 1:
                        high_half(s, 0)
                        high_half(s, 1)
                        square(s - 1, KC - 1)
                        root(0)
                    high_half(s + 1, 0)
                    high_half(s + 1, 1)
                    if h == 0:
                        mix_high_2(0)
                        mix_high_2(1)
                    square(s, 0, first=(h == 0))
                    with act.Fori(2, KC) as t:
                        high_half(s + t, 0)
                        high_half(s + t, 1)
                        if h == 0:
                            mix_high_2(t)
                        square(s + t - 1, t - 1)
                square(LAST, KC - 1)
                root(1)

            @block.vector
            def _(dve):
                def low_half(s, half):
                    dve.wait_ge(w_high[half], s + 1)
                    nc.vector.tensor_tensor(w_lo[half][:], w_raw[half][:], w_hi[half][:].bitcast(F32),
                                            ALU.subtract).then_inc(w_ready[half], 1)

                def mix_low(i):
                    dve.wait_ge(m_high, i + 1)
                    two = slice(2 * i, 2 * i + 2)
                    nc.vector.tensor_tensor(m_lo[:, 0, two], xn[:, two], m_hi[:, 0, two].bitcast(F32),
                                            ALU.subtract).then_inc(m_ready, 1)

                def mix_low_2(k):
                    dve.wait_ge(m_high, KC // 2 + k + 1)
                    lo, hi = (m[:, 1, ds(k, 1)].rearrange("p a t -> p (a t)") for m in (m_lo, m_hi))
                    nc.vector.tensor_tensor(lo, m_in[:], hi.bitcast(F32), ALU.subtract).then_inc(m_ready, 1)

                def add(s, t, bank, h):
                    dve.wait_ge(tile_done, s + 1)
                    dve.wait_ge(x_landed, 16 * (s + 1))
                    if h == 1:
                        which = min(t, 2) if isinstance(t, int) else 2
                        dve.wait_ge(out_stored[which], 16 * (1, 1, (KC - 2) // GROUP)[which])
                    nc.vector.tensor_tensor(xn[:, ds(t, 1)].rearrange("p a t -> p (a t)"), psum[:, bank],
                                            x_in[:], ALU.add).then_inc(tile_read, 1)

                def invert(h):
                    dve.wait_ge(rooted, h + 1)
                    nc.vector.reciprocal(rms[:], rms[:]).then_inc(rms_ready, 1)

                nc.vector.memset(eps[:], RMS_EPS).then_inc(inited, 1)
                low_half(0, 0)
                for i in range(KC // 2):
                    if i == 3:
                        low_half(0, 1)
                    mix_low(i)
                for h in range(2):
                    s = h * KC
                    if h == 1:
                        low_half(s, 0)
                        low_half(s, 1)
                        add(s - 1, KC - 1, 1, 0)
                        invert(0)
                        dve.wait_ge(rms_ready, 1)
                        dve.wait_ge(gained, KC)
                    low_half(s + 1, 0)
                    for t in range(BY_DVE[0]) if h else ():
                        if t == 2:
                            low_half(s + 1, 1)
                        nc.vector.tensor_tensor(xn[:, t], xn[:, t], rms[:], ALU.mult).then_inc(scaled_dve, 1)
                    if h == 0:
                        low_half(s + 1, 1)
                    if h == 0:
                        mix_low_2(0)
                        mix_low_2(1)
                    add(s, 0, 0, h)
                    if h == 1:
                        low_half(s + 2, 0)
                        low_half(s + 2, 1)
                        add(s + 1, 1, 1, h)
                        low_half(s + 3, 0)
                        low_half(s + 3, 1)
                        add(s + 2, 2, 0, h)
                    with dve.Fori(1 + h, KC // 2) as m:
                        for i in range(2):
                            low_half(s + 2 * m + i, 0)
                            low_half(s + 2 * m + i, 1)
                            if h == 0:
                                mix_low_2(2 * m + i)
                            add(s + 2 * m + i - 1, 2 * m + i - 1, 1 - i, h)
                add(LAST, KC - 1, 1, 1)
                invert(1)
                dve.wait_ge(rms_ready, 2)
                dve.wait_ge(gained, 2 * KC)
                for t in range(0, BY_DVE[1], GROUP):
                    group = xn[:, t:t + GROUP]
                    nc.vector.tensor_tensor(group, group, rms[:].unsqueeze(1).broadcast_to([P, GROUP, HALF]),
                                            ALU.mult).then_inc(scaled_dve, 1)

            @block.gpsimd
            def _(pool):
                def accumulate(s, first=False):
                    pool.wait_ge(squared, s + 1)
                    if first:
                        ins = nc.gpsimd.tensor_copy(acc[:], sq[:])
                    else:
                        pool.wait_ge(summed, s)
                        ins = nc.gpsimd.tensor_tensor(acc[:], acc[:], sq[:], ALU.add)
                    ins.then_inc(summed, 1)

                def scale(t, n=1):
                    group = xn[:, t:t + n]
                    nc.gpsimd.tensor_tensor(group, group, rms[:].unsqueeze(1).broadcast_to([P, n, HALF]),
                                            ALU.mult).then_inc(scaled_pool, 1)

                def store(t, n):
                    if t < BY_DVE[0]:
                        pool.wait_ge(scaled_dve, t + n)
                    else:
                        pool.wait_ge(scaled_pool, (t - BY_DVE[0]) // GROUP + 1)
                    pool.dma_start(io["out"][t:t + n, :, 0:HALF].rearrange("k p n -> p k n"), xn[:, t:t + n]
                                   ).then_inc(out_stored[min(t, 2)], 16)

                accumulate(0, True)
                with pool.Fori(1, KC) as t:
                    accumulate(t)
                pool.wait_ge(mean_done, 1)
                pool.wait_ge(rms_ready, 1)
                pool.wait_ge(gained, KC)
                scale(BY_DVE[0], GROUP)
                store(0, 1)
                store(1, 1)
                store(2, 2)
                store(BY_DVE[0], GROUP)
                for t in range(BY_DVE[0] + GROUP, KC, GROUP):
                    if t == KC // 2:
                        accumulate(KC, True)
                    scale(t, GROUP)
                    store(t, GROUP)
                with pool.Fori(KC + 1, 2 * KC) as s:
                    accumulate(s)
                pool.wait_ge(rms_ready, 2)
                pool.wait_ge(gained, 2 * KC)
                for t in range(BY_DVE[1], KC, GROUP):
                    scale(t, GROUP)
                for i, n in enumerate((1, 1, (KC - 2) // GROUP)):
                    pool.wait_ge(out_stored[i], 16 * n)

            @block.tensor
            def _(pe):
                def project(s, bank, h, pace=False, between=None):
                    if between is not None or not pace:
                        pe.wait_ge(tile_read, s - 1)
                    for half in range(2):
                        pe.wait_ge(w_ready[half], s + 1)
                        for kk in range(KH):
                            c = half * KH + kk
                            if pace:
                                pe.wait_ge(m_ready, (c // 2 + 1) if h == 0 else KC // 2 + c + 1)
                            cols = slice(kk * P, (kk + 1) * P)
                            for wt, mt in ((w_hi, m_hi), (w_hi, m_lo), (w_lo, m_hi)):
                                mm = nc.tensor.matmul(psum[:, bank], wt[half][:, cols], mt[:, h, c],
                                                      start=(c == 0 and wt is w_hi and mt is m_hi),
                                                      stop=(c == KC - 1 and wt is w_lo))
                        mm.then_inc(tile_done if half else w_used, 1)
                        if half == 0 and between is not None:
                            between()

                def mean(h):
                    pe.wait_ge(summed, (h + 1) * KC)
                    nc.tensor.matmul(psum[:, 4], cst[:, slice(*CONSTS["mean"])], acc[:],
                                     start=True, stop=True).then_inc(mean_done, 1)

                for h in range(2):
                    s = h * KC
                    if h == 0:
                        project(0, 0, 0, pace=True)
                        project(1, 1, 0, pace=True)
                    else:
                        project(s, 0, 1, pace=True, between=lambda: mean(0))
                        project(s + 1, 1, 1)
                    with pe.Fori(1, KC // 2) as m:
                        project(s + 2 * m, 0, h)
                        project(s + 2 * m + 1, 1, h)
                mean(1)


SCRATCH = {
    "KB": (NB, P, PAIRS, 4, C), "QR": (NB, P, PAIRS, 4, C),
    "V": (NB, P, PAIRS, BT), "GS": (NB, P, PAIRS, BT), "BS": (NB, P, PAIRS, BT),
    "Q": (NB, P, PAIRS, BT), "SA": (NB, P, PAIRS, BT),
    "KVA": (2, P, T), "MIX": (NB, P, KC, BT),
    "L": (P // SUB, HEADS, SUB, SUB), "X": (P // SUB, HEADS, 2, SUB, SUB),
}


def layout(inputs):
    a = {n: np.asarray(v) for n, v in inputs.items()}

    def tiles(w, starts):
        w = w.reshape(2, KH, P, -1)
        w = np.stack([w[..., s:s + P] for s in starts])
        return np.ascontiguousarray(w.transpose(0, 1, 3, 2, 4)).reshape(len(starts), 2, P, KH * P)

    def channels(v, n):
        return np.asarray(v).reshape(n, P).T

    att = RWKV_COLS
    starts = [3 * RW, att + AW, att + AW + KVW]
    for j in range(PAIRS):
        starts += [j * P, RW + j * P, 2 * RW + j * P, 3 * RW + 2 * LORA + j * P,
                   att + j * P, att + AW + 2 * KVW + j * P]
    mu = a["mu_rwkv"][0]
    per = {"mu_r": mu[:RW], "mu_k": mu[RW:2 * RW], "mu_v": mu[2 * RW:3 * RW],
           "mu_g": mu[3 * RW + 2 * LORA:], "w0": a["w0"], "a0": a["a0"], "k_k": a["k_k"],
           "k_a": a["k_a"], "r_k": a["r_k"], "gain": a["lnx_gain"], "bias": a["lnx_bias"]}
    par = np.stack([channels(per[n], PAIRS) for n in PAR], axis=2)
    lora_up = np.concatenate([a["w_up"][0], a["a_up"][0]]).reshape(2 * LORA, PAIRS, P).transpose(1, 0, 2)
    quads = [4 * i + 2 * (hh % 2) + hh // 2 for i in range(HEADS // 4) for hh in range(4)]
    x_t = np.ascontiguousarray(a["x"][0].T).reshape(KC, P, T)
    out = {
        "x_t": x_t,
        "w_in": tiles(a["w_in"][0], starts),
        "w_out": tiles(a["w_out"][0], range(0, D, P)),
        "par": par,
        "par1": np.concatenate([channels(a["norm_gain"][0], KC), mu[3 * RW:3 * RW + 2 * LORA, None]], axis=1),
        "final_gain": channels(a["final_gain"], KC),
        "sinks": np.broadcast_to(a["attn_sinks"][0, quads], (P, HEADS)),
        "lora_up": lora_up,
        "consts": constants(),
    }
    return {n: np.ascontiguousarray(v) for n, v in out.items()}


def program(nc, io, scr):
    with ExitStack() as ctx:
        pc_all = ctx.enter_context(nc.sbuf_tensor("pc_all", [P, PAIRS, NC_], F32))
        cst = ctx.enter_context(nc.sbuf_tensor("cst", [P, CONST_COLS], F32))
        used = stage_a(nc, io, scr, pc_all, cst)
        stage_b(nc, io, scr, pc_all, cst, used)
        stage_c(nc, io, scr, cst)


def kernel(**inputs):
    from concourse import bacc
    from concourse.bass_utils import run_bass_kernel_spmd

    nc = bacc.Bacc("TRN2", target_bir_lowering=False, num_devices=1)
    arrays = {f"in_{name}": a for name, a in layout(inputs).items()}
    io = {name: nc.dram_tensor(f"in_{name}", arrays[f"in_{name}"].shape, F32, kind="ExternalInput").ap()
          for name in (n[3:] for n in arrays)}
    scr = {name: nc.dram_tensor(f"scratch_{name}", shape, F32).ap() for name, shape in SCRATCH.items()}
    io["out"] = nc.dram_tensor("out", (KC, P, T), F32, kind="ExternalOutput").ap()
    program(nc, io, scr)
    r = run_bass_kernel_spmd(nc, [arrays], core_ids=[0])
    return np.ascontiguousarray(np.asarray(r.results[0]["out"]).reshape(D, T).T)[None]
```
